# Optimizing a Trainium2 kernel written in Bass

```python
import jax, jax.numpy as jnp
from jax import lax
import numpy as np

D_MODEL = 1024
BATCH = 1
SEQ = 512
DEPTH = 2
DEC_BATCH = 8
DEC_SEQ = 16
PAST_LEN = 256

CHUNK = 64
WINDOW = 128
WIN_CHUNKS = WINDOW // CHUNK
Q_BLOCK = 128
ROPE_THETA = 10000.0
EPS = 1e-6

A_HEADS = 8
A_KV_HEADS = 2
A_GROUP = A_HEADS // A_KV_HEADS
HEAD_DIM = 64
A_WIDTH = A_HEADS * HEAD_DIM
A_SCALE = HEAD_DIM ** -0.5

B_HEADS = 4
NOPE_DIM = 128
ROPE_DIM = 64
V_DIM = 128
Q_LORA = 384
KV_LORA = 256
B_WIDTH = B_HEADS * V_DIM
MLA_SCALE = (NOPE_DIM + ROPE_DIM) ** -0.5

MIX_WIDTH = A_WIDTH + B_WIDTH
IN_SPLITS = (A_WIDTH, A_KV_HEADS * HEAD_DIM, A_KV_HEADS * HEAD_DIM, Q_LORA, KV_LORA, ROPE_DIM)
IN_OFFSETS = tuple(int(v) for v in np.cumsum((0,) + IN_SPLITS))
IN_WIDTH = IN_OFFSETS[-1]

D_FF = -(-8 * D_MODEL // (3 * 256)) * 256

kernel_name = "hymba_swa_sink_mla_stream_step"

def rms_norm(x, g):
    xf = x.astype(jnp.float32)
    y = xf * lax.rsqrt(jnp.mean(xf * xf, axis=-1, keepdims=True) + EPS)
    return (y * g.astype(jnp.float32)).astype(x.dtype)

def rope(x, pos):
    half = x.shape[-1] // 2
    inv = jnp.power(jnp.float32(ROPE_THETA), -jnp.arange(half, dtype=jnp.float32) / half)
    ang = pos.astype(jnp.float32)[:, None] * inv[None, :]
    cos = jnp.cos(ang)[:, None, :]
    sin = jnp.sin(ang)[:, None, :]
    xf = x.astype(jnp.float32)
    x1, x2 = xf[..., :half], xf[..., half:]
    return jnp.concatenate([x1 * cos - x2 * sin, x2 * cos + x1 * sin], axis=-1).astype(x.dtype)

def mixer_inputs(n, pos, w_in, q_norm, w_uq, kv_norm, w_uk):
    b, s, _ = n.shape
    h = n @ w_in
    o = IN_OFFSETS
    q_a = rope(h[..., o[0]:o[1]].reshape(b, s, A_HEADS, HEAD_DIM), pos)
    k_a = rope(h[..., o[1]:o[2]].reshape(b, s, A_KV_HEADS, HEAD_DIM), pos)
    v_a = h[..., o[2]:o[3]].reshape(b, s, A_KV_HEADS, HEAD_DIM)
    q_b = (rms_norm(h[..., o[3]:o[4]], q_norm) @ w_uq).reshape(b, s, B_HEADS, NOPE_DIM + ROPE_DIM)
    q_lat = jnp.einsum('bshn,chn->bshc', q_b[..., :NOPE_DIM], w_uk)
    q_rope = rope(q_b[..., NOPE_DIM:], pos)
    ckv = rms_norm(h[..., o[4]:o[5]], kv_norm)
    k_rope = rope(h[..., o[5]:o[6]][:, :, None, :], pos)[:, :, 0, :]
    return q_a, k_a, v_a, q_lat, q_rope, ckv, k_rope

def sink_softmax(s, sink):
    sk = sink.astype(jnp.float32)[:, :, None, None]
    m = jnp.maximum(jnp.max(s, axis=-1, keepdims=True), sk)
    e = jnp.exp(s - m)
    return e / (jnp.sum(e, axis=-1, keepdims=True) + jnp.exp(sk - m))

def window_attn_prompt(q, k, v, sink):
    b, s, _, d = q.shape
    nc = s // CHUNK
    qc = q.reshape(b, nc, CHUNK, A_KV_HEADS, A_GROUP, d)

    def band(t):
        tc = t.reshape(b, nc, CHUNK, A_KV_HEADS, d)
        tp = jnp.pad(tc, ((0, 0), (WIN_CHUNKS, 0), (0, 0), (0, 0), (0, 0)))
        return jnp.concatenate([tp[:, i:i + nc] for i in range(WIN_CHUNKS + 1)], axis=2)

    kb, vb = band(k), band(v)
    valid = (jnp.arange(nc)[:, None] - WIN_CHUNKS + jnp.arange(WIN_CHUNKS + 1)[None, :]) >= 0
    valid = jnp.repeat(valid, CHUNK, axis=1)
    sc = jnp.einsum('bnqkgd,bnskd->bnkgqs', qc, kb,
                    preferred_element_type=jnp.float32) * A_SCALE
    sc = jnp.where(valid[None, :, None, None, None, :], sc, -jnp.inf)
    p = sink_softmax(sc, sink.reshape(A_KV_HEADS, A_GROUP)).astype(v.dtype)
    o = jnp.einsum('bnkgqs,bnskd->bnqkgd', p, vb)
    return o.reshape(b, s, A_WIDTH)

def window_attn_sample(q, k_all, v_all, sink):
    b, s, _, d = q.shape
    qg = q.reshape(b, s, A_KV_HEADS, A_GROUP, d)
    sc = jnp.einsum('bqkgd,bskd->bkgqs', qg, k_all,
                    preferred_element_type=jnp.float32) * A_SCALE
    p = sink_softmax(sc, sink.reshape(A_KV_HEADS, A_GROUP)).astype(v_all.dtype)
    o = jnp.einsum('bkgqs,bskd->bqkgd', p, v_all)
    return o.reshape(b, s, A_WIDTH)

def mla_attend(q_lat, q_rope, ckv, k_rope, mask):
    sc = (jnp.einsum('bqhc,btc->bhqt', q_lat, ckv, preferred_element_type=jnp.float32)
          + jnp.einsum('bqhr,btr->bhqt', q_rope, k_rope, preferred_element_type=jnp.float32)) * MLA_SCALE
    if mask is not None:
        sc = jnp.where(mask, sc, -jnp.inf)
    p = jax.nn.softmax(sc, axis=-1).astype(ckv.dtype)
    return jnp.einsum('bhqt,btc->bqhc', p, ckv)

def mla_prompt(q_lat, q_rope, ckv, k_rope):
    b, s, h, c = q_lat.shape
    nb = s // Q_BLOCK
    qlb = q_lat.reshape(b, nb, Q_BLOCK, h, c).swapaxes(0, 1)
    qrb = q_rope.reshape(b, nb, Q_BLOCK, h, ROPE_DIM).swapaxes(0, 1)
    k_chunk = jnp.arange(s) // CHUNK

    def block(args):
        ql, qr, i = args
        q_chunk = (i * Q_BLOCK + jnp.arange(Q_BLOCK)) // CHUNK
        mask = k_chunk[None, :] <= q_chunk[:, None]
        return mla_attend(ql, qr, ckv, k_rope, mask)

    out = lax.map(block, (qlb, qrb, jnp.arange(nb)))
    return out.swapaxes(0, 1).reshape(b, s, h, c)

def mix_output(o_a, o_lat, w_uv, gn_a, gn_b, w_out):
    b, s = o_a.shape[:2]
    o_b = jnp.einsum('bshc,chv->bshv', o_lat, w_uv).reshape(b, s, B_WIDTH)
    merged = jnp.concatenate([rms_norm(o_a, gn_a), rms_norm(o_b, gn_b)], axis=-1)
    return merged @ w_out

def swiglu(x, g, w_gate, w_up, w_down):
    n = rms_norm(x, g)
    return (jax.nn.silu(n @ w_gate) * (n @ w_up)) @ w_down

def setup_inputs(seed: int = 0) -> dict:
    key = jax.random.key(seed)
    ks = jax.random.split(key, 32)
    nrm = lambda k, shp, sc: jax.random.normal(k, shp, jnp.float32) * sc
    gain = lambda k, shp: 1.0 + 0.02 * jax.random.normal(k, shp, jnp.float32)
    return {
        "x_prompt": nrm(ks[0], (BATCH, SEQ, D_MODEL), 1.0),
        "x_sample": nrm(ks[1], (DEC_BATCH, DEC_SEQ, D_MODEL), 1.0),
        "cache_win_k": nrm(ks[2], (DEPTH, DEC_BATCH, min(WINDOW, PAST_LEN), A_KV_HEADS, HEAD_DIM), 1.0),
        "cache_win_v": nrm(ks[3], (DEPTH, DEC_BATCH, min(WINDOW, PAST_LEN), A_KV_HEADS, HEAD_DIM), 1.0),
        "cache_mla_ckv": nrm(ks[4], (DEPTH, DEC_BATCH, PAST_LEN, KV_LORA), 1.0),
        "cache_mla_krope": nrm(ks[5], (DEPTH, DEC_BATCH, PAST_LEN, ROPE_DIM), 1.0),
        "attn_norm": gain(ks[6], (DEPTH, D_MODEL)),
        "w_in": nrm(ks[7], (DEPTH, D_MODEL, IN_WIDTH), D_MODEL ** -0.5),
        "q_norm": gain(ks[8], (DEPTH, Q_LORA)),
        "w_uq": nrm(ks[9], (DEPTH, Q_LORA, B_HEADS * (NOPE_DIM + ROPE_DIM)), Q_LORA ** -0.5),
        "kv_norm": gain(ks[10], (DEPTH, KV_LORA)),
        "w_uk": nrm(ks[11], (DEPTH, KV_LORA, B_HEADS, NOPE_DIM), KV_LORA ** -0.5),
        "w_uv": nrm(ks[12], (DEPTH, KV_LORA, B_HEADS, V_DIM), KV_LORA ** -0.5),
        "sinks": nrm(ks[13], (DEPTH, A_HEADS), 0.5),
        "gn_a": gain(ks[14], (DEPTH, A_WIDTH)),
        "gn_b": gain(ks[15], (DEPTH, B_WIDTH)),
        "w_out": nrm(ks[16], (DEPTH, MIX_WIDTH, D_MODEL), MIX_WIDTH ** -0.5),
        "ffn_norm": gain(ks[17], (DEPTH, D_MODEL)),
        "w_gate": nrm(ks[18], (DEPTH, D_MODEL, D_FF), D_MODEL ** -0.5),
        "w_up": nrm(ks[19], (DEPTH, D_MODEL, D_FF), D_MODEL ** -0.5),
        "w_down": nrm(ks[20], (DEPTH, D_FF, D_MODEL), D_FF ** -0.5),
        "final_norm": gain(ks[21], (D_MODEL,)),
    }

def reference(x_prompt, x_sample, cache_win_k, cache_win_v, cache_mla_ckv, cache_mla_krope,
              attn_norm, w_in, q_norm, w_uq, kv_norm, w_uk, w_uv, sinks, gn_a, gn_b, w_out,
              ffn_norm, w_gate, w_up, w_down, final_norm):
    past = cache_mla_ckv.shape[2]
    pos_p = jnp.arange(x_prompt.shape[1], dtype=jnp.int32)
    pos_s = past + jnp.arange(x_sample.shape[1], dtype=jnp.int32)
    win = cache_win_k.shape[2]
    xp, xs = x_prompt, x_sample
    p_wk, p_wv, p_ckv, p_kr = [], [], [], []
    s_wk, s_wv, s_ckv, s_kr = [], [], [], []
    for l in range(DEPTH):
        proj = (w_in[l], q_norm[l], w_uq[l], kv_norm[l], w_uk[l])
        qa, ka, va, ql, qr, ckv, kr = mixer_inputs(rms_norm(xp, attn_norm[l]), pos_p, *proj)
        o_a = window_attn_prompt(qa, ka, va, sinks[l])
        o_lat = mla_prompt(ql, qr, ckv, kr)
        xp = xp + mix_output(o_a, o_lat, w_uv[l], gn_a[l], gn_b[l], w_out[l])
        xp = xp + swiglu(xp, ffn_norm[l], w_gate[l], w_up[l], w_down[l])
        p_wk.append(ka[:, -win:])
        p_wv.append(va[:, -win:])
        p_ckv.append(ckv)
        p_kr.append(kr)
        qa, ka, va, ql, qr, ckv, kr = mixer_inputs(rms_norm(xs, attn_norm[l]), pos_s, *proj)
        k_all = jnp.concatenate([cache_win_k[l], ka], axis=1)
        v_all = jnp.concatenate([cache_win_v[l], va], axis=1)
        o_a = window_attn_sample(qa, k_all, v_all, sinks[l])
        ckv_all = jnp.concatenate([cache_mla_ckv[l], ckv], axis=1)
        kr_all = jnp.concatenate([cache_mla_krope[l], kr], axis=1)
        o_lat = mla_attend(ql, qr, ckv_all, kr_all, None)
        xs = xs + mix_output(o_a, o_lat, w_uv[l], gn_a[l], gn_b[l], w_out[l])
        xs = xs + swiglu(xs, ffn_norm[l], w_gate[l], w_up[l], w_down[l])
        s_wk.append(k_all[:, -win:])
        s_wv.append(v_all[:, -win:])
        s_ckv.append(ckv)
        s_kr.append(kr)
    y_prompt = rms_norm(xp, final_norm)
    y_sample = rms_norm(xs, final_norm)
    return (y_prompt, y_sample,
            jnp.stack(p_wk), jnp.stack(p_wv), jnp.stack(p_ckv), jnp.stack(p_kr),
            jnp.stack(s_wk), jnp.stack(s_wv), jnp.stack(s_ckv), jnp.stack(s_kr))


_drawn_inputs = setup_inputs


def setup_inputs(seed=0):
    import zlib

    import numpy as np

    out = dict(_drawn_inputs(seed))
    spreads = {}
    factors = {'q_norm': 4.328,
     'sinks': 8.0,
     'gn_a': 4.01,
     'gn_b': 3.96,
     'ffn_norm': 3.828,
     'final_norm': 2.729}
    for name, (base, spread) in spreads.items():
        noise = np.random.default_rng([zlib.crc32(name.encode()), seed]).standard_normal(out[name].shape)
        drawn = base * np.exp(spread * noise) if base else spread * noise
        out[name] = __import__('jax').numpy.asarray(drawn.astype(out[name].dtype))
    for name, factor in factors.items():
        out[name] = (out[name] * factor).astype(out[name].dtype)
    return out
```

```python
from contextlib import ExitStack

import concourse.bass as bass
from concourse import mybir

F32 = mybir.dt.float32
F32R = mybir.dt.float32r
ALU = mybir.AluOpType
ACT = mybir.ActivationFunctionType
AX = mybir.AxisListType

P = 128
D = 1024
NC_ = D // P
PROMPT, DECB, DECS = 512, 8, 16
T = PROMPT + DECB * DECS
NT = T // P
TS = NT - 1
HALF = T // 2
DEPTH = 2
PAST, WIN = 256, 128
EPS = 1e-6
AH, HD = 8, 64
BH, NOPE, ROPE, VD = 4, 128, 64, 128
QL, KL = 384, 256
A_SCALE = HD ** -0.5
B_SCALE = (NOPE + ROPE) ** -0.5
C_K, C_V, C_Q, C_KV, C_KR, IN_W = 512, 640, 768, 1152, 1408, 1472
FF = 2816
NBLK = 2
FT = FF // P // NBLK
GROUPS = [(960, IN_W - 960), (512, 448), (0, 512)]
WIN_U = 12
U_UQ = WIN_U
U_OUT = U_UQ + 1
U_FFN = U_OUT + NC_
BLK_U = 2 * FT + NC_
UNITS = U_FFN + NBLK * BLK_U
SLOT = FT * P
G_NEXT, G_FFN, G_MIX, G_Q, G_SINK, G_SINKS, G_KV = 0, 8, 16, 24, 27, 35, 36
G_W = G_KV + KL
K_ID, K_ROPE, K_GAIN = 0, 128, 128 + NT * 128
K_ONE, K_EPS = K_GAIN + NC_, K_GAIN + NC_ + 1
K_ONES = K_EPS + 1
K_W = -(-(K_ONES + P) // 8) * 8
M_OWN, M_BAND, M_ID, M_W = 0, 384, 640, 768
HIDDEN = -1e30
POFF = [0, 128, 384, 768, 1280]
TOFF = [0, 512, 896, 1152]
DOWN_PAIR = [2, 3, 0, 1, 0, 1, 2, 3]


class Signal:

    def __init__(self, ctx, nc, name, per, pre=0):
        self.sem, self.per, self.pre = ctx.enter_context(nc.semaphore(name)), per, pre

    def at(self, layer, k):
        return layer * self.per + (self.pre + k)


def hybrid_encoder_step(nc, a):
    ctx = ExitStack()

    def place(offset, specs):
        with ExitStack() as r:
            if offset:
                r.enter_context(nc.sbuf_tensor(f"skip_{specs[0][0]}", [P, offset // 4], F32))
            return [r.enter_context(nc.sbuf_tensor(n, s, d)) for n, s, d in specs]

    W0, H0, S0, K0 = 61440, 95232, 151552, 164352
    xT, nh, nl = place(0, [("xT", [P, NC_, T], F32), ("nh", [P, NC_, T], F32R), ("nl", [P, NC_, T], F32R)])
    wraw, whi, wlo = place(W0, [("wraw", [P, 2 * SLOT], F32), ("whi", [P, 2 * SLOT], F32R), ("wlo", [P, 2 * SLOT], F32R)])
    hh, hl = place(H0, [("hh", [P, FT, T], F32R), ("hl", [P, FT, T], F32R)])
    ssq, rA, sq, ssqB = place(S0, [("ssq", [P, T], F32), ("rA", [P, T], F32), ("sq", [P, 2, T], F32), ("ssqB", [P, T], F32)])
    _, rB = place(S0, [("skip_rB", [P, 4 * T], F32), ("rB", [P, T], F32)])
    kc, kmask, gv, small = place(K0, [("kc", [P, K_W], F32), ("kmask", [P, M_W], F32R), ("gv", [P, 40], F32), ("small", [P, 144], F32)])
    R0 = K0 + 4 * (K_W + M_W + 40 + 144)
    mh, ml = place(R0, [("mh", [P, NC_, T], F32R), ("ml", [P, NC_, T], F32R)])
    tg, tu = place(R0, [("tg", [P, 2, T], F32), ("tu", [P, 2, T], F32)])
    _, xt, _, diag = place(H0, [("skip_xt", [P, 1280], F32), ("xt", [P, 2, T], F32), ("skip_diag", [P, 2560], F32), ("diag", [P, 10, P], F32)])
    xin, mask_in = place(H0, [("xin", [P, NT, D], F32), ("mask_in", [P, M_W], F32)])
    yout, = place(H0, [("yout", [P, NT, D], F32)])
    ckh, ckl, krT, qrT, cqh, cql, qnh, qnl = place(20480, [
        ("ckh", [P, 2, PROMPT], F32R), ("ckl", [P, 2, PROMPT], F32R), ("krT", [P, 2, PROMPT], F32R),
        ("qrT", [P, BH, PROMPT], F32R), ("cqh", [P, 3, T], F32R), ("cql", [P, 3, T], F32R),
        ("qnh", [P, T], F32R), ("qnl", [P, T], F32R)])
    hm, qaT, kaT, qTs = place(H0, [("hm", [P, NT, IN_W], F32), ("qaT", [P, AH, PROMPT], F32R),
                                   ("kaT", [P, 4, PROMPT], F32R), ("qTs", [P, DECB, 4, DECS], F32)])
    pwx, = place(H0 + 10240, [("pwx", [P, 2, 4, 256], F32)])
    oT, cr = place(H0, [("oT", [P, NC_, T], F32), ("cr", [P, 2, 1024], F32)])
    pws, = place(H0 + 20480, [("pws", [P, DECB, 256], F32)])
    kTc, ptw = place(S0, [("kTc", [P, DECB, 144], F32), ("ptw", [P, DECB, 2, P], F32)])
    qlh, qll, pm = place(H0 + 29440, [("qlh", [P, 2, 2, PROMPT], F32R), ("qll", [P, 2, 2, PROMPT], F32R),
                                      ("pm", [P, 1280], F32)])
    uv, = place(H0 + 50944, [("uv", [P, 2, 512], F32)])
    cx, = place(20480, [("cx", [P, 6, 1024], F32)])
    cTo, = place(56320, [("cTo", [P, 3, 272], F32)])
    olats, olTs, psm, pts = place(H0 + 29440, [("olats", [P, KL], F32), ("olTs", [P, 2, BH, P], F32),
                                               ("psm", [P, 2, 384], F32), ("pts", [P, 3, P], F32)])
    v, ckv, vn, cT, kTs, qrTs, ckTs, krTs, ptm, ukh, ukl, qlTs, kvg = place(R0, [
        ("v", [P, NT, 128], F32), ("ckv", [P, NT, KL], F32), ("vn", [16, DECB, 128], F32), ("cT", [P, 3, 272], F32),
        ("kTs", [P, P], F32), ("qrTs", [P, DECB, BH, DECS], F32), ("ckTs", [P, 2, P], F32), ("krTs", [P, P], F32),
        ("ptm", [P, 2048], F32), ("ukh", [P, BH, KL], F32R), ("ukl", [P, BH, KL], F32R),
        ("qlTs", [P, 2, DECB, BH, DECS], F32), ("kvg", [P, KL], F32)])
    _, krd = place(R0, [("skip_krd", [P, 2944], F32), ("krd", [P, 2, 64], F32)])
    _, wk, wv = place(R0, [("skip_wk", [P, 4784], F32), ("wk", [P, DECB, 128], F32), ("wv", [P, DECB, 128], F32)])
    _, qcos, qsin = place(R0, [("skip_qcos", [P, 4784], F32), ("qcos", [P, 2, 512], F32), ("qsin", [P, 2, 512], F32)])
    _, q2r = place(R0, [("skip_q2r", [P, 8880], F32), ("q2r", [P, 2, BH, P], F32R)])
    kcos, ksin, junk = place(H0 + 29440, [("kcos", [P, NT, 128], F32), ("ksin", [P, NT, 128], F32), ("junk", [P, NT, QL + KL], F32)])
    k2, = place(S0, [("k2", [P, TS, 12, 64], F32R)])
    q2, qra, qrb = place(S0, [("q2", [P, 2, AH, 128], F32R), ("qra", [P, 2, 256], F32), ("qrb", [P, 256], F32)])
    q2s, = place(S0, [("q2s", [P, 4, 2, 64], F32)])
    pw, pt = place(S0, [("pw", [P, 2, 4, 256], F32), ("pt", [P, 2, 512], F32)])
    olat, = place(S0, [("olat", [P, 2, PROMPT], F32)])
    cache_end = R0 + 40960
    assert cache_end + 16512 <= nc.sbuf_usable_end, (cache_end + 16512, nc.sbuf_usable_end)
    ps = ctx.enter_context(nc.psum_tensor("ps", [P, 8, 512], F32))

    ident = kc[:, K_ID:K_ID + P]
    mask_first, mask_own, mask_band = (kmask[:, x:x + 256] for x in (M_OWN + P, M_OWN, M_BAND))
    ident_r = kmask[:, M_ID:M_ID + P]
    cos = [kc[:, K_ROPE + 128 * t:K_ROPE + 128 * t + 64] for t in range(NT)]
    sin = [kc[:, K_ROPE + 128 * t + 64:K_ROPE + 128 * t + 128] for t in range(NT)]
    onesq = kc[:, K_ONES:K_ONES + P]
    one, eps = kc[:, K_ONE:K_ONE + 1], kc[:, K_EPS:K_EPS + 1]
    ms, sd, rs, mx, nsink, rl = (small[:, x:x + w] for x, w in ((0, 10), (10, 10), (20, 10), (30, 8), (38, 9), (128, 10)))
    pwb = [pw[:, 0], pw[:, 1], pwx[:, 0], pwx[:, 1]]

    def four_of(buffers, n):
        return buffers[n // 2 % 2][:, 4 * (n % 2):4 * (n % 2) + 4]

    nm, ed, rsum, es, rinv = ([small[:, x + 8 * b:x + 8 * b + 8] for b in range(2)] for x in (48, 64, 80, 96, 112))

    def cache(b):
        return cr[:, b] if b < 2 else cx[:, b - 2]

    def sig(name, per, pre=0):
        return Signal(ctx, nc, name, per, pre)

    consts_in, x_in = sig("consts_in", 0), sig("x_in", 0)
    vectors_in = sig("vectors_in", 32)
    raw_in = [sig("raw_in0", 16 * 50), sig("raw_in1", 16 * 48)]
    win_in, vnew_in, uv_in, cache_in = sig("win_in", 32), sig("vnew_in", 16), sig("uv_in", 16), [sig(f"cache_in{b}", 16 * 4) for b in range(DECB)]
    out_hm, out_ckv, out_sample, out_copy, out_y = sig("out_hm", 16 * 5), sig("out_ckv", 16), sig("out_sample", 32), sig("out_copy", 32), sig("out_y", 0)
    unit_hi, unit_lo, unit_used = sig("unit_hi", UNITS), sig("unit_lo", UNITS, 2), sig("unit_used", UNITS, 2)
    x_new, n_hi, n_lo = sig("x_new", 24, 8), sig("n_hi", 16, 8), sig("n_lo", 16, 8)
    x_turned = sig("x_turned", 0)
    sq_new, ssq_new = sig("sq_new", 25, 8), sig("ssq_new", 23, 7)
    m_hi, m_lo = sig("m_hi", 8), sig("m_lo", 8)
    stat_sum, stat_sd, stat_r, diag_new, bcast, r_new = (sig(n, p) for n, p in (
        ("stat_sum", 4), ("stat_sd", 5), ("stat_r", 1), ("diag_new", 3), ("bcast", 3), ("r_new", 2)))
    in_done, hm_new, k_roped, q_cos, q_roped = (sig(n, p) for n, p in (
        ("in_done", 12), ("hm_new", 15), ("k_roped", 1), ("q_cos", 5), ("q_roped", 5)))
    lat_ms, cq_norm, ckv_norm, v_new = sig("lat_ms", 10), sig("cq_norm", 5), sig("ckv_norm", 5), sig("v_new", 1)
    k_hi, k_lo, q_hi, q_lo = sig("k_hi", 1), sig("k_lo", 1), sig("q_hi", 5), sig("q_lo", 4)
    k_turned, k_act, k_dve, q_turned, q_act, q_dve = (sig(n, p) for n, p in (
        ("k_turned", 14), ("k_act", 13), ("k_dve", 10), ("q_turned", 9), ("q_act", 5), ("q_dve", 4)))
    uk_turned, uk_hi, uk_lo = sig("uk_turned", 2), sig("uk_hi", 2), sig("uk_lo", 2)
    uqr_rope = sig("uqr_rope", 5)
    uqr_done, uqr_hi, uqr_lo, uqr_turned, uqr_new, uqr_new_read = (sig(n, 5) for n in (
        "uqr_done", "uqr_hi", "uqr_lo", "uqr_turned", "uqr_new", "uqr_read"))
    w_s, w_nm, w_e, w_rinv, w_p, w_t, w_tact, w_tdve, w_pv, w_o = (sig(n, p) for n, p in (
        ("w_scores", 8), ("w_negmax", 8), ("w_exp", 8), ("w_rinv", 8), ("w_probs", 8), ("w_turned", 14),
        ("w_turned_act", 8), ("w_turned_dve", 6), ("w_pv", 8), ("w_out", 4)))
    v_kt, v_ktact, v_ktdve, v_knew, v_zero, v_s, v_nm, v_e, v_p, v_t, v_tact, v_tdve, v_pv, v_o = (sig(n, p) for n, p in (
        ("v_keys_turned", 2), ("v_keys_act", 1), ("v_keys_dve", 1), ("v_keys_new", 1), ("v_zero", 1), ("v_scores", 1), ("v_negmax", 1), ("v_exp", 1),
        ("v_probs", 1), ("v_turned", 4), ("v_turned_act", 2), ("v_turned_dve", 2), ("v_pv", 1), ("v_out", 1)))
    qn_done, qn_hi, qn_lo, ql_done, ql_hi, ql_lo = (sig(n, p) for n, p in (
        ("qn_done", 3), ("qn_hi", 4), ("qn_lo", 4), ("ql_done", 8), ("ql_hi", 8), ("ql_lo", 8)))
    p_s, p_nm, p_e, p_p, p_t, p_tact, p_tdve, p_pv, p_lat, p_latd, p_ob, p_o = (sig(n, p) for n, p in (
        ("p_scores", 16), ("p_negmax", 16), ("p_exp", 16), ("p_probs", 16), ("p_turned", 16), ("p_turned_act", 8),
        ("p_turned_dve", 8), ("p_pv", 8), ("p_lat_act", 4), ("p_lat_dve", 4), ("p_ob", 4), ("p_out", 4)))
    c_zero, c_t, c_act, c_dve, c_s, c_nm, c_e, c_p, c_pt, c_ptact, c_pv, c_lat, c_lt, c_ltact, c_ob, c_o = (sig(n, p) for n, p in (
        ("c_zero", 1), ("c_turned", 8), ("c_keys_act", 8), ("c_keys_dve", 8), ("c_scores", 8), ("c_negmax", 4), ("c_exp", 4), ("c_probs", 4),
        ("c_probs_turned", 4), ("c_probs_act", 4), ("c_pv", 8), ("c_lat", 4), ("c_lat_turned", 4), ("c_lat_new", 4),
        ("c_ob", 1), ("c_out", 1)))
    g_scaled, u_scaled, silu_new, h_new, h_hi, h_lo = (sig(n, NBLK * FT) for n in (
        "gate_scaled", "up_scaled", "silu_new", "h_new", "h_hi", "h_lo"))
    dve_r = sig("dve_r", 1)
    dve_step = sig("dve_step", 96)
    y_gain, y_turned, y_act, y_dve = (sig(n, 0) for n in ("y_gain", "y_turned", "y_act", "y_dve"))

    def slot(s, n=SLOT):
        return slice(s * SLOT, s * SLOT + n)

    def raw_value(s, layer, u):
        base = 7 if s == 0 else 6
        if u == "uk":
            n = base + 1
        elif u < WIN_U:
            n = u // 2 + 1
        elif u == U_UQ:
            n = 7
        elif u < U_FFN:
            n = base + (s == 0) + 3 * ((u - U_OUT) // 2 + 1)
        else:
            n = base + (s == 0) + 12 + (u - U_FFN) // 2 + 1
        return raw_in[s].at(layer, 16 * n)

    def unit_slot(u):
        return u % 2 if u < WIN_U else 0 if u == U_UQ else (u - U_OUT) % 2 if u < U_FFN else (u - U_FFN) % 2

    def unit_width(u):
        if u < WIN_U:
            return 1024
        if u == U_UQ:
            return 3 * BH * (NOPE + ROPE)
        return 1024 if u < U_FFN or (u - U_FFN) % BLK_U < 2 * FT else FT * P

    def used_before(u):
        return U_OUT if u in (U_OUT, U_OUT + 1) else WIN_U if u == U_UQ else u - 1

    uq_hi = whi[:, 0:2304].rearrange("p (k n) -> p k n", k=3)
    uq_lo = wlo[:, 0:2304].rearrange("p (k n) -> p k n", k=3)

    def rope_cols(w, k):
        return w[:, k, :].rearrange("p (h n) -> p h n", h=BH)[:, :, NOPE:]

    def layers(eng):
        with eng.Fori(0, DEPTH) as layer:
            yield layer

    def turned_by(n):
        return n + 1 if n < 2 else 2 * n

    def tok(t):
        return slice(t * P, (t + 1) * P)

    def half(j):
        return slice(j * HALF, (j + 1) * HALF)

    def halves(ap):
        return ap.rearrange("p (j n) -> p j n", j=2)

    block = ctx.enter_context(nc.Block())

    @block.sync
    def _(sp):
        sp.dma_start(kc[:, :], a["consts"][:, 0:K_W]).then_inc(consts_in.sem, 16)
        sp.dma_start(mask_in[:, :], a["consts"][:, K_W:]).then_inc(consts_in.sem, 16)
        for t in range(TS):
            sp.dma_start(xin[:, t, :], a["x_prompt"][0, tok(t), :]).then_inc(x_in.sem, 16)
        sp.dma_start(xin[:, TS, :], a["x_sample"].rearrange("b s d -> (b s) d")).then_inc(x_in.sem, 16)
        w_in = a["w_in"].rearrange("l (k p) n -> l p k n", p=P)
        w_uq = a["w_uq"].rearrange("l (k p) n -> l p k n", p=P)
        w_uk = a["w_uk"].rearrange("l (k p) h n -> l p k (h n)", p=P)
        w_uv = a["w_uv"].rearrange("l (k p) h n -> l p k (h n)", p=P)
        wo_low = a["w_out"].rearrange("l (e j p) n -> l e p j n", p=64, j=4)
        wo_high = a["w_out"].rearrange("l (k p) n -> l p k n", p=P)
        w_gate = a["w_gate"].rearrange("l (k p) n -> l p k n", p=P)
        w_up = a["w_up"].rearrange("l (k p) n -> l p k n", p=P)
        w_down = a["w_down"].rearrange("l (f p) n -> l p f n", p=P)
        for l in layers(sp):
            def load(u, source):
                s = unit_slot(u)
                if u == U_OUT:
                    sp.wait_ge(uk_turned.sem, uk_turned.at(l, 2))
                else:
                    sp.wait_ge(unit_lo.sem, unit_lo.at(l, used_before(u)))
                if u == 8:
                    sp.dma_start(kvg[:, :], a["vectors"][l][:, G_KV:G_W]).then_inc(vectors_in.sem, 16)
                for part0, first, width, src in source:
                    parts, k, w = src.shape
                    dst = wraw[part0:part0 + parts, s * SLOT + first * width:s * SLOT + (first + k) * width]
                    dst = dst.rearrange("p (k n) -> p k n", k=k)[:, :, 0:w]
                    sp.dma_start(dst, src).then_inc(raw_in[s].sem, 16)

            for u in range(WIN_U):
                c0, w = GROUPS[u // 4]
                kp = u % 4
                load(u, [(0, 0, 512, w_in[l][:, 2 * kp:2 * kp + 2, c0:c0 + w])])
                if u == 1:
                    sp.wait_ge(n_lo.sem, n_lo.at(l, 0))
                    sp.dma_start(gv[:, 0:36], a["vectors"][l][:, 0:36]).then_inc(vectors_in.sem, 16)
            keep = WIN - DECS
            sp.dma_start(a["out_wks"][l][:, 0:keep], a["cache_win_k"][l][:, DECS:]).then_inc(out_copy.sem, 16)
            sp.dma_start(a["out_wvs"][l][:, 0:keep], a["cache_win_v"][l][:, DECS:]).then_inc(out_copy.sem, 16)
            load(U_UQ, [(0, 0, 768, w_uq[l])])
            sp.wait_ge(unit_lo.sem, unit_lo.at(l, U_OUT))
            sp.dma_start(wraw[:, slot(0, 1024)].rearrange("p (k n) -> p k n", k=2), w_uk[l]).then_inc(raw_in[0].sem, 16)
            sp.wait_ge(ckv_norm.sem, ckv_norm.at(l, 5))
            sp.dma_start(a["out_ckvs"][l].rearrange("b s c -> (b s) c"), ckv[:, TS, :]).then_inc(out_sample.sem, 16)
            sp.wait_ge(v_new.sem, v_new.at(l, 1))
            sp.dma_start(a["out_wvs"][l][:, keep:].rearrange("b s h d -> b s (h d)"), v[:, TS, :]).then_inc(out_sample.sem, 16)
            sp.dma_start(a["out_ckv"][l, 0].rearrange("(t p) c -> p t c", p=P), ckv[:, 0:TS, :]).then_inc(out_ckv.sem, 16)
            sp.wait_ge(k_roped.sem, k_roped.at(l, 1))
            sp.dma_start(a["out_wk"][l, 0].rearrange("s h d -> s (h d)"), hm[:, 3, C_K:C_V]).then_inc(out_hm.sem, 16)
            sp.dma_start(a["out_wv"][l, 0].rearrange("s h d -> s (h d)"), hm[:, 3, C_V:C_Q]).then_inc(out_hm.sem, 16)
            sp.dma_start(a["out_kr"][l, 0].rearrange("(t p) c -> p t c", p=P), hm[:, 0:TS, C_KR:IN_W]).then_inc(out_hm.sem, 16)
            sp.dma_start(a["out_wks"][l][:, keep:].rearrange("b s h d -> b s (h d)"), hm[:, TS, C_K:C_V]).then_inc(out_hm.sem, 16)
            sp.dma_start(a["out_krs"][l].rearrange("b s c -> (b s) c"), hm[:, TS, C_KR:IN_W]).then_inc(out_hm.sem, 16)
            sp.wait_ge(out_sample.sem, out_sample.at(l, 32))
            sp.dma_start(vn[:, :, :], a["out_wvs"][l][:, keep:].rearrange("b s h d -> s b (h d)")).then_inc(vnew_in.sem, 16)
            sp.wait_ge(q_roped.sem, q_roped.at(l, NT))
            sp.dma_start(wk[:, :, :], a["cache_win_k"][l].rearrange("b s h d -> s b (h d)")).then_inc(win_in.sem, 16)
            sp.dma_start(wv[:, :, :], a["cache_win_v"][l].rearrange("b s h d -> s b (h d)")).then_inc(win_in.sem, 16)
            load_out = lambda d: load(U_OUT + d, [
                (0, 0, P, wo_low[l, 0][:, :, d * P:(d + 1) * P]),
                (64, 0, P, wo_low[l, 1][:, :, d * P:(d + 1) * P]),
                (0, 4, P, wo_high[l][:, 4:8, d * P:(d + 1) * P])])
            load_out(0)
            load_out(1)
            sp.wait_ge(v_s.sem, v_s.at(l, 1))
            sp.dma_start(uv[:, :, :], w_uv[l]).then_inc(uv_in.sem, 16)
            for b in range(DECB):
                if b == 0:
                    sp.wait_ge(out_hm.sem, out_hm.at(l, 80))
                    sp.wait_ge(v_t.sem, v_t.at(l, 4))
                if b == 2:
                    sp.wait_ge(p_s.sem, p_s.at(l, 16))
                tiles = cache(b)[:, 0:768].rearrange("p (k n) -> p k n", k=2)
                sp.dma_start(tiles[:, :, 0:KL], a["cache_mla_ckv"][l][b].rearrange("(k p) c -> p k c", p=P)).then_inc(cache_in[b].sem, 16)
                for twice in range(2):
                    r = KL + 64 * twice
                    sp.dma_start(tiles[:, :, r:r + 64], a["cache_mla_krope"][l][b].rearrange("(k p) c -> p k c", p=P)).then_inc(cache_in[b].sem, 16)
                sp.dma_start(cache(b)[0:16, 768:1024], a["out_ckvs"][l][b]).then_inc(cache_in[b].sem, 16)
            for d in range(2, NC_):
                load_out(d)
            for blk in range(NBLK):
                u0 = U_FFN + blk * BLK_U
                for i in range(FT):
                    cols = slice((blk * FT + i) * P, (blk * FT + i + 1) * P)
                    load(u0 + 2 * i, [(0, 0, P, w_gate[l][:, :, cols])])
                    load(u0 + 2 * i + 1, [(0, 0, P, w_up[l][:, :, cols])])
                for d in range(NC_):
                    load(u0 + 2 * FT + d, [(0, 0, P, w_down[l][:, blk * FT:(blk + 1) * FT, d * P:(d + 1) * P])])
        for t in range(NT):
            sp.wait_ge(y_act.sem, t + 1)
            sp.wait_ge(y_dve.sem, t + 1)
            dst = a["out_y"][0, tok(t), :] if t < TS else a["out_ys"].rearrange("b s d -> (b s) d")
            sp.dma_start(dst, yout[:, t, :]).then_inc(out_y.sem, 16)
        sp.wait_ge(out_y.sem, 16 * NT)
        sp.wait_ge(out_hm.sem, 80 * DEPTH)
        sp.wait_ge(out_ckv.sem, 16 * DEPTH)
        sp.wait_ge(out_sample.sem, 32 * DEPTH)
        sp.wait_ge(out_copy.sem, 32 * DEPTH)

    @block.tensor
    def _(pe):
        mm, turn = nc.tensor.matmul, nc.tensor.transpose

        def unit_parts(u, n):
            s = unit_slot(u)
            return [w[:, slot(s, unit_width(u))].rearrange("p (k n) -> p k n", n=n) for w in (whi, wlo)]

        def by_weights(outs, w, k, cols, xh, xl, first, last):
            for part, (wt, xs) in enumerate(((w[0], (xh, xl)), (w[1], (xh,)))):
                for x in xs:
                    for j in range(2):
                        ins = mm(outs[j], wt[:, k, cols], x[:, half(j)], start=first and part == 0 and x is xh,
                                 stop=last and part == 1)
            return ins

        def sums(source, bank, col):
            for t in range(NT):
                ins = mm(ps[:, bank, col + t:col + t + 1], source[:, tok(t)], one, start=True, stop=True)
            ins.then_inc(stat_sum.sem, 1)

        def spread(n, bank):
            for t in range(NT):
                ins = mm(ps[:, bank + t // 4, (t % 4) * P:(t % 4 + 1) * P], onesq, diag[:, NT * n + t, :], start=True, stop=True)
            ins.then_inc(bcast.sem, 1)

        pe.sem_inc(unit_used.sem, 2)
        pe.wait_ge(consts_in.sem, 32)
        pe.wait_ge(x_in.sem, 16 * NT)
        for c in range(NC_):
            if c >= 4:
                pe.wait_ge(x_new.sem, c - 3)
            for t in range(NT):
                bank = 2 * (c % 4) + t // 4
                ins = turn(ps[:, bank, (t % 4) * P:(t % 4 + 1) * P], xin[:, t, c * P:(c + 1) * P], ident)
            ins.then_inc(x_turned.sem, 1)
        for l in layers(pe):
            pe.wait_ge(x_new.sem, x_new.at(l, -1))
            for u in range(WIN_U):
                g, kp = divmod(u, 4)
                w = GROUPS[g][1]
                wh, wl = unit_parts(u, 512)
                pe.wait_ge(unit_lo.sem, unit_lo.at(l, u + 1))
                for t in range(NT):
                    i = g * NT + t
                    if kp == 0 and i >= 7:
                        pe.wait_ge(hm_new.sem, hm_new.at(l, i - 6))
                    for k in range(2):
                        c = 2 * kp + k
                        if g == 0 and t == 0:
                            pe.wait_ge(n_lo.sem, n_lo.at(l, c - 7))
                        o = ps[:, i % 7, 0:w]
                        mm(o, nh[:, c, tok(t)], wh[:, k, 0:w], start=c == 0, stop=False)
                        mm(o, nh[:, c, tok(t)], wl[:, k, 0:w], start=False, stop=False)
                        ins = mm(o, nl[:, c, tok(t)], wh[:, k, 0:w], start=False, stop=c == NC_ - 1)
                    if t == TS:
                        ins.then_inc(unit_used.sem, 1)
                    elif kp == 3:
                        ins.then_inc(in_done.sem, 1)
                if u == 3:
                    pe.wait_ge(ssq_new.sem, ssq_new.at(l, 0))
                    sums(ssq, 7, 0)
            def batch(bank, pieces, done):
                for j, src in enumerate(pieces):
                    ins = turn(ps[:, bank, j * P:(j + 1) * P], src, ident)
                ins.then_inc(done.sem, 1)

            pe.wait_ge(k_lo.sem, k_lo.at(l, 1))
            pe.wait_ge(ckv_norm.sem, ckv_norm.at(l, NT))
            pe.wait_ge(cq_norm.sem, cq_norm.at(l, NT))
            for t in range(NT):
                banks = (3, 4, 5) if t % 2 else (1, 2, 7)
                if t == 1:
                    pe.wait_ge(hm_new.sem, hm_new.at(l, 13))
                if t >= 2:
                    pe.wait_ge(k_act.sem, k_act.at(l, 3 * (t - 1)))
                    pe.wait_ge(k_dve.sem, k_dve.at(l, 2 * (t - 1)))
                latents = [ckv[:, t, c * P:(c + 1) * P] for c in range(2)]
                if t < TS:
                    pairs = [k2[:, t, 2 * x:2 * x + 2, :].rearrange("p a d -> p (a d)").bitcast(F32) for x in range(6)]
                    batch(banks[0], pairs[0:4], k_turned)
                    batch(banks[1], pairs[4:6] + latents, k_turned)
                else:
                    batch(banks[1], [hm[:, TS, C_K:C_V], krd[:, :, :].rearrange("p a d -> p (a d)")] + latents, k_turned)
                batch(banks[2], [hm[:, t, C_Q + k * P:C_Q + (k + 1) * P] for k in range(3)], k_turned)

            def rope_q(t):
                if t >= 2:
                    pe.wait_ge(uqr_new_read.sem, uqr_new_read.at(l, t - 1))
                for k in range(3):
                    o = ps[:, 2 if t % 2 else 5, 0:256]
                    mm(o, cqh[:, k, tok(t)], rope_cols(uq_hi, k), start=k == 0, stop=False)
                    mm(o, cqh[:, k, tok(t)], rope_cols(uq_lo, k), start=False, stop=False)
                    ins = mm(o, cql[:, k, tok(t)], rope_cols(uq_hi, k), start=False, stop=k == 2)
                ins.then_inc(uqr_done.sem, 1)

            def rope_q_turn(t):
                pe.wait_ge(uqr_lo.sem, uqr_lo.at(l, t + 1))
                if t >= 2:
                    pe.wait_ge(uqr_new.sem, uqr_new.at(l, t - 1))
                for h in range(BH):
                    ins = turn(ps[:, 1 if t % 2 else 7, h * P:(h + 1) * P], q2r[:, t % 2, h, :].bitcast(F32), ident)
                ins.then_inc(uqr_turned.sem, 1)

            def queries_turn(t):
                banks = (3, 4) if t % 2 else (6, 0)
                if t == 0:
                    pe.wait_ge(hm_new.sem, hm_new.at(l, 15))
                if t >= 2:
                    pe.wait_ge(q_act.sem, q_act.at(l, t - 1))
                    pe.wait_ge(q_dve.sem, q_dve.at(l, t - 1))
                if t < TS:
                    pe.wait_ge(q_lo.sem, q_lo.at(l, t + 1))
                    heads = [q2[:, t % 2, h, :].bitcast(F32) for h in range(AH)]
                    batch(banks[0], heads[0:4], q_turned)
                    batch(banks[1], heads[4:8], q_turned)
                else:
                    pe.wait_ge(q_hi.sem, q_hi.at(l, NT))
                    batch(banks[0], [q2s[:, g, :, :].rearrange("p e d -> p (e d)") for g in range(4)], q_turned)

            pe.wait_ge(unit_lo.sem, unit_lo.at(l, U_UQ + 1))
            pe.wait_ge(k_act.sem, k_act.at(l, 13))
            pe.wait_ge(k_dve.sem, k_dve.at(l, 10))
            rope_q(0)
            rope_q(1)
            for t in range(NT):
                queries_turn(t)
                rope_q_turn(t)
                if t + 2 < NT:
                    rope_q(t + 2)
            pe.wait_ge(q_dve.sem, q_dve.at(l, TS))
            pe.wait_ge(uqr_new_read.sem, uqr_new_read.at(l, NT))
            pe.wait_ge(raw_in[0].sem, raw_value(0, l, "uk"))
            for cc in range(2):
                for h in range(BH):
                    o = cc * 512 + h * P
                    ins = turn(ps[:, 4 + cc, h * P:(h + 1) * P], wraw[:, o:o + P], ident)
                ins.then_inc(uk_turned.sem, 1)
            pe.wait_ge(q_act.sem, q_act.at(l, NT))
            pe.wait_ge(uqr_new.sem, uqr_new.at(l, TS))
            pe.wait_ge(uqr_new_read.sem, uqr_new_read.at(l, NT))
            pe.wait_ge(v_new.sem, v_new.at(l, 1))

            def w_scores(n):
                i, kv = divmod(n, 2)
                k0 = max(i - 1, 0) * P
                if n >= 2:
                    pe.wait_ge(w_e.sem, w_e.at(l, n - 1))
                for g in range(4):
                    o = ps[:, 2 * (n % 2) + g // 2, (g % 2) * 256:(g % 2 + 1) * 256]
                    for x in range(2):
                        mm(o, qaT[:, kv * 4 + g, tok(i)], kaT[:, kv * 2 + x, k0:k0 + 256], start=x == 0, stop=False)
                    ins = mm(o, ident_r, mask_band if i else mask_first, start=False, stop=True)
                ins.then_inc(w_s.sem, 1)

            def w_turn(n):
                pe.wait_ge(w_p.sem, w_p.at(l, n + 1))
                for kt in range(2 if n >= 2 else 1):
                    if kt == 0 and n >= 1:
                        pe.wait_ge(w_tact.sem, w_tact.at(l, n))
                    if kt == 0 and n == 0:
                        pe.wait_ge(uk_lo.sem, uk_lo.at(l, 2))
                        pe.wait_ge(uqr_new.sem, uqr_new.at(l, NT))
                    if kt == 1 and n >= 3:
                        pe.wait_ge(w_tdve.sem, w_tdve.at(l, n - 2))
                    for g in range(4):
                        ins = turn(ps[:, 4 + kt, g * P:(g + 1) * P], pwb[n % 4][:, g, kt * P:(kt + 1) * P], ident)
                    ins.then_inc(w_t.sem, 1)

            def w_values(n):
                i, kv = divmod(n, 2)
                pe.wait_ge(w_tact.sem, w_tact.at(l, n + 1))
                if n >= 2:
                    pe.wait_ge(w_tdve.sem, w_tdve.at(l, n - 1))
                if kv == 0 and i >= 2:
                    pe.wait_ge(w_o.sem, w_o.at(l, i - 1))
                tiles = [0] if i == 0 else [i - 1, i]
                for kt, key in enumerate(tiles):
                    ins = mm(ps[kv * 64:kv * 64 + 64, 6 + i % 2, :], v[:, key, kv * 64:kv * 64 + 64], pt[:, kt, :],
                             start=kt == 0, stop=kt == len(tiles) - 1)
                ins.then_inc(w_pv.sem, 1)

            def q_nope(h):
                bank = 6 if h == 0 else 4
                for k in range(3):
                    ins = by_weights([ps[:, bank, 0:HALF], ps[:, bank + 1, 0:HALF]], (uq_hi, uq_lo), k,
                                     slice(h * (NOPE + ROPE), h * (NOPE + ROPE) + NOPE), cqh[:, k], cql[:, k], k == 0, k == 2)
                if h < BH - 1:
                    ins.then_inc(qn_done.sem, 1)
                else:
                    ins.then_inc(unit_used.sem, 1)

            w_scores(0)
            w_scores(1)
            pe.wait_ge(q_act.sem, q_act.at(l, NT))
            pe.wait_ge(uqr_new.sem, uqr_new.at(l, NT))
            q_nope(0)
            w_scores(2)
            for n in range(8):
                w_turn(n)
                if n + 3 < 8:
                    w_scores(n + 3)
                if n == 0:
                    pe.wait_ge(qn_lo.sem, qn_lo.at(l, 1))
                w_values(n)
            def q_latent(h):
                pe.wait_ge(qn_lo.sem, qn_lo.at(l, h + 1))
                for c in range(2):
                    bank = 4 + 2 * c
                    if h == 0 and c == 0:
                        pe.wait_ge(w_tact.sem, w_tact.at(l, 8))
                        pe.wait_ge(w_tdve.sem, w_tdve.at(l, 6))
                    if h >= 1 and c == 1:
                        if h == 1:
                            pe.wait_ge(v_o.sem, v_o.at(l, 1))
                        else:
                            pe.wait_ge(p_o.sem, p_o.at(l, h - 1))
                    if h == 0 and c == 1:
                        pe.wait_ge(w_o.sem, w_o.at(l, 4))
                        pe.wait_ge(v_ktact.sem, v_ktact.at(l, 1))
                        pe.wait_ge(v_knew.sem, v_knew.at(l, 1))
                    ins = by_weights([ps[:, bank, 0:HALF], ps[:, bank + 1, 0:HALF]], (ukh, ukl), h,
                                     slice(c * P, (c + 1) * P), qnh, qnl, True, True)
                    ins.then_inc(ql_done.sem, 1)

            def p_scores(h):
                pe.wait_ge(ql_lo.sem, ql_lo.at(l, 2 * h + 2))
                for i in range(TS):
                    w = max(256, (i + 1) * P)
                    o = ps[:, i, 0:w]
                    if h == 0:
                        if i == 0:
                            pe.wait_ge(v_e.sem, v_e.at(l, 1))
                    else:
                        pe.wait_ge(p_e.sem, p_e.at(l, 4 * (h - 1) + i + 1))
                    for c in range(2):
                        qh, ql = qlh[:, h % 2, c, tok(i)], qll[:, h % 2, c, tok(i)]
                        mm(o, qh, ckh[:, c, 0:w], start=c == 0, stop=False)
                        mm(o, qh, ckl[:, c, 0:w], start=False, stop=False)
                        mm(o, ql, ckh[:, c, 0:w], start=False, stop=False)
                    for x in range(2):
                        mm(o, qrT[:, h, tok(i)], krT[:, x, 0:w], start=False, stop=False)
                    ins = mm(ps[:, i, w - 256:w], ident_r, mask_own if i else mask_first, start=False, stop=True)
                    ins.then_inc(p_s.sem, 1)

            pe.wait_ge(win_in.sem, win_in.at(l, 32))
            pe.wait_ge(w_e.sem, w_e.at(l, 8))
            for b in range(DECB):
                ins = turn(ps[:, b // 4, (b % 4) * P:(b % 4 + 1) * P], wk[:, b, :], ident)
                if b % 4 == 3:
                    ins.then_inc(v_kt.sem, 1)
            q_latent(0)
            for b in range(DECB):
                for kv in range(2):
                    r = slice(kv * 64, kv * 64 + 64)
                    o = (b % 2) * 144
                    ins = mm(ps[r, b // 2, o:o + 144], qTs[r, b].rearrange("p g q -> p (g q)"), kTc[r, b, :], start=True, stop=True)
            ins.then_inc(v_s.sem, 1)
            pe.wait_ge(ql_lo.sem, ql_lo.at(l, 1))
            q_nope(1)
            pe.wait_ge(v_zero.sem, v_zero.at(l, 1))
            pe.wait_ge(v_p.sem, v_p.at(l, 1))
            pe.wait_ge(qn_lo.sem, qn_lo.at(l, 2))
            for j in range(4):
                if j == 2:
                    pe.wait_ge(v_tact.sem, v_tact.at(l, 1))
                if j == 3:
                    pe.wait_ge(v_tdve.sem, v_tdve.at(l, 1))
                for m in range(4):
                    b, kt = 2 * j + m // 2, m % 2
                    ins = turn(ps[:, 4 + j % 2, m * P:(m + 1) * P], pws[:, b, kt * P:(kt + 1) * P], ident)
                ins.then_inc(v_t.sem, 1)
            p_scores(0)
            pe.wait_ge(vnew_in.sem, vnew_in.at(l, 16))
            pe.wait_ge(v_tact.sem, v_tact.at(l, 2))
            pe.wait_ge(v_tdve.sem, v_tdve.at(l, 2))
            for b in range(DECB):
                for kv in range(2):
                    r = slice(kv * 64, kv * 64 + 64)
                    o = ps[r, 6, b * 64:(b + 1) * 64]
                    mm(o, wv[:, b, r], ptw[:, b, 0, r], start=True, stop=False)
                    ins = mm(o, vn[:, b, r], ptw[0:DECS, b, 1, r], start=False, stop=True)
            ins.then_inc(v_pv.sem, 1)

            def p_turn(h):
                pe.wait_ge(p_p.sem, p_p.at(l, 4 * h + 4))
                for j in range(TS):
                    if j == 0:
                        if h < BH - 1:
                            pe.wait_ge(ql_hi.sem, ql_hi.at(l, 2 * h + 3))
                            pe.wait_ge(ql_lo.sem, ql_lo.at(l, 2 * h + 3))
                        else:
                            pe.wait_ge(p_tact.sem, p_tact.at(l, 2 * h))
                            pe.wait_ge(p_tdve.sem, p_tdve.at(l, 2 * h))
                    if j == 2:
                        pe.wait_ge(p_tact.sem, p_tact.at(l, 2 * h + 1))
                    if j == 3:
                        pe.wait_ge(p_tdve.sem, p_tdve.at(l, 2 * h + 1))
                    for i in range(j, TS):
                        ins = turn(ps[:, 4 + j % 2, (i - j) * P:(i - j + 1) * P], pm[:, POFF[i] + j * P:POFF[i] + (j + 1) * P], ident)
                    ins.then_inc(p_t.sem, 1)

            def p_values(h):
                pe.wait_ge(p_tact.sem, p_tact.at(l, 2 * h + 2))
                pe.wait_ge(p_tdve.sem, p_tdve.at(l, 2 * h + 2))
                if h == BH - 1:
                    pe.wait_ge(p_o.sem, p_o.at(l, h))
                for c in range(2):
                    for j in range(TS):
                        ins = mm(ps[:, 6 + c, j * P:512], ckv[:, j, c * P:(c + 1) * P], ptm[:, TOFF[j]:TOFF[j] + (4 - j) * P],
                                 start=j == 0, stop=j == TS - 1)
                    ins.then_inc(p_pv.sem, 1)

            def p_out(h):
                if h == 0:
                    pe.wait_ge(uv_in.sem, uv_in.at(l, 16))
                pe.wait_ge(p_lat.sem, p_lat.at(l, h + 1))
                pe.wait_ge(p_latd.sem, p_latd.at(l, h + 1))
                for cc in range(2):
                    ins = mm(ps[:, 6, :], uv[:, cc, h * P:(h + 1) * P], olat[:, cc, :], start=cc == 0, stop=cc == 1)
                ins.then_inc(p_ob.sem, 1)

            def c_turn(b):
                pe.wait_ge(cache_in[b].sem, cache_in[b].at(l, 64))
                if b >= 2:
                    pe.wait_ge(c_act.sem, c_act.at(l, b - 1))
                    pe.wait_ge(c_dve.sem, c_dve.at(l, b - 1))
                for c in range(3):
                    for kt in range(2):
                        o = (c % 2) * 256 + kt * P
                        ins = turn(ps[:, 2 + 2 * (b % 2) + c // 2, o:o + P], cache(b)[:, kt * 384 + c * P:kt * 384 + (c + 1) * P], ident)
                ins.then_inc(c_t.sem, 1)

            def c_score(b):
                pe.wait_ge(c_act.sem, c_act.at(l, b + 1))
                pe.wait_ge(c_dve.sem, c_dve.at(l, b + 1))
                if b % 2 == 0 and b >= 4:
                    pe.wait_ge(c_e.sem, c_e.at(l, b // 2 - 1))
                r = slice((b % 2) * 64, (b % 2) * 64 + 64)
                keys = cTo if b % 2 else cT
                for c in range(3):
                    q = (qlTs[:, c, b] if c < 2 else qrTs[:, b]).rearrange("p h q -> p (h q)")
                    ins = mm(ps[r, (b // 2) % 2, 0:272], q, keys[:, c, :], start=c == 0, stop=c == 2)
                ins.then_inc(c_s.sem, 1)

            def c_probs(p):
                if p == 0:
                    pe.wait_ge(c_zero.sem, c_zero.at(l, 1))
                    pe.wait_ge(p_o.sem, p_o.at(l, 4))
                else:
                    pe.wait_ge(c_ptact.sem, c_ptact.at(l, p))
                pe.wait_ge(c_p.sem, c_p.at(l, p + 1))
                for kt in range(3):
                    ins = turn(ps[:, 6, kt * P:(kt + 1) * P], psm[:, p % 2, kt * P:(kt + 1) * P], ident)
                ins.then_inc(c_pt.sem, 1)

            def c_values(p):
                pe.wait_ge(c_ptact.sem, c_ptact.at(l, p + 1))
                if p >= 1:
                    pe.wait_ge(c_ltact.sem, c_ltact.at(l, p))
                for b in (2 * p, 2 * p + 1):
                    r = slice((b % 2) * 64, (b % 2) * 64 + 64)
                    for kt in range(2):
                        mm(ps[r, 7, 0:KL], pts[:, kt, r], cache(b)[:, kt * 384:kt * 384 + KL], start=kt == 0, stop=False)
                    ins = mm(ps[r, 7, 0:KL], pts[0:DECS, 2, r], cache(b)[0:DECS, 768:1024], start=False, stop=True)
                    ins.then_inc(c_pv.sem, 1)

            def c_lat_turn(p):
                pe.wait_ge(c_lat.sem, c_lat.at(l, p + 1))
                for c in range(2):
                    ins = turn(ps[:, 7, 256 + c * P:256 + (c + 1) * P], olats[:, c * P:(c + 1) * P], ident)
                ins.then_inc(c_lt.sem, 1)

            for h in range(BH):
                if h + 1 < BH:
                    q_latent(h + 1)
                p_turn(h)
                if h + 1 < BH:
                    p_scores(h + 1)
                else:
                    c_turn(0)
                p_values(h)
                if h + 2 < BH:
                    q_nope(h + 2)
                if h == BH - 1:
                    c_turn(1)
                p_out(h)

            def out_part(d, group):
                u = U_OUT + d
                w = unit_parts(u, P)
                pe.wait_ge(unit_lo.sem, unit_lo.at(l, u + 1))
                if d >= 2:
                    pe.wait_ge(x_new.sem, x_new.at(l, d - 1))
                b0 = 4 * group + 2 * (d % 2)
                for c in range(4 * group, 4 * group + 4):
                    if d == 0:
                        pe.wait_ge(m_lo.sem, m_lo.at(l, c + 1))
                    ins = by_weights([ps[:, b0, 0:HALF], ps[:, b0 + 1, 0:HALF]], w, c, slice(0, P), mh[:, c], ml[:, c], c % 4 == 0, c % 4 == 3)
                if group == 1:
                    ins.then_inc(unit_used.sem, 1)

            for b in range(11):
                if 2 <= b + 1 < DECB:
                    c_turn(b + 1)
                if b % 2 and b >= 3:
                    c_probs((b - 3) // 2)
                if b < DECB:
                    c_score(b)
                if b == 9:
                    out_part(1, 0)
                if b % 2 and b >= 3:
                    c_values((b - 3) // 2)
                if b == 10:
                    pe.wait_ge(ssq_new.sem, ssq_new.at(l, 6))
                    sums(ssq, 5, 0)
                if b % 2 == 0 and b >= 4:
                    c_lat_turn((b - 4) // 2)
                if b == 8:
                    pe.wait_ge(c_e.sem, c_e.at(l, 4))
                    pe.wait_ge(c_act.sem, c_act.at(l, 8))
                    pe.wait_ge(c_dve.sem, c_dve.at(l, 8))
                    out_part(0, 0)
            pe.wait_ge(c_ltact.sem, c_ltact.at(l, 4))
            for h in range(BH):
                for cc in range(2):
                    ins = mm(ps[:, 6, h * P:(h + 1) * P], uv[:, cc, h * P:(h + 1) * P], olTs[:, cc, h, :], start=cc == 0, stop=cc == 1)
            ins.then_inc(c_ob.sem, 1)
            pe.wait_ge(c_o.sem, c_o.at(l, 1))
            pe.wait_ge(diag_new.sem, diag_new.at(l, 1))
            spread(0, 6)
            out_part(0, 1)
            pe.wait_ge(ssq_new.sem, ssq_new.at(l, 9))
            pe.wait_ge(r_new.sem, r_new.at(l, 1))
            sums(ssqB, 7, 500)
            pe.wait_ge(diag_new.sem, diag_new.at(l, 2))
            spread(1, 6)
            pe.wait_ge(dve_r.sem, dve_r.at(l, 1))
            out_part(1, 1)
            for d in range(2, NC_):
                out_part(d, 0)
                out_part(d, 1)

            for blk in range(NBLK):
                u0 = U_FFN + blk * BLK_U
                for i in range(FT):
                    n = blk * FT + i
                    base = 4 * (i % 2)
                    if i < 2:
                        pe.wait_ge(x_new.sem, x_new.at(l, 8 + 8 * blk - 1 + i))
                    else:
                        pe.wait_ge(u_scaled.sem, u_scaled.at(l, n - 1))
                    for up in range(2):
                        u = u0 + 2 * i + up
                        pe.wait_ge(unit_lo.sem, unit_lo.at(l, u + 1))
                        w = unit_parts(u, P)
                        for c in range(NC_):
                            if n == 0 and up == 0:
                                pe.wait_ge(n_lo.sem, n_lo.at(l, c + 1))
                            b0 = base + 2 * up
                            ins = by_weights([ps[:, b0, 0:HALF], ps[:, b0 + 1, 0:HALF]], w, c, slice(0, P), nh[:, c], nl[:, c], c == 0, c == NC_ - 1)
                        ins.then_inc(unit_used.sem, 1)
                        if n == 0 and up == 0:
                            pe.wait_ge(ssq_new.sem, ssq_new.at(l, 16))
                            sums(ssq, 7, 500)
                        if n == 0 and up == 1:
                            pe.wait_ge(diag_new.sem, diag_new.at(l, 3))
                            spread(0, 4)
                            pe.wait_ge(r_new.sem, r_new.at(l, 2))
                for d in range(NC_):
                    u = u0 + 2 * FT + d
                    w = unit_parts(u, P)
                    b0 = 2 * DOWN_PAIR[d]
                    pe.wait_ge(unit_lo.sem, unit_lo.at(l, u + 1))
                    if d < 4:
                        pe.wait_ge(u_scaled.sem, u_scaled.at(l, blk * FT + (FT - 1 if d < 2 else FT)))
                    elif d < 6:
                        pe.wait_ge(x_new.sem, x_new.at(l, 8 + 8 * blk + d - 1))
                    for f in range(FT):
                        if d == 0:
                            pe.wait_ge(h_lo.sem, h_lo.at(l, blk * FT + f + 1))
                        ins = by_weights([ps[:, b0, 0:HALF], ps[:, b0 + 1, 0:HALF]], w, f, slice(0, P), hh[:, f], hl[:, f], f == 0, f == FT - 1)
                    ins.then_inc(unit_used.sem, 1)
        pe.wait_ge(ssq_new.sem, ssq_new.at(DEPTH, 0))
        pe.wait_ge(n_lo.sem, n_lo.at(DEPTH, 0))
        sums(ssq, 7, 500)
        pe.wait_ge(y_gain.sem, NC_)
        pe.wait_ge(stat_sd.sem, stat_sd.at(DEPTH, 1))
        for t in range(NT):
            if t >= 3:
                pe.wait_ge(y_act.sem, t - 2)
                pe.wait_ge(y_dve.sem, t - 2)
            for c in range(NC_):
                ins = turn(ps[:, 2 * (t % 3) + c // 4, (c % 4) * P:(c % 4 + 1) * P], xT[:, c, tok(t)], ident)
            ins.then_inc(y_turned.sem, 1)

    def adds_before(c):
        return 0 if c < 2 else max(1, c - 2)

    @block.scalar
    def _(act):
        run = nc.scalar.activation

        def normed(l, c, src, gain, hi, hi_done, sq_done_before):
            run(hi[:, c, :], src[:, c, :], ACT.Copy, scale=gain).then_inc(hi_done.sem, 1)
            act.wait_ge(ssq_new.sem, sq_done_before)
            run(sq[:, c % 2, :], src[:, c, :], ACT.Square).then_inc(sq_new.sem, 1)

        def weight_hi(l, u):
            s = unit_slot(u)
            act.wait_ge(raw_in[s].sem, raw_value(s, l, u))
            act.wait_ge(unit_used.sem, unit_used.at(l, used_before(u)))
            run(whi[:, slot(s, unit_width(u))], wraw[:, slot(s, unit_width(u))], ACT.Copy).then_inc(unit_hi.sem, 1)

        act.wait_ge(consts_in.sem, 32)
        for c in range(NC_):
            act.wait_ge(x_turned.sem, c + 1)
            turned = ps[:, 2 * (c % 4):2 * (c % 4) + 2, :].rearrange("p a n -> p (a n)")[:, 0:T]
            run(nh[:, c, :], turned, ACT.Copy, scale=kc[:, K_GAIN + c:K_GAIN + c + 1]).then_inc(n_hi.sem, 1)
        for l in layers(act):
            weight_hi(l, 0)
            weight_hi(l, 1)
            for u in range(WIN_U):
                g, kp = divmod(u, 4)
                if u + 2 < WIN_U:
                    weight_hi(l, u + 2)
                if kp == 3:
                    if g == 0:
                        act.wait_ge(stat_sum.sem, stat_sum.at(l, 1))
                        run(sd[:, 0:NT], ps[:, 7, 0:NT], ACT.Sqrt, bias=eps, scale=1.0 / D).then_inc(stat_sd.sem, 1)
                        act.wait_ge(stat_r.sem, stat_r.at(l, 1))
                    c0, w = GROUPS[g]
                    for t in range(NT):
                        if t < TS:
                            act.wait_ge(in_done.sem, in_done.at(l, 4 * g + t + 1))
                        else:
                            act.wait_ge(unit_used.sem, unit_used.at(l, u + 1))
                        run(hm[:, t, c0:c0 + w], ps[:, (g * NT + t) % 7, 0:w], ACT.Copy, scale=rs[:, t:t + 1]).then_inc(hm_new.sem, 1)
                    if g == 1:
                        act.wait_ge(hm_new.sem, hm_new.at(l, 10))
                        for t in range(NT):
                            run(junk[:, t, 0:QL], hm[:, t, C_Q:C_KV], ACT.Square, scale=QL ** -0.5, accum_out=ms[:, t:t + 1]).then_inc(lat_ms.sem, 1)
                            run(junk[:, t, QL:], hm[:, t, C_KV:C_KR], ACT.Square, scale=KL ** -0.5, accum_out=ms[:, NT + t:NT + t + 1]).then_inc(lat_ms.sem, 1)
                        act.wait_ge(lat_ms.sem, lat_ms.at(l, 10))
                        run(sd[:, 0:10], ms[:, 0:10], ACT.Sqrt, bias=eps).then_inc(stat_sd.sem, 1)
                        run(v[:, :, :], hm[:, :, C_V:C_Q], ACT.Copy).then_inc(v_new.sem, 1)
                if u == 8:
                    act.wait_ge(k_roped.sem, k_roped.at(l, 1))
                    k = hm[:, 0:TS, C_K:C_V].rearrange("p t (h d) -> p t h d", d=64)
                    for x in range(2):
                        run(k2[:, :, x:8:4, :], k, ACT.Copy)
                    for x in range(2):
                        run(k2[:, :, 8 + x, :], hm[:, 0:TS, C_KR:IN_W], ACT.Copy)
                    for x in range(2):
                        ins = run(krd[:, x, :], hm[:, TS, C_KR:IN_W], ACT.Copy)
                    ins.then_inc(k_hi.sem, 1)

            def keys_out_act(t):
                banks = (3, 4, 5) if t % 2 else (1, 2, 7)
                if t < TS:
                    act.wait_ge(k_turned.sem, k_turned.at(l, 3 * t + 1))
                    run(kaT[:, :, tok(t)], ps[:, banks[0], :].rearrange("p (h n) -> p h n", h=4), ACT.Copy).then_inc(k_act.sem, 1)
                    act.wait_ge(k_turned.sem, k_turned.at(l, 3 * t + 2))
                    run(ckh[:, :, tok(t)], ps[:, banks[1], 256:512].rearrange("p (h n) -> p h n", h=2), ACT.Copy).then_inc(k_act.sem, 1)
                act.wait_ge(k_turned.sem, k_turned.at(l, min(3 * t + 3, 14)))
                for k in range(3):
                    ins = run(cqh[:, k, tok(t)], ps[:, banks[2], k * P:(k + 1) * P], ACT.Copy, scale=gv[:, G_Q + k:G_Q + k + 1])
                ins.then_inc(k_act.sem, 1)

            def queries_hi(t):
                act.wait_ge(q_roped.sem, q_roped.at(l, t + 1))
                if t < 2:
                    act.wait_ge(k_turned.sem, k_turned.at(l, 3 * t + 5))
                else:
                    act.wait_ge(q_turned.sem, q_turned.at(l, 2 * (t - 1)))
                q = hm[:, t, 0:C_K]
                if t < TS:
                    run(q2[:, t % 2, :, 0:64], q.rearrange("p (h d) -> p h d", d=64), ACT.Copy).then_inc(q_hi.sem, 1)
                else:
                    run(q2s[:, :, :, :], q.rearrange("p (e g d) -> p g e d", e=2, g=4), ACT.Copy).then_inc(q_hi.sem, 1)

            def queries_out_act(t):
                bank = 3 if t % 2 else 6
                act.wait_ge(q_turned.sem, q_turned.at(l, 2 * t + 1))
                if t < TS:
                    run(qaT[:, 0:4, tok(t)], ps[:, bank, :].rearrange("p (h n) -> p h n", h=4), ACT.Copy).then_inc(q_act.sem, 1)
                else:
                    run(qTs[:, :, :, :], ps[:, bank, :].rearrange("p (g b q) -> p b g q", g=4, b=DECB), ACT.Copy).then_inc(q_act.sem, 1)

            def rope_q_hi(t):
                act.wait_ge(uqr_rope.sem, uqr_rope.at(l, t + 1))
                if t >= 2:
                    act.wait_ge(uqr_turned.sem, uqr_turned.at(l, t - 1))
                run(q2r[:, t % 2, :, 0:64], qra[:, t % 2, :].rearrange("p (h d) -> p h d", d=64), ACT.Copy).then_inc(uqr_hi.sem, 1)

            def rope_q_out(t):
                act.wait_ge(uqr_turned.sem, uqr_turned.at(l, t + 1))
                src = ps[:, 1 if t % 2 else 7, :]
                if t < TS:
                    dst, src = qrT[:, :, tok(t)], src.rearrange("p (h n) -> p h n", h=BH)
                else:
                    dst, src = qrTs[:, :, :, :], src.rearrange("p (h b q) -> p b h q", h=BH, b=DECB)
                run(dst, src, ACT.Copy).then_inc(uqr_new.sem, 1)

            keys_out_act(0)
            keys_out_act(1)
            weight_hi(l, U_UQ)
            queries_hi(0)
            keys_out_act(2)
            queries_hi(1)
            keys_out_act(3)
            keys_out_act(4)
            rope_q_hi(0)
            queries_out_act(0)
            for t in range(1, NT):
                if t + 1 < NT:
                    queries_hi(t + 1)
                rope_q_hi(t)
                rope_q_out(t - 1)
                queries_out_act(t)
            rope_q_out(TS)
            for cc in range(2):
                act.wait_ge(uk_turned.sem, uk_turned.at(l, cc + 1))
                run(ukh[:, :, cc * P:(cc + 1) * P], ps[:, 4 + cc, :].rearrange("p (h n) -> p h n", h=BH), ACT.Copy).then_inc(uk_hi.sem, 1)

            def w_exps(n):
                act.wait_ge(w_nm.sem, w_nm.at(l, n + 1))
                if n >= 4:
                    act.wait_ge(w_t.sem, w_t.at(l, turned_by(n - 4)))
                for g in range(4):
                    run(pwb[n % 4][:, g, :], ps[:, 2 * (n % 2) + g // 2, (g % 2) * 256:(g % 2 + 1) * 256], ACT.Exp,
                        bias=four_of(nm, n)[:, g:g + 1], scale=A_SCALE, accum_out=four_of(rsum, n)[:, g:g + 1])
                run(four_of(es, n), four_of(ed, n), ACT.Exp).then_inc(w_e.sem, 1)

            def w_out_act(i):
                act.wait_ge(w_pv.sem, w_pv.at(l, 2 * i + 2))
                run(oT[:, 0:4, tok(i)], ps[:, 6 + i % 2, :].rearrange("p (g n) -> p g n", g=4), ACT.Copy).then_inc(w_o.sem, 1)

            def q_nope_hi(h):
                if h < BH - 1:
                    act.wait_ge(qn_done.sem, qn_done.at(l, h + 1))
                else:
                    act.wait_ge(unit_used.sem, unit_used.at(l, U_UQ + 1))
                bank = 6 if h == 0 else 4
                run(halves(qnh[:, :]), ps[:, bank:bank + 2, 0:HALF], ACT.Copy).then_inc(qn_hi.sem, 1)

            w_exps(0)
            w_exps(1)
            q_nope_hi(0)
            act.wait_ge(out_hm.sem, out_hm.at(l, 80))
            w_exps(2)
            for n in range(8):
                act.wait_ge(w_t.sem, w_t.at(l, turned_by(n) - (n >= 2)))
                if n >= 1:
                    act.wait_ge(w_pv.sem, w_pv.at(l, n))
                run(pt[:, 0, :], ps[:, 4, :], ACT.Copy).then_inc(w_tact.sem, 1)
                if n + 3 < 8:
                    w_exps(n + 3)
                if n >= 2 and n % 2 == 0:
                    w_out_act(n // 2 - 1)
            w_out_act(3)
            def q_latent_hi(h):
                rest = PROMPT - HALF
                for c in range(2):
                    act.wait_ge(ql_done.sem, ql_done.at(l, 2 * h + c + 1))
                    bank = 4 + 2 * c
                    run(qlh[:, h % 2, c, 0:HALF], ps[:, bank, 0:HALF], ACT.Copy)
                    run(qlh[:, h % 2, c, HALF:PROMPT], ps[:, bank + 1, 0:rest], ACT.Copy)
                    run(qlTs[:, c, :, h, :], ps[:, bank + 1, rest:HALF].rearrange("p (b q) -> p b q", b=DECB), ACT.Copy).then_inc(ql_hi.sem, 1)

            def p_exps(h):
                for i in range(TS):
                    w = (i + 1) * P
                    act.wait_ge(p_nm.sem, p_nm.at(l, 4 * h + i + 1))
                    if h >= 1 and i == 0:
                        act.wait_ge(p_t.sem, p_t.at(l, 4 * h))
                    run(pm[:, POFF[i]:POFF[i] + w], ps[:, i, 0:w], ACT.Exp, bias=nm[0][:, i:i + 1], scale=B_SCALE,
                        accum_out=rsum[0][:, i:i + 1]).then_inc(p_e.sem, 1)

            act.wait_ge(v_kt.sem, v_kt.at(l, 1))
            run(kTc[:, 0:4, 0:P], ps[:, 0, :].rearrange("p (b n) -> p b n", b=4), ACT.Copy).then_inc(v_ktact.sem, 1)
            q_latent_hi(0)
            act.wait_ge(v_nm.sem, v_nm.at(l, 1))
            for b in range(DECB):
                run(pws[:, b, 0:144], ps[:, b // 2, (b % 2) * 144:(b % 2 + 1) * 144], ACT.Exp, bias=nm[0][:, b:b + 1],
                    scale=A_SCALE, accum_out=rsum[0][:, b:b + 1])
            run(es[0][:, 0:8], nm[0][:, 0:8], ACT.Exp, bias=gv[:, G_SINKS:G_SINKS + 1]).then_inc(v_e.sem, 1)
            q_nope_hi(1)
            for j in (0, 2):
                act.wait_ge(v_t.sem, v_t.at(l, j + 1))
                run(ptw[:, 2 * j:2 * j + 2, :, :], ps[:, 4, :].rearrange("p (b k n) -> p b k n", b=2, k=2), ACT.Copy).then_inc(v_tact.sem, 1)
            p_exps(0)
            act.wait_ge(v_pv.sem, v_pv.at(l, 1))
            for g in range(4):
                ins = run(oT[:, g, PROMPT:T].rearrange("p (b q) -> p b q", b=DECB),
                          ps[:, 6, :].rearrange("p (b g q) -> p b g q", b=DECB, g=4)[:, :, g, :], ACT.Copy)
            ins.then_inc(v_o.sem, 1)

            def keys_copy(b):
                act.wait_ge(c_t.sem, c_t.at(l, b + 1))
                if b >= 2:
                    act.wait_ge(c_s.sem, c_s.at(l, b - 1))
                keys, bank = (cTo, 4) if b % 2 else (cT, 2)
                run(keys[:, 0:2, 0:PAST], ps[:, bank, :].rearrange("p (c n) -> p c n", c=2), ACT.Copy).then_inc(c_act.sem, 1)

            for h in range(BH):
                if h + 1 < BH:
                    q_latent_hi(h + 1)
                for j in (0, 2):
                    act.wait_ge(p_t.sem, p_t.at(l, 4 * h + j + 1))
                    run(ptm[:, TOFF[j]:TOFF[j] + (4 - j) * P], ps[:, 4, 0:(4 - j) * P], ACT.Copy).then_inc(p_tact.sem, 1)
                if h + 1 < BH:
                    p_exps(h + 1)
                else:
                    keys_copy(0)
                act.wait_ge(p_pv.sem, p_pv.at(l, 2 * h + 1))
                run(olat[:, 0, :], ps[:, 6, :], ACT.Copy).then_inc(p_lat.sem, 1)
                if h + 2 < BH:
                    q_nope_hi(h + 2)
                if h == BH - 1:
                    keys_copy(1)
                act.wait_ge(p_ob.sem, p_ob.at(l, h + 1))
                run(oT[:, 4 + h, 0:PROMPT], ps[:, 6, :], ACT.Copy).then_inc(p_o.sem, 1)
                act.wait_ge(p_o.sem, p_o.at(l, h + 1))
                act.wait_ge(ssq_new.sem, ssq_new.at(l, h // 2))
                run(sq[:, h % 2, 0:PROMPT], oT[:, 4 + h, 0:PROMPT], ACT.Square).then_inc(sq_new.sem, 1)
            weight_hi(l, U_OUT)
            weight_hi(l, U_OUT + 1)

            def mixed(c):
                run(mh[:, c, :], oT[:, c, :], ACT.Copy, scale=gv[:, G_MIX + c:G_MIX + c + 1]).then_inc(m_hi.sem, 1)

            def mixed_square(c):
                act.wait_ge(ssq_new.sem, ssq_new.at(l, min(c + 2, 4)))
                run(sq[:, c % 2, :], oT[:, c, :], ACT.Square).then_inc(sq_new.sem, 1)

            def spread_out(k, read):
                act.wait_ge(bcast.sem, bcast.at(l, k))
                run(rA[:, :], read.rearrange("p a n -> p (a n)")[:, 0:T], ACT.Copy).then_inc(r_new.sem, 1)

            act.wait_ge(out_ckv.sem, out_ckv.at(l, 16))
            for b in range(11):
                if 2 <= b + 1 < DECB:
                    keys_copy(b + 1)
                if b % 2 and b >= 3:
                    p = (b - 3) // 2
                    act.wait_ge(c_pt.sem, c_pt.at(l, p + 1))
                    run(pts[:, :, :], ps[:, 6, 0:384].rearrange("p (k n) -> p k n", k=3), ACT.Copy).then_inc(c_ptact.sem, 1)
                if b % 2 and b < DECB:
                    p = b // 2
                    act.wait_ge(c_nm.sem, c_nm.at(l, p + 1))
                    if p >= 2:
                        act.wait_ge(c_pt.sem, c_pt.at(l, p - 1))
                    run(psm[:, p % 2, 0:272], ps[:, p % 2, 0:272], ACT.Exp, bias=nm[1][:, p:p + 1], scale=B_SCALE,
                        accum_out=rsum[1][:, p:p + 1]).then_inc(c_e.sem, 1)
                    mixed(p)
                    mixed_square(p)
                if b == 10:
                    act.wait_ge(stat_sum.sem, stat_sum.at(l, 2))
                    run(sd[:, 0:NT], ps[:, 5, 0:NT], ACT.Sqrt, bias=eps, scale=2.0 / D).then_inc(stat_sd.sem, 1)
                if b % 2 == 0 and b >= 4:
                    p = (b - 4) // 2
                    act.wait_ge(c_lt.sem, c_lt.at(l, p + 1))
                    for c in range(2):
                        dst = olTs[:, c, :, 32 * p:32 * (p + 1)].rearrange("p h (b q) -> p h b q", b=2)
                        src = ps[:, 7, 256 + c * P:256 + (c + 1) * P].rearrange("p (b h q) -> p h b q", b=2, h=BH)
                        ins = run(dst, src, ACT.Copy)
                    ins.then_inc(c_ltact.sem, 1)
            act.wait_ge(c_ob.sem, c_ob.at(l, 1))
            run(oT[:, 4:8, PROMPT:T], ps[:, 6, :].rearrange("p (h n) -> p h n", h=BH), ACT.Copy).then_inc(c_o.sem, 1)
            act.wait_ge(c_o.sem, c_o.at(l, 1))
            mixed(4)
            act.wait_ge(ssq_new.sem, ssq_new.at(l, 5))
            run(sq[:, 0, 0:PROMPT].rearrange("p (h n) -> p h n", h=BH), oT[:, 4:8, PROMPT:T], ACT.Square).then_inc(sq_new.sem, 1)
            mixed(5)
            spread_out(1, ps[:, 6:8, :])
            mixed(6)
            mixed(7)
            act.wait_ge(stat_sum.sem, stat_sum.at(l, 3))
            run(sd[:, NT:10], ps[:, 7, 500:505], ACT.Sqrt, bias=eps, scale=2.0 / D).then_inc(stat_sd.sem, 1)
            for d in range(NC_):
                weight_hi(l, U_OUT + d + 2)
                act.wait_ge(x_new.sem, x_new.at(l, d + 1))
                normed(l, d, xT, gv[:, G_FFN + d:G_FFN + d + 1], nh, n_hi, ssq_new.at(l, 9 + adds_before(d)))
            for blk in range(NBLK):
                u0 = U_FFN + blk * BLK_U
                for i in range(FT):
                    n = blk * FT + i
                    weight_hi(l, u0 + 2 * i + 2)
                    if n == 0:
                        act.wait_ge(stat_sum.sem, stat_sum.at(l, 4))
                        run(sd[:, 0:NT], ps[:, 7, 500:505], ACT.Sqrt, bias=eps, scale=1.0 / D).then_inc(stat_sd.sem, 1)
                        spread_out(3, ps[:, 4:6, :])
                    act.wait_ge(g_scaled.sem, g_scaled.at(l, n + 1))
                    run(tg[:, i % 2, :], tg[:, i % 2, :], ACT.Silu).then_inc(silu_new.sem, 1)
                    weight_hi(l, u0 + 2 * i + 3)
                    act.wait_ge(h_new.sem, h_new.at(l, n + 1))
                    run(hh[:, i, :], tu[:, i % 2, :], ACT.Copy).then_inc(h_hi.sem, 1)
                for d in range(NC_):
                    u = u0 + 2 * FT + d
                    if u + 2 < UNITS:
                        weight_hi(l, u + 2)
                    if blk == NBLK - 1:
                        act.wait_ge(x_new.sem, x_new.at(l, 8 + 8 * blk + d + 1))
                        normed(l, d, xT, gv[:, G_NEXT + d:G_NEXT + d + 1], nh, n_hi, ssq_new.at(l, 16 + adds_before(d)))
        act.wait_ge(n_lo.sem, n_lo.at(DEPTH, 0))
        for c in range(NC_):
            run(xT[:, c, :], xT[:, c, :], ACT.Copy, scale=gv[:, G_NEXT + c:G_NEXT + c + 1]).then_inc(y_gain.sem, 1)
        act.wait_ge(stat_sum.sem, stat_sum.at(DEPTH, 1))
        run(sd[:, 0:NT], ps[:, 7, 500:505], ACT.Sqrt, bias=eps, scale=1.0 / D).then_inc(stat_sd.sem, 1)
        act.wait_ge(stat_r.sem, stat_r.at(DEPTH, 1))
        for t in range(NT):
            act.wait_ge(y_turned.sem, t + 1)
            run(yout[:, t, 0:512], ps[:, 2 * (t % 3), :], ACT.Copy, scale=rs[:, t:t + 1]).then_inc(y_act.sem, 1)

    @block.vector
    def _(dve):
        vec = nc.vector
        steps = [0]

        def weight_lo(l, u):
            s = unit_slot(u)
            dve.wait_ge(unit_hi.sem, unit_hi.at(l, u + 1))
            w = slot(s, unit_width(u))
            vec.tensor_tensor(wlo[:, w], wraw[:, w], whi[:, w], ALU.subtract).then_inc(unit_lo.sem, 1)

        def low(out, src, gain, high):
            return vec.scalar_tensor_tensor(out=out, in0=src, scalar=gain, in1=high, op0=ALU.mult, op1=ALU.subtract)

        dve.sem_inc(unit_lo.sem, 2)
        dve.wait_ge(consts_in.sem, 32)
        vec.tensor_copy(kmask[:, :], mask_in[:, :])
        for c in range(NC_):
            dve.wait_ge(n_hi.sem, c + 1)
            turned = ps[:, 2 * (c % 4):2 * (c % 4) + 2, :].rearrange("p a n -> p (a n)")[:, 0:T]
            vec.tensor_copy(xT[:, c, :], turned).then_inc(x_new.sem, 1)
            dve.wait_ge(x_new.sem, c + 1)
            low(nl[:, c, :], xT[:, c, :], kc[:, K_GAIN + c:K_GAIN + c + 1], nh[:, c, :]).then_inc(n_lo.sem, 1)
        for l in layers(dve):
            steps[0] = 0

            def link(ins):
                steps[0] += 1
                ins.then_inc(dve_step.sem, 1)
                dve.wait_ge(dve_step.sem, dve_step.at(l, steps[0]))

            def rotate_keys():
                tables = kc[:, K_ROPE:K_ROPE + NT * 128].rearrange("p (t n) -> p t n", t=NT)
                for c0, heads in ((C_K, 2), (C_KR, 1)):
                    for h in range(heads):
                        col = c0 + 64 * h
                        src, o = hm[:, :, col:col + 64], slice(64 * h, 64 * h + 64)
                        vec.tensor_tensor(kcos[:, :, o], src, tables[:, :, 0:64], ALU.mult)
                        vec.tensor_tensor(ksin[:, :, 64 * h:64 * h + 32], src[:, :, 32:64], tables[:, :, 64:96], ALU.mult)
                        ins = vec.tensor_tensor(ksin[:, :, 64 * h + 32:64 * h + 64], src[:, :, 0:32], tables[:, :, 96:128], ALU.mult)
                    link(ins)
                    w = 64 * heads
                    ins = vec.tensor_tensor(hm[:, :, c0:c0 + w], kcos[:, :, 0:w], ksin[:, :, 0:w], ALU.add)
                    if heads == 2:
                        link(ins)
                ins.then_inc(k_roped.sem, 1)

            def rotate_queries(t):
                dve.wait_ge(hm_new.sem, hm_new.at(l, 10 + t + 1))
                q = hm[:, t, 0:C_K].rearrange("p (h d) -> p h d", d=64)
                a3, b3 = (x[:, t % 2, :].rearrange("p (h d) -> p h d", d=64) for x in (qcos, qsin))
                s3 = sin[t].unsqueeze(1)
                vec.tensor_tensor(b3[:, :, 0:32], q[:, :, 32:64], s3[:, :, 0:32].broadcast_to([P, AH, 32]), ALU.mult)
                link(vec.tensor_tensor(b3[:, :, 32:64], q[:, :, 0:32], s3[:, :, 32:64].broadcast_to([P, AH, 32]), ALU.mult))
                dve.wait_ge(q_cos.sem, q_cos.at(l, t + 1))
                vec.tensor_tensor(q, a3, b3, ALU.add).then_inc(q_roped.sem, 1)

            def latents_norm():
                dve.wait_ge(stat_sd.sem, stat_sd.at(l, 2))
                link(vec.reciprocal(rl[:, 0:10], sd[:, 0:10]))
                dve.wait_ge(vectors_in.sem, vectors_in.at(l, 32))
                for t in range(NT):
                    vec.scalar_tensor_tensor(out=ckv[:, t, :], in0=hm[:, t, C_KV:C_KR], scalar=rl[:, NT + t:NT + t + 1], in1=kvg[:, :],
                                             op0=ALU.mult, op1=ALU.mult).then_inc(ckv_norm.sem, 1)
                    q = hm[:, t, C_Q:C_KV]
                    vec.tensor_scalar(q, q, rl[:, t:t + 1], None, ALU.mult).then_inc(cq_norm.sem, 1)

            weight_lo(l, 0)
            weight_lo(l, 1)
            for u in range(WIN_U):
                if u + 2 < WIN_U:
                    weight_lo(l, u + 2)
                if u == 3:
                    dve.wait_ge(stat_sd.sem, stat_sd.at(l, 1))
                    vec.reciprocal(rs[:, 0:NT], sd[:, 0:NT]).then_inc(stat_r.sem, 1)
                if u == 7:
                    dve.wait_ge(hm_new.sem, hm_new.at(l, 10))
                    rotate_keys()
                if u == 8:
                    latents_norm()

            def keys_out_dve(t):
                banks = (3, 4, 5) if t % 2 else (1, 2, 7)
                four = ps[:, banks[1], :].rearrange("p (h n) -> p h n", h=4)
                if t < TS:
                    dve.wait_ge(k_turned.sem, k_turned.at(l, 3 * t + 2))
                    dve.wait_ge(k_act.sem, k_act.at(l, 3 * t + 2))
                    vec.tensor_copy(krT[:, :, tok(t)], four[:, 0:2, :])
                    vec.tensor_tensor(ckl[:, :, tok(t)], four[:, 2:4, :], ckh[:, :, tok(t)], ALU.subtract).then_inc(k_dve.sem, 1)
                else:
                    dve.wait_ge(k_turned.sem, k_turned.at(l, 13))
                    vec.tensor_copy(kTs[:, :], four[:, 0, :])
                    vec.tensor_copy(krTs[:, :], four[:, 1, :])
                    vec.tensor_copy(ckTs[:, :, :], four[:, 2:4, :]).then_inc(k_dve.sem, 1)
                dve.wait_ge(k_act.sem, k_act.at(l, min(3 * t + 3, 13)))
                for k in range(3):
                    ins = low(cql[:, k, tok(t)], ps[:, banks[2], k * P:(k + 1) * P], gv[:, G_Q + k:G_Q + k + 1], cqh[:, k, tok(t)])
                ins.then_inc(k_dve.sem, 1)

            def queries_out_dve(t):
                dve.wait_ge(q_turned.sem, q_turned.at(l, 2 * t + 2))
                vec.tensor_copy(qaT[:, 4:8, tok(t)], ps[:, 4 if t % 2 else 0, :].rearrange("p (h n) -> p h n", h=4)).then_inc(q_dve.sem, 1)

            def rotate_rope_queries(t):
                dve.wait_ge(uqr_done.sem, uqr_done.at(l, t + 1))
                src = ps[:, 2 if t % 2 else 5, 0:256].rearrange("p (h d) -> p h d", d=64)
                dst = qra[:, t % 2, :].rearrange("p (h d) -> p h d", d=64)
                c3 = cos[t].unsqueeze(1).broadcast_to([P, BH, 64])
                s3 = sin[t].unsqueeze(1)
                b3 = qrb[:, :].rearrange("p (h d) -> p h d", d=64)
                if t >= 1:
                    dve.wait_ge(uqr_rope.sem, uqr_rope.at(l, t))
                if t >= 2:
                    dve.wait_ge(uqr_lo.sem, uqr_lo.at(l, t - 1))
                vec.tensor_tensor(dst, src, c3, ALU.mult)
                vec.tensor_tensor(b3[:, :, 0:32], src[:, :, 32:64], s3[:, :, 0:32].broadcast_to([P, BH, 32]), ALU.mult)
                vec.tensor_tensor(b3[:, :, 32:64], src[:, :, 0:32], s3[:, :, 32:64].broadcast_to([P, BH, 32]), ALU.mult).then_inc(uqr_new_read.sem, 1)
                dve.wait_ge(uqr_new_read.sem, uqr_new_read.at(l, t + 1))
                vec.tensor_tensor(dst, dst, b3, ALU.add).then_inc(uqr_rope.sem, 1)

            rotate_queries(0)
            keys_out_dve(0)
            rotate_queries(1)
            keys_out_dve(1)
            weight_lo(l, U_UQ)
            keys_out_dve(2)
            keys_out_dve(3)
            keys_out_dve(4)
            rotate_rope_queries(0)
            rotate_rope_queries(1)
            for t in range(TS):
                if t + 2 < NT:
                    rotate_queries(t + 2)
                queries_out_dve(t)
                if t + 2 < NT:
                    rotate_rope_queries(t + 2)
            for cc in range(2):
                dve.wait_ge(uk_hi.sem, uk_hi.at(l, cc + 1))
                vec.tensor_tensor(ukl[:, :, cc * P:(cc + 1) * P], ps[:, 4 + cc, :].rearrange("p (h n) -> p h n", h=BH),
                                  ukh[:, :, cc * P:(cc + 1) * P], ALU.subtract).then_inc(uk_lo.sem, 1)

            link(vec.tensor_scalar(nsink[:, 0:9], gv[:, G_SINK:G_SINK + 9], -1.0, None, ALU.mult))

            def w_max(n):
                kv = n % 2
                dve.wait_ge(w_s.sem, w_s.at(l, n + 1))
                s3 = ps[:, 2 * (n % 2):2 * (n % 2) + 2, :].rearrange("p a (g n) -> p a g n", g=2)
                link(vec.tensor_reduce(mx[:, 0:4].rearrange("p (a g) -> p a g", a=2), s3, AX.X, ALU.max))
                link(vec.scalar_tensor_tensor(out=four_of(nm, n), in0=mx[:, 0:4], scalar=-A_SCALE, in1=nsink[:, 4 * kv:4 * kv + 4],
                                              op0=ALU.mult, op1=ALU.min))
                vec.tensor_tensor(four_of(ed, n), four_of(nm, n), nsink[:, 4 * kv:4 * kv + 4], ALU.subtract).then_inc(w_nm.sem, 1)

            def w_norm(n):
                dve.wait_ge(w_e.sem, w_e.at(l, n + 1))
                link(vec.tensor_tensor(four_of(rsum, n), four_of(rsum, n), four_of(es, n), ALU.add))
                vec.reciprocal(four_of(rinv, n), four_of(rsum, n)).then_inc(w_rinv.sem, 1)

            def q_nope_lo(h):
                dve.wait_ge(qn_hi.sem, qn_hi.at(l, h + 1))
                bank = 6 if h == 0 else 4
                vec.tensor_tensor(halves(qnl[:, :]), ps[:, bank:bank + 2, 0:HALF], halves(qnh[:, :]), ALU.subtract).then_inc(qn_lo.sem, 1)

            w_max(0)
            w_max(1)
            w_norm(0)
            q_nope_lo(0)
            w_max(2)
            for n in range(8):
                if n + 1 < 8:
                    w_norm(n + 1)
                if n >= 2:
                    dve.wait_ge(w_t.sem, w_t.at(l, turned_by(n)))
                    dve.wait_ge(w_pv.sem, w_pv.at(l, n))
                    vec.tensor_copy(pt[:, 1, :], ps[:, 5, :]).then_inc(w_tdve.sem, 1)
                if n + 3 < 8:
                    w_max(n + 3)
            vec.memset(pws[:, :, 144:256], 0.0).then_inc(v_zero.sem, 1)
            dve.wait_ge(v_kt.sem, v_kt.at(l, 2))
            vec.tensor_copy(kTc[:, 4:8, 0:P], ps[:, 1, :].rearrange("p (b n) -> p b n", b=4))
            vec.tensor_copy(kTc[:, :, P:144], kTs[:, :].rearrange("p (b n) -> p b n", b=DECB)).then_inc(v_knew.sem, 1)

            def q_latent_lo(h):
                rest = PROMPT - HALF
                for c in range(2):
                    dve.wait_ge(ql_hi.sem, ql_hi.at(l, 2 * h + c + 1))
                    bank = 4 + 2 * c
                    vec.tensor_tensor(qll[:, h % 2, c, 0:HALF], ps[:, bank, 0:HALF], qlh[:, h % 2, c, 0:HALF], ALU.subtract)
                    vec.tensor_tensor(qll[:, h % 2, c, HALF:PROMPT], ps[:, bank + 1, 0:rest], qlh[:, h % 2, c, HALF:PROMPT], ALU.subtract)\
                       .then_inc(ql_lo.sem, 1)

            def p_max(h):
                for i in range(TS):
                    dve.wait_ge(p_s.sem, p_s.at(l, 4 * h + i + 1))
                    link(vec.tensor_reduce(mx[:, i:i + 1], ps[:, i, 0:(i + 1) * P], AX.X, ALU.max))
                    vec.tensor_scalar(nm[0][:, i:i + 1], mx[:, i:i + 1], -B_SCALE, None, ALU.mult).then_inc(p_nm.sem, 1)

            def p_norm(h):
                for i in range(TS):
                    dve.wait_ge(p_e.sem, p_e.at(l, 4 * h + i + 1))
                    link(vec.reciprocal(rinv[0][:, i:i + 1], rsum[0][:, i:i + 1]))
                    q = pm[:, POFF[i]:POFF[i] + (i + 1) * P]
                    vec.tensor_scalar(q, q, rinv[0][:, i:i + 1], None, ALU.mult).then_inc(p_p.sem, 1)

            q_latent_lo(0)
            dve.wait_ge(v_s.sem, v_s.at(l, 1))
            link(vec.tensor_reduce(mx[:, 0:8].rearrange("p (a b) -> p a b", a=4), ps[:, 0:4, 0:288].rearrange("p a (b n) -> p a b n", b=2), AX.X, ALU.max))
            vec.tensor_scalar(nm[0][:, 0:8], mx[:, 0:8], -A_SCALE, nsink[:, 8:9], ALU.mult, ALU.min).then_inc(v_nm.sem, 1)
            dve.wait_ge(v_e.sem, v_e.at(l, 1))
            link(vec.tensor_tensor(rsum[0][:, 0:8], rsum[0][:, 0:8], es[0][:, 0:8], ALU.add))
            link(vec.reciprocal(rinv[0][:, 0:8], rsum[0][:, 0:8]))
            vec.tensor_tensor(pws[:, :, 0:144], pws[:, :, 0:144], rinv[0][:, 0:8].unsqueeze(2).broadcast_to([P, DECB, 144]), ALU.mult).then_inc(v_p.sem, 1)
            q_nope_lo(1)
            for j in (1, 3):
                dve.wait_ge(v_t.sem, v_t.at(l, j + 1))
                vec.tensor_copy(ptw[:, 2 * j:2 * j + 2, :, :], ps[:, 5, :].rearrange("p (b k n) -> p b k n", b=2, k=2)).then_inc(v_tdve.sem, 1)
            p_max(0)
            p_norm(0)

            def keys_copy(b):
                mine = slice(b * DECS, (b + 1) * DECS)
                keys, bank = (cTo, 5) if b % 2 else (cT, 3)
                if b >= 2:
                    dve.wait_ge(c_s.sem, c_s.at(l, b - 1))
                vec.tensor_copy(keys[:, 0:2, PAST:272], ckTs[:, :, mine])
                vec.tensor_copy(keys[:, 2, PAST:272], krTs[:, mine])
                dve.wait_ge(c_t.sem, c_t.at(l, b + 1))
                vec.tensor_copy(keys[:, 2, 0:PAST], ps[:, bank, 0:PAST]).then_inc(c_dve.sem, 1)

            for h in range(BH):
                if h + 1 < BH:
                    q_latent_lo(h + 1)
                for j in (1, 3):
                    dve.wait_ge(p_t.sem, p_t.at(l, 4 * h + j + 1))
                    vec.tensor_copy(ptm[:, TOFF[j]:TOFF[j] + (4 - j) * P], ps[:, 5, 0:(4 - j) * P]).then_inc(p_tdve.sem, 1)
                if h + 1 < BH:
                    p_max(h + 1)
                else:
                    keys_copy(0)
                dve.wait_ge(p_pv.sem, p_pv.at(l, 2 * h + 2))
                vec.tensor_copy(olat[:, 1, :], ps[:, 7, :]).then_inc(p_latd.sem, 1)
                if h + 2 < BH:
                    q_nope_lo(h + 2)
                if h + 1 < BH:
                    p_norm(h + 1)
                else:
                    keys_copy(1)
            vec.memset(psm[:, :, 272:384], 0.0).then_inc(c_zero.sem, 1)
            weight_lo(l, U_OUT)
            weight_lo(l, U_OUT + 1)

            def mixed_lo(c):
                dve.wait_ge(m_hi.sem, m_hi.at(l, c + 1))
                low(ml[:, c, :], oT[:, c, :], gv[:, G_MIX + c:G_MIX + c + 1], mh[:, c, :]).then_inc(m_lo.sem, 1)

            for b in range(10):
                if 2 <= b + 1 < DECB:
                    keys_copy(b + 1)
                if b % 2 and b < DECB:
                    p = b // 2
                    dve.wait_ge(c_s.sem, c_s.at(l, b + 1))
                    link(vec.tensor_reduce(mx[:, 0:1], ps[:, p % 2, 0:272], AX.X, ALU.max))
                    vec.tensor_scalar(nm[1][:, p:p + 1], mx[:, 0:1], -B_SCALE, None, ALU.mult).then_inc(c_nm.sem, 1)
                    dve.wait_ge(c_e.sem, c_e.at(l, p + 1))
                    link(vec.reciprocal(rinv[1][:, p:p + 1], rsum[1][:, p:p + 1]))
                    vec.tensor_scalar(psm[:, p % 2, 0:272], psm[:, p % 2, 0:272], rinv[1][:, p:p + 1], None, ALU.mult).then_inc(c_p.sem, 1)
                if b % 2 and b >= 3:
                    dve.wait_ge(c_pv.sem, c_pv.at(l, b - 1))
                    vec.tensor_copy(olats[:, :], ps[:, 7, 0:KL]).then_inc(c_lat.sem, 1)
                if b % 2 and b < DECB:
                    mixed_lo(b // 2)

            def diagonal(k, n):
                dve.wait_ge(stat_sd.sem, stat_sd.at(l, k))
                g = slice(NT * n, NT * n + NT)
                link(vec.reciprocal(rs[:, g], sd[:, g]))
                vec.tensor_tensor(diag[:, g, :], ident.unsqueeze(1).broadcast_to([P, NT, P]), rs[:, g].unsqueeze(2).broadcast_to([P, NT, P]),
                                  ALU.mult).then_inc(diag_new.sem, 1)

            diagonal(3, 0)
            for c in range(4, NC_):
                mixed_lo(c)
            diagonal(4, 1)
            dve.wait_ge(bcast.sem, bcast.at(l, 2))
            vec.tensor_copy(rB[:, :], ps[:, 6:8, :].rearrange("p a n -> p (a n)")[:, 0:T]).then_inc(dve_r.sem, 1)
            dve.wait_ge(r_new.sem, r_new.at(l, 1))
            dve.wait_ge(dve_r.sem, dve_r.at(l, 1))
            for d in range(NC_):
                b0 = 2 * (d % 2)
                dve.wait_ge(unit_used.sem, unit_used.at(l, U_OUT + d + 1))
                vec.tensor_tensor(halves(xt[:, 0, :]), ps[:, b0:b0 + 2, 0:HALF], halves(rA[:, :]), ALU.mult)
                link(vec.tensor_tensor(halves(xt[:, 1, :]), ps[:, b0 + 4:b0 + 6, 0:HALF], halves(rB[:, :]), ALU.mult))
                link(vec.tensor_tensor(xt[:, 0, :], xt[:, 0, :], xt[:, 1, :], ALU.add))
                vec.tensor_tensor(xT[:, d, :], xT[:, d, :], xt[:, 0, :], ALU.add).then_inc(x_new.sem, 1)
                weight_lo(l, U_OUT + d + 2)
                dve.wait_ge(n_hi.sem, n_hi.at(l, d + 1))
                low(nl[:, d, :], xT[:, d, :], gv[:, G_FFN + d:G_FFN + d + 1], nh[:, d, :]).then_inc(n_lo.sem, 1)
            for blk in range(NBLK):
                u0 = U_FFN + blk * BLK_U
                for i in range(FT):
                    n = blk * FT + i
                    base = 4 * (i % 2)
                    weight_lo(l, u0 + 2 * i + 2)
                    if n == 0:
                        diagonal(5, 0)
                        dve.wait_ge(r_new.sem, r_new.at(l, 2))
                    dve.wait_ge(unit_used.sem, unit_used.at(l, u0 + 2 * i + 1))
                    vec.tensor_tensor(halves(tg[:, i % 2, :]), ps[:, base:base + 2, 0:HALF], halves(rA[:, :]), ALU.mult).then_inc(g_scaled.sem, 1)
                    weight_lo(l, u0 + 2 * i + 3)
                    dve.wait_ge(unit_used.sem, unit_used.at(l, u0 + 2 * i + 2))
                    vec.tensor_tensor(halves(tu[:, i % 2, :]), ps[:, base + 2:base + 4, 0:HALF], halves(rA[:, :]), ALU.mult).then_inc(u_scaled.sem, 1)
                    dve.wait_ge(u_scaled.sem, u_scaled.at(l, n + 1))
                    dve.wait_ge(silu_new.sem, silu_new.at(l, n + 1))
                    vec.tensor_tensor(tu[:, i % 2, :], tu[:, i % 2, :], tg[:, i % 2, :], ALU.mult).then_inc(h_new.sem, 1)
                    dve.wait_ge(h_hi.sem, h_hi.at(l, n + 1))
                    vec.tensor_tensor(hl[:, i, :], tu[:, i % 2, :], hh[:, i, :], ALU.subtract).then_inc(h_lo.sem, 1)
                for d in range(NC_):
                    u = u0 + 2 * FT + d
                    if u + 2 < UNITS:
                        weight_lo(l, u + 2)
                    b0 = 2 * DOWN_PAIR[d]
                    dve.wait_ge(unit_used.sem, unit_used.at(l, u + 1))
                    vec.tensor_tensor(halves(xT[:, d, :]), ps[:, b0:b0 + 2, 0:HALF], halves(xT[:, d, :]), ALU.add).then_inc(x_new.sem, 1)
                    if blk == NBLK - 1:
                        dve.wait_ge(n_hi.sem, n_hi.at(l, 8 + d + 1))
                        low(nl[:, d, :], xT[:, d, :], gv[:, G_NEXT + d:G_NEXT + d + 1], nh[:, d, :]).then_inc(n_lo.sem, 1)
            assert steps[0] == dve_step.per, steps[0]
        dve.wait_ge(stat_sd.sem, stat_sd.at(DEPTH, 1))
        vec.reciprocal(rs[:, 0:NT], sd[:, 0:NT]).then_inc(stat_r.sem, 1)
        dve.wait_ge(stat_r.sem, stat_r.at(DEPTH, 1))
        for t in range(NT):
            dve.wait_ge(y_turned.sem, t + 1)
            vec.tensor_scalar(yout[:, t, 512:D], ps[:, 2 * (t % 3) + 1, :], rs[:, t:t + 1], None, ALU.mult).then_inc(y_dve.sem, 1)

    @block.gpsimd
    def _(pool):
        add = nc.gpsimd.tensor_tensor

        def sum_squares(l, into, squares_before, adds_before_, chunks):
            for c in range(1, chunks):
                pool.wait_ge(sq_new.sem, sq_new.at(l, squares_before + c + 1))
                if c >= 2:
                    pool.wait_ge(ssq_new.sem, ssq_new.at(l, adds_before_ + c - 1))
                first = sq[:, 0, :] if c == 1 else into[:, :]
                add(into[:, :], first, sq[:, c % 2, :], ALU.add).then_inc(ssq_new.sem, 1)

        for c in range(NC_):
            pool.wait_ge(x_new.sem, c + 1)
            add(sq[:, c % 2, :] if c else ssq[:, :], xT[:, c, :], xT[:, c, :], ALU.mult).then_inc(sq_new.sem, 1)
            pool.wait_ge(sq_new.sem, c + 1)
            if c >= 1:
                if c >= 2:
                    pool.wait_ge(ssq_new.sem, c - 1)
                add(ssq[:, :], ssq[:, :], sq[:, c % 2, :], ALU.add).then_inc(ssq_new.sem, 1)
        for l in layers(pool):
            pool.wait_ge(k_hi.sem, k_hi.at(l, 1))
            k = hm[:, 0:TS, C_K:C_V].rearrange("p t (h d) -> p t h d", d=64)
            for x in range(2):
                add(k2[:, :, 2 + x:8:4, :], k, k2[:, :, x:8:4, :], ALU.subtract)
            for x in range(2):
                ins = add(k2[:, :, 10 + x, :], hm[:, 0:TS, C_KR:IN_W], k2[:, :, 8 + x, :], ALU.subtract)
            ins.then_inc(k_lo.sem, 1)

            def cos_queries(t):
                pool.wait_ge(hm_new.sem, hm_new.at(l, 10 + t + 1))
                if t >= 2:
                    pool.wait_ge(q_roped.sem, q_roped.at(l, t - 1))
                c3 = cos[t].unsqueeze(1).broadcast_to([P, AH, 64])
                q, a3 = (x.rearrange("p (h d) -> p h d", d=64) for x in (hm[:, t, 0:C_K], qcos[:, t % 2, :]))
                add(a3, q, c3, ALU.mult).then_inc(q_cos.sem, 1)

            def queries_lo(t):
                pool.wait_ge(q_hi.sem, q_hi.at(l, t + 1))
                q = hm[:, t, 0:C_K].rearrange("p (h d) -> p h d", d=64)
                add(q2[:, t % 2, :, 64:128], q, q2[:, t % 2, :, 0:64], ALU.subtract).then_inc(q_lo.sem, 1)

            def rope_q_lo(t):
                pool.wait_ge(uqr_hi.sem, uqr_hi.at(l, t + 1))
                q = qra[:, t % 2, :].rearrange("p (h d) -> p h d", d=64)
                add(q2r[:, t % 2, :, 64:128], q, q2r[:, t % 2, :, 0:64], ALU.subtract).then_inc(uqr_lo.sem, 1)

            cos_queries(0)
            cos_queries(1)
            queries_lo(0)
            queries_lo(1)
            cos_queries(2)
            rope_q_lo(0)
            for t in range(1, NT):
                if t + 1 < TS:
                    queries_lo(t + 1)
                if t + 2 < NT:
                    cos_queries(t + 2)
                rope_q_lo(t)
            for n in range(8):
                pool.wait_ge(w_rinv.sem, w_rinv.at(l, n + 1))
                r = four_of(rinv, n).unsqueeze(2).broadcast_to([P, 4, 256])
                add(pwb[n % 4], pwb[n % 4], r, ALU.mult).then_inc(w_p.sem, 1)
            for h in range(1, BH):
                pool.wait_ge(sq_new.sem, sq_new.at(l, h + 1))
                if h >= 2:
                    pool.wait_ge(ssq_new.sem, ssq_new.at(l, h - 1))
                first = sq[:, 0, 0:PROMPT] if h == 1 else ssqB[:, 0:PROMPT]
                add(ssqB[:, 0:PROMPT], first, sq[:, h % 2, 0:PROMPT], ALU.add).then_inc(ssq_new.sem, 1)
            sum_squares(l, ssq, 4, 3, 4)
            pool.wait_ge(sq_new.sem, sq_new.at(l, 9))
            for h in range(1, BH):
                if h >= 2:
                    pool.wait_ge(ssq_new.sem, ssq_new.at(l, 5 + h))
                first = sq[:, 0, 0:P] if h == 1 else ssqB[:, PROMPT:T]
                add(ssqB[:, PROMPT:T], first, sq[:, 0, h * P:(h + 1) * P], ALU.add).then_inc(ssq_new.sem, 1)
            sum_squares(l, ssq, 9, 9, NC_)
            sum_squares(l, ssq, 17, 16, NC_)


def constants():
    import numpy as np

    k = np.zeros((P, K_W + M_W), np.float32)
    k[:, K_ID:K_ID + P] = np.eye(P, dtype=np.float32)
    row, key = np.arange(P)[:, None], np.arange(256)[None, :]
    masks = k[:, K_W:]
    masks[:, M_OWN + P:M_OWN + P + 256] = np.where(key // 64 <= row // 64, 0, HIDDEN)
    masks[:, M_BAND:M_BAND + 256] = np.where((key // 64 >= row // 64) & (key // 64 <= row // 64 + 2), 0, HIDDEN)
    masks[:, M_ID:M_ID + P] = np.eye(P, dtype=np.float32)
    half = ROPE // 2
    inv = np.power(np.float32(10000.0), -np.arange(half, dtype=np.float32) / np.float32(half)).astype(np.float32)
    pos = np.concatenate([np.arange(PROMPT), np.tile(PAST + np.arange(DECS), DECB)]).astype(np.float32)
    ang = pos[:, None] * inv[None, :]
    c, s = np.cos(ang).astype(np.float32), np.sin(ang).astype(np.float32)
    table = np.concatenate([c, c, -s, s], axis=1).reshape(NT, P, 128)
    k[:, K_ROPE:K_ROPE + NT * 128] = table.transpose(1, 0, 2).reshape(P, NT * 128)
    k[:, K_ONE] = 1.0
    k[:, K_EPS] = EPS
    k[:, K_ONES:K_ONES + P] = 1.0
    return k


_INS = ["x_prompt", "x_sample", "cache_win_k", "cache_win_v", "cache_mla_ckv", "cache_mla_krope", "w_in", "w_uq", "w_uk",
        "w_uv", "w_out", "w_gate", "w_up", "w_down"]
_OUTS = {"out_y": (1, PROMPT, D), "out_ys": (DECB, DECS, D),
         "out_wk": (DEPTH, 1, WIN, 2, HD), "out_wv": (DEPTH, 1, WIN, 2, HD), "out_ckv": (DEPTH, 1, PROMPT, KL), "out_kr": (DEPTH, 1, PROMPT, ROPE),
         "out_wks": (DEPTH, DECB, WIN, 2, HD), "out_wvs": (DEPTH, DECB, WIN, 2, HD), "out_ckvs": (DEPTH, DECB, DECS, KL), "out_krs": (DEPTH, DECB, DECS, ROPE)}


def kernel(**inputs):
    import numpy as np
    from concourse import bacc
    from concourse.bass_utils import run_bass_kernel_spmd

    arrays = {n: np.ascontiguousarray(inputs[n]) for n in _INS}
    g = {n: np.asarray(inputs[n]) for n in ("attn_norm", "ffn_norm", "gn_a", "gn_b", "q_norm", "kv_norm", "sinks", "final_norm")}
    packed = np.empty((DEPTH, P, G_W), np.float32)
    for l in range(DEPTH):
        following = g["attn_norm"][l + 1] if l + 1 < DEPTH else g["final_norm"]
        packed[l, :, G_NEXT:G_NEXT + 8] = following.reshape(8, P).T
        packed[l, :, G_FFN:G_FFN + 8] = g["ffn_norm"][l].reshape(8, P).T
        packed[l, :, G_MIX:G_MIX + 4] = g["gn_a"][l].reshape(2, 4, 64).transpose(0, 2, 1).reshape(P, 4)
        packed[l, :, G_MIX + 4:G_MIX + 8] = g["gn_b"][l].reshape(4, P).T
        packed[l, :, G_Q:G_Q + 3] = g["q_norm"][l].reshape(3, P).T
        packed[l, :, G_SINK:G_SINK + 8] = g["sinks"][l][None, :]
        packed[l, :, G_SINKS] = np.repeat(g["sinks"][l], DECS)
        packed[l, :, G_KV:G_W] = g["kv_norm"][l][None, :]
    arrays["vectors"] = packed
    arrays["consts"] = constants()
    arrays["consts"][:, K_GAIN:K_GAIN + 8] = g["attn_norm"][0].reshape(8, P).T
    nc = bacc.Bacc("TRN2", target_bir_lowering=False, num_devices=1)
    a = {n: nc.dram_tensor(n, v.shape, F32, kind="ExternalInput").ap() for n, v in arrays.items()}
    a.update({n: nc.dram_tensor(n, s, F32, kind="ExternalOutput").ap() for n, s in _OUTS.items()})
    hybrid_encoder_step(nc, a)
    r = run_bass_kernel_spmd(nc, [arrays], core_ids=[0]).results[0]
    return tuple(r[n] for n in _OUTS)
```

```python
from contextlib import ExitStack

import concourse.bass as bass
from concourse import mybir

F32 = mybir.dt.float32
F32R = mybir.dt.float32r
ALU = mybir.AluOpType
ACT = mybir.ActivationFunctionType
AX = mybir.AxisListType

P = 128
D = 1024
NC_ = D // P
PROMPT, DECB, DECS = 512, 8, 16
T = PROMPT + DECB * DECS
NT = T // P
TS = NT - 1
HALF = T // 2
DEPTH = 2
PAST, WIN = 256, 128
EPS = 1e-6
AH, HD = 8, 64
BH, NOPE, ROPE, VD = 4, 128, 64, 128
QL, KL = 384, 256
A_SCALE = HD ** -0.5
B_SCALE = (NOPE + ROPE) ** -0.5
C_K, C_V, C_Q, C_KV, C_KR, IN_W = 512, 640, 768, 1152, 1408, 1472
FF = 2816
NBLK = 2
FT = FF // P // NBLK
GROUPS = [(960, IN_W - 960), (512, 448), (0, 512)]
WIN_U = 12
U_UQ = WIN_U
U_OUT = U_UQ + 1
U_FFN = U_OUT + NC_
BLK_U = 2 * FT + NC_
UNITS = U_FFN + NBLK * BLK_U
SLOT = FT * P
G_NEXT, G_FFN, G_MIX, G_SINK, G_SINKS, G_KV = 0, 8, 16, 24, 32, 33
G_Q = G_KV + KL
G_W = G_Q + QL
K_ID, K_ROPE, K_GAIN = 0, 128, 128 + NT * 128
K_ONE, K_EPS = K_GAIN + NC_, K_GAIN + NC_ + 1
K_ONES = K_EPS + 1
K_W = -(-(K_ONES + P) // 8) * 8
M_OWN, M_BAND, M_ID, M_W = 0, 384, 640, 768
HIDDEN = -1e30
POFF = [0, 128, 384, 768, 1280]
TOFF = [0, 512, 896, 1152]
RAW_BEFORE_FFN = [7 + 1 + 12, 6 + 12]
DOWN_PAIR = [2, 3, 0, 1, 0, 1, 2, 3]


class Signal:

    def __init__(self, ctx, nc, name, per, pre=0):
        self.sem, self.per, self.pre = ctx.enter_context(nc.semaphore(name)), per, pre

    def at(self, layer, k):
        return layer * self.per + (k + self.pre)


def hybrid_encoder_step(nc, a):
    ctx = ExitStack()

    def place(offset, specs):
        with ExitStack() as r:
            if offset:
                r.enter_context(nc.sbuf_tensor(f"skip_{specs[0][0]}", [P, offset // 4], F32))
            return [r.enter_context(nc.sbuf_tensor(n, s, d)) for n, s, d in specs]

    W0, H0, S0, K0 = 61440, 95232, 151552, 164352
    xT, nh, nl = place(0, [("xT", [P, NC_, T], F32), ("nh", [P, NC_, T], F32R), ("nl", [P, NC_, T], F32R)])
    wraw, whi, wlo = place(W0, [("wraw", [P, 2 * SLOT], F32), ("whi", [P, 2 * SLOT], F32R), ("wlo", [P, 2 * SLOT], F32R)])
    hh, hl = place(H0, [("hh", [P, FT, T], F32R), ("hl", [P, FT, T], F32R)])
    ssq, rA, sq, ssqB = place(S0, [("ssq", [P, T], F32), ("rA", [P, T], F32), ("sq", [P, 2, T], F32), ("ssqB", [P, T], F32)])
    _, rB = place(S0, [("skip_rB", [P, 4 * T], F32), ("rB", [P, T], F32)])
    kc, kmask, gv, small = place(K0, [("kc", [P, K_W], F32), ("kmask", [P, M_W], F32R), ("gv", [P, 40], F32), ("small", [P, 144], F32)])
    R0 = K0 + 4 * (K_W + M_W + 40 + 144)
    mh, ml = place(R0, [("mh", [P, NC_, T], F32R), ("ml", [P, NC_, T], F32R)])
    fg, = place(R0, [("fg", [P, D], F32)])
    tg, tu = place(R0, [("tg", [P, 2, T], F32), ("tu", [P, 2, T], F32)])
    _, xt, _, diag = place(H0, [("skip_xt", [P, 1280], F32), ("xt", [P, 2, T], F32), ("skip_diag", [P, 2560], F32), ("diag", [P, 10, P], F32)])
    xin, mask_in = place(H0, [("xin", [P, NT, D], F32), ("mask_in", [P, M_W], F32)])
    yout, = place(H0, [("yout", [P, NT, D], F32)])
    ckh, ckl, krT, qrT, cqh, cql, qnh, qnl = place(20480, [
        ("ckh", [P, 2, PROMPT], F32R), ("ckl", [P, 2, PROMPT], F32R), ("krT", [P, 2, PROMPT], F32R),
        ("qrT", [P, BH, PROMPT], F32R), ("cqh", [P, 3, T], F32R), ("cql", [P, 3, T], F32R),
        ("qnh", [P, T], F32R), ("qnl", [P, T], F32R)])
    hm, qaT, kaT, qTs = place(H0, [("hm", [P, NT, IN_W], F32), ("qaT", [P, AH, PROMPT], F32R),
                                   ("kaT", [P, 4, PROMPT], F32R), ("qTs", [P, DECB, 4, DECS], F32)])
    pwx, = place(H0 + 10240, [("pwx", [P, 2, 4, 256], F32)])
    oT, cr = place(H0, [("oT", [P, NC_, T], F32), ("cr", [P, 2, 1024], F32)])
    pws, = place(H0 + 20480, [("pws", [P, DECB, 256], F32)])
    kTc, ptw = place(S0, [("kTc", [P, DECB, 144], F32), ("ptw", [P, DECB, 2, P], F32)])
    qlh, qll, pm = place(H0 + 29440, [("qlh", [P, 2, 2, PROMPT], F32R), ("qll", [P, 2, 2, PROMPT], F32R),
                                      ("pm", [P, 1280], F32)])
    uv, = place(H0 + 50944, [("uv", [P, 2, 512], F32)])
    cx, = place(20480, [("cx", [P, 6, 1024], F32)])
    cTo, = place(56320, [("cTo", [P, 3, 272], F32)])
    olats, olTs, psm, pts = place(H0 + 29440, [("olats", [P, KL], F32), ("olTs", [P, 2, BH, P], F32),
                                               ("psm", [P, 2, 384], F32), ("pts", [P, 3, P], F32)])
    v, ckv, vn, cT, kTs, qrTs, ckTs, krTs, ptm, ukh, ukl, qlTs, kvg = place(R0, [
        ("v", [P, NT, 128], F32), ("ckv", [P, NT, KL], F32), ("vn", [16, DECB, 128], F32), ("cT", [P, 3, 272], F32),
        ("kTs", [P, P], F32), ("qrTs", [P, DECB, BH, DECS], F32), ("ckTs", [P, 2, P], F32), ("krTs", [P, P], F32),
        ("ptm", [P, 2048], F32), ("ukh", [P, BH, KL], F32R), ("ukl", [P, BH, KL], F32R),
        ("qlTs", [P, 2, DECB, BH, DECS], F32), ("kvg", [P, KL], F32)])
    _, krd = place(R0, [("skip_krd", [P, 2944], F32), ("krd", [P, 2, 64], F32)])
    _, wk, wv = place(R0, [("skip_wk", [P, 4784], F32), ("wk", [P, DECB, 128], F32), ("wv", [P, DECB, 128], F32)])
    _, qcos, qsin = place(R0, [("skip_qcos", [P, 4784], F32), ("qcos", [P, 2, 512], F32), ("qsin", [P, 2, 512], F32)])
    _, q2r = place(R0, [("skip_q2r", [P, 8880], F32), ("q2r", [P, 2, BH, P], F32R)])
    kcos, ksin, junk = place(H0 + 29440, [("kcos", [P, NT, 128], F32), ("ksin", [P, NT, 128], F32), ("junk", [P, NT, QL + KL], F32)])
    _, qg = place(H0 + 29440, [("skip_qg", [P, 4480], F32), ("qg", [P, QL], F32)])
    k2, = place(S0, [("k2", [P, TS, 12, 64], F32R)])
    q2, qra, qrb = place(S0, [("q2", [P, 2, AH, 128], F32R), ("qra", [P, 2, 256], F32), ("qrb", [P, 256], F32)])
    q2s, = place(S0, [("q2s", [P, 4, 2, 64], F32)])
    _, ptx = place(R0, [("skip_ptx", [P, 8880], F32), ("ptx", [P, 2, 512], F32)])
    pw, pt = place(S0, [("pw", [P, 2, 4, 256], F32), ("pt", [P, 2, 512], F32)])
    olat, = place(S0, [("olat", [P, 2, PROMPT], F32)])
    last_end = R0 + 4 * (8880 + 2 * 512 + 4464)
    assert last_end <= nc.sbuf_usable_end, (last_end, nc.sbuf_usable_end)
    ps = ctx.enter_context(nc.psum_tensor("ps", [P, 8, 512], F32))

    ident = kc[:, K_ID:K_ID + P]
    mask_first, mask_own, mask_band = (kmask[:, x:x + 256] for x in (M_OWN + P, M_OWN, M_BAND))
    ident_r = kmask[:, M_ID:M_ID + P]
    cos = [kc[:, K_ROPE + 128 * t:K_ROPE + 128 * t + 64] for t in range(NT)]
    sin = [kc[:, K_ROPE + 128 * t + 64:K_ROPE + 128 * t + 128] for t in range(NT)]
    onesq = kc[:, K_ONES:K_ONES + P]
    one, eps = kc[:, K_ONE:K_ONE + 1], kc[:, K_EPS:K_EPS + 1]
    ms, sd, rs, mx, nsink, rl = (small[:, x:x + w] for x, w in ((0, 10), (10, 10), (20, 10), (30, 8), (38, 9), (128, 10)))
    pwb = [pw[:, 0], pw[:, 1], pwx[:, 0], pwx[:, 1]]
    ptb = [pt, ptx]

    def four_of(buffers, n):
        return buffers[n // 2 % 2][:, 4 * (n % 2):4 * (n % 2) + 4]

    nm, ed, rsum, es, rinv = ([small[:, x + 8 * b:x + 8 * b + 8] for b in range(2)] for x in (48, 64, 80, 96, 112))

    def cache(b):
        return cr[:, b] if b < 2 else cx[:, b - 2]

    def sig(name, per, pre=0):
        return Signal(ctx, nc, name, per, pre)

    consts_in, x_in = sig("consts_in", 0), sig("x_in", 0)
    vectors_in = sig("vectors_in", 48)
    raw_in = [sig("raw_in0", 16 * 50), sig("raw_in1", 16 * 48)]
    win_in, vnew_in, uv_in, cache_in = sig("win_in", 32), sig("vnew_in", 16), sig("uv_in", 16), [sig(f"cache_in{b}", 16 * 4) for b in range(DECB)]
    out_hm, out_ckv, out_sample, out_copy, out_y = sig("out_hm", 16 * 5), sig("out_ckv", 16), sig("out_sample", 32), sig("out_copy", 32), sig("out_y", 0)
    uq_hi_first, uq_lo_first = sig("uq_hi_first", 1), sig("uq_lo_first", 1)
    unit_hi, unit_lo, unit_used = sig("unit_hi", UNITS), sig("unit_lo", UNITS, 2), sig("unit_used", UNITS, 2)
    x_new, n_hi, n_lo = sig("x_new", 24, 8), sig("n_hi", 16, 7), sig("n_lo", 16, 7)
    x_turned, x_squared = sig("x_turned", 0), sig("x_squared", 0)
    sq_new, ssq_new = sig("sq_new", 25), sig("ssq_new", 23, 6)
    m_hi, m_lo = sig("m_hi", 8), sig("m_lo", 8)
    stat_sum, stat_sd, stat_r, diag_new, bcast, r_new = (sig(n, p) for n, p in (
        ("stat_sum", 4), ("stat_sd", 5), ("stat_r", 1), ("diag_new", 3), ("bcast", 3), ("r_new", 2)))
    in_done, hm_new, k_roped, q_cos, q_roped = (sig(n, p) for n, p in (
        ("in_done", 12), ("hm_new", 15), ("k_roped", 1), ("q_cos", 5), ("q_roped", 5)))
    lat_ms, cq_norm, ckv_norm, v_new = sig("lat_ms", 10), sig("cq_norm", 5), sig("ckv_norm", 5), sig("v_new", 1)
    k_hi, k_lo, q_hi, q_lo = sig("k_hi", 1), sig("k_lo", 1), sig("q_hi", 5), sig("q_lo", 4)
    k_turned, k_act, k_dve, q_turned, q_act, q_dve = (sig(n, p) for n, p in (
        ("k_turned", 14), ("k_act", 13), ("k_dve", 10), ("q_turned", 9), ("q_act", 5), ("q_dve", 4)))
    uk_turned, uk_hi, uk_lo = sig("uk_turned", 2), sig("uk_hi", 2), sig("uk_lo", 2)
    uqr_rope = sig("uqr_rope", 5)
    uqr_done, uqr_hi, uqr_lo, uqr_turned, uqr_new, uqr_new_read = (sig(n, 5) for n in (
        "uqr_done", "uqr_hi", "uqr_lo", "uqr_turned", "uqr_new", "uqr_read"))
    w_s, w_nm, w_e, w_rinv, w_p, w_t, w_tact, w_tdve, w_pv, w_o = (sig(n, p) for n, p in (
        ("w_scores", 8), ("w_negmax", 8), ("w_exp", 8), ("w_rinv", 8), ("w_probs", 8), ("w_turned", 14),
        ("w_turned_act", 8), ("w_turned_dve", 6), ("w_pv", 8), ("w_out", 4)))
    v_kt, v_ktact, v_knew, v_zero, v_s, v_nm, v_e, v_p, v_t, v_tact, v_tdve, v_pv, v_o = (sig(n, p) for n, p in (
        ("v_keys_turned", 2), ("v_keys_act", 1), ("v_keys_new", 1), ("v_zero", 1), ("v_scores", 1), ("v_negmax", 1), ("v_exp", 1),
        ("v_probs", 1), ("v_turned", 4), ("v_turned_act", 2), ("v_turned_dve", 2), ("v_pv", 1), ("v_out", 1)))
    qn_done, qn_hi, qn_lo, ql_done, ql_hi, ql_lo = (sig(n, p) for n, p in (
        ("qn_done", 3), ("qn_hi", 4), ("qn_lo", 4), ("ql_done", 8), ("ql_hi", 8), ("ql_lo", 8)))
    p_s, p_nm, p_e, p_p, p_t, p_tact, p_tdve, p_pv, p_lat, p_latd, p_ob, p_o = (sig(n, p) for n, p in (
        ("p_scores", 16), ("p_negmax", 16), ("p_exp", 16), ("p_probs", 16), ("p_turned", 16), ("p_turned_act", 8),
        ("p_turned_dve", 8), ("p_pv", 8), ("p_lat_act", 4), ("p_lat_dve", 4), ("p_ob", 4), ("p_out", 4)))
    c_zero, c_t, c_act, c_dve, c_s, c_nm, c_e, c_p, c_pt, c_ptact, c_pv, c_lat, c_lt, c_ltact, c_ob, c_o = (sig(n, p) for n, p in (
        ("c_zero", 1), ("c_turned", 8), ("c_keys_act", 8), ("c_keys_dve", 8), ("c_scores", 8), ("c_negmax", 4), ("c_exp", 4), ("c_probs", 4),
        ("c_probs_turned", 4), ("c_probs_act", 4), ("c_pv", 8), ("c_lat", 4), ("c_lat_turned", 4), ("c_lat_new", 4),
        ("c_ob", 1), ("c_out", 1)))
    g_scaled, u_scaled, silu_new, h_new, h_hi, h_lo = (sig(n, NBLK * FT) for n in (
        "gate_scaled", "up_scaled", "silu_new", "h_new", "h_hi", "h_lo"))
    dve_r = sig("dve_r", 1)
    dve_step = sig("dve_step", 96)
    fg_in, y_turned, y_scaled, y_pool, y_dve = (sig(n, 0) for n in ("fg_in", "y_turned", "y_scaled", "y_pool", "y_dve"))

    def slot(s, n=SLOT):
        return slice(s * SLOT, s * SLOT + n)

    def raw_value(s, layer, u):
        base = 7 if s == 0 else 6
        if u == "uk":
            n = base + 1
        elif u < WIN_U:
            n = u // 2 + 1
        elif u == U_UQ:
            n = 7
        elif u < U_FFN:
            n = base + (s == 0) + 3 * ((u - U_OUT) // 2 + 1)
        else:
            n = RAW_BEFORE_FFN[s] + (u - U_FFN) // 2 + 1
        return raw_in[s].at(layer, 16 * n)

    def raw_ffn(s, layer, blk, i):
        return raw_in[s].at(layer, i * 16 + 16 * (RAW_BEFORE_FFN[s] + blk * BLK_U // 2 + 1))

    def unit_slot(u):
        return u % 2 if u < WIN_U else 0 if u == U_UQ else (u - U_OUT) % 2 if u < U_FFN else (u - U_FFN) % 2

    def unit_width(u):
        if u < WIN_U:
            return 1024
        if u == U_UQ:
            return 3 * BH * (NOPE + ROPE)
        return 1024 if u < U_FFN or (u - U_FFN) % BLK_U < 2 * FT else FT * P

    def used_before(u):
        return U_OUT if u in (U_OUT, U_OUT + 1) else WIN_U if u == U_UQ else u - 1

    uq_hi = whi[:, 0:2304].rearrange("p (k n) -> p k n", k=3)
    uq_lo = wlo[:, 0:2304].rearrange("p (k n) -> p k n", k=3)

    def rope_cols(w, k):
        return w[:, k, :].rearrange("p (h n) -> p h n", h=BH)[:, :, NOPE:]

    def layers(eng):
        with eng.Fori(0, DEPTH) as layer:
            yield layer

    def turned_by(n):
        return n + 1 if n < 2 else 2 * n

    def tok(t):
        return slice(t * P, (t + 1) * P)

    def half(j):
        return slice(j * HALF, (j + 1) * HALF)

    def halves(ap):
        return ap.rearrange("p (j n) -> p j n", j=2)

    block = ctx.enter_context(nc.Block())

    @block.sync
    def _(sp):
        sp.dma_start(kc[:, :], a["consts"][:, 0:K_W]).then_inc(consts_in.sem, 16)
        sp.dma_start(gv[:, G_NEXT:G_NEXT + NC_], a["consts"][:, K_GAIN:K_GAIN + NC_]).then_inc(consts_in.sem, 16)
        sp.dma_start(mask_in[:, :], a["consts"][:, K_W:]).then_inc(consts_in.sem, 16)
        for t in range(TS):
            sp.dma_start(xin[:, t, :], a["x_prompt"][0, tok(t), :]).then_inc(x_in.sem, 16)
        sp.dma_start(xin[:, TS, :], a["x_sample"].rearrange("b s d -> (b s) d")).then_inc(x_in.sem, 16)
        w_in = a["w_in"].rearrange("l (k p) n -> l p k n", p=P)
        w_uq = a["w_uq"].rearrange("l (k p) n -> l p k n", p=P)
        w_uk = a["w_uk"].rearrange("l (k p) h n -> l p k (h n)", p=P)
        w_uv = a["w_uv"].rearrange("l (k p) h n -> l p k (h n)", p=P)
        wo_low = a["w_out"].rearrange("l (e j p) n -> l e p j n", p=64, j=4)
        wo_high = a["w_out"].rearrange("l (k p) n -> l p k n", p=P)
        w_gate = a["w_gate"].rearrange("l (k p) (f n) -> l p k f n", p=P, n=P)
        w_up = a["w_up"].rearrange("l (k p) (f n) -> l p k f n", p=P, n=P)
        w_down = a["w_down"].rearrange("l (f p) n -> l p f n", p=P)
        for l in layers(sp):
            def load(u, source):
                s = unit_slot(u)
                if u == U_OUT:
                    sp.wait_ge(uk_turned.sem, uk_turned.at(l, 2))
                else:
                    sp.wait_ge(unit_lo.sem, unit_lo.at(l, used_before(u)))
                if u == 8:
                    sp.dma_start(kvg[:, :], a["vectors"][l][:, G_KV:G_Q]).then_inc(vectors_in.sem, 16)
                    sp.dma_start(qg[:, :], a["vectors"][l][:, G_Q:G_W]).then_inc(vectors_in.sem, 16)
                for part0, first, width, src in source:
                    parts, k, w = src.shape
                    dst = wraw[part0:part0 + parts, s * SLOT + first * width:s * SLOT + (first + k) * width]
                    dst = dst.rearrange("p (k n) -> p k n", k=k)[:, :, 0:w]
                    sp.dma_start(dst, src).then_inc(raw_in[s].sem, 16)

            for u in range(WIN_U):
                c0, w = GROUPS[u // 4]
                kp = u % 4
                load(u, [(0, 0, 512, w_in[l][:, 2 * kp:2 * kp + 2, c0:c0 + w])])
                if u == 1:
                    sp.wait_ge(n_lo.sem, n_lo.at(l, 1))
                    sp.dma_start(gv[:, 0:G_KV], a["vectors"][l][:, 0:G_KV]).then_inc(vectors_in.sem, 16)
            keep = WIN - DECS
            sp.dma_start(a["out_wks"][l][:, 0:keep], a["cache_win_k"][l][:, DECS:]).then_inc(out_copy.sem, 16)
            sp.dma_start(a["out_wvs"][l][:, 0:keep], a["cache_win_v"][l][:, DECS:]).then_inc(out_copy.sem, 16)
            load(U_UQ, [(0, 0, 768, w_uq[l])])
            sp.wait_ge(unit_lo.sem, unit_lo.at(l, U_OUT))
            sp.dma_start(wraw[:, slot(0, 1024)].rearrange("p (k n) -> p k n", k=2), w_uk[l]).then_inc(raw_in[0].sem, 16)
            sp.wait_ge(ckv_norm.sem, ckv_norm.at(l, 5))
            sp.dma_start(a["out_ckvs"][l].rearrange("b s c -> (b s) c"), ckv[:, TS, :]).then_inc(out_sample.sem, 16)
            sp.wait_ge(v_new.sem, v_new.at(l, 1))
            sp.dma_start(a["out_wvs"][l][:, keep:].rearrange("b s h d -> b s (h d)"), v[:, TS, :]).then_inc(out_sample.sem, 16)
            sp.dma_start(a["out_ckv"][l, 0].rearrange("(t p) c -> p t c", p=P), ckv[:, 0:TS, :]).then_inc(out_ckv.sem, 16)
            sp.wait_ge(k_roped.sem, k_roped.at(l, 1))
            sp.dma_start(a["out_wk"][l, 0].rearrange("s h d -> s (h d)"), hm[:, 3, C_K:C_V]).then_inc(out_hm.sem, 16)
            sp.dma_start(a["out_wv"][l, 0].rearrange("s h d -> s (h d)"), hm[:, 3, C_V:C_Q]).then_inc(out_hm.sem, 16)
            sp.dma_start(a["out_kr"][l, 0].rearrange("(t p) c -> p t c", p=P), hm[:, 0:TS, C_KR:IN_W]).then_inc(out_hm.sem, 16)
            sp.dma_start(a["out_wks"][l][:, keep:].rearrange("b s h d -> b s (h d)"), hm[:, TS, C_K:C_V]).then_inc(out_hm.sem, 16)
            sp.dma_start(a["out_krs"][l].rearrange("b s c -> (b s) c"), hm[:, TS, C_KR:IN_W]).then_inc(out_hm.sem, 16)
            sp.wait_ge(out_sample.sem, out_sample.at(l, 32))
            sp.dma_start(vn[:, :, :], a["out_wvs"][l][:, keep:].rearrange("b s h d -> s b (h d)")).then_inc(vnew_in.sem, 16)
            sp.wait_ge(q_roped.sem, q_roped.at(l, NT))
            sp.dma_start(wk[:, :, :], a["cache_win_k"][l].rearrange("b s h d -> s b (h d)")).then_inc(win_in.sem, 16)
            sp.dma_start(wv[:, :, :], a["cache_win_v"][l].rearrange("b s h d -> s b (h d)")).then_inc(win_in.sem, 16)
            load_out = lambda d: load(U_OUT + d, [
                (0, 0, P, wo_low[l, 0][:, :, d * P:(d + 1) * P]),
                (64, 0, P, wo_low[l, 1][:, :, d * P:(d + 1) * P]),
                (0, 4, P, wo_high[l][:, 4:8, d * P:(d + 1) * P])])
            load_out(0)
            load_out(1)
            sp.wait_ge(v_s.sem, v_s.at(l, 1))
            sp.dma_start(uv[:, :, :], w_uv[l]).then_inc(uv_in.sem, 16)
            for b in range(DECB):
                if b == 0:
                    sp.wait_ge(out_hm.sem, out_hm.at(l, 80))
                    sp.wait_ge(v_t.sem, v_t.at(l, 4))
                if b == 2:
                    sp.wait_ge(p_s.sem, p_s.at(l, 16))
                tiles = cache(b)[:, 0:768].rearrange("p (k n) -> p k n", k=2)
                sp.dma_start(tiles[:, :, 0:KL], a["cache_mla_ckv"][l][b].rearrange("(k p) c -> p k c", p=P)).then_inc(cache_in[b].sem, 16)
                for twice in range(2):
                    r = KL + 64 * twice
                    sp.dma_start(tiles[:, :, r:r + 64], a["cache_mla_krope"][l][b].rearrange("(k p) c -> p k c", p=P)).then_inc(cache_in[b].sem, 16)
                sp.dma_start(cache(b)[0:16, 768:1024], a["out_ckvs"][l][b]).then_inc(cache_in[b].sem, 16)
            for d in range(2, NC_):
                load_out(d)
            for blk in range(NBLK):
                u0 = U_FFN + blk * BLK_U
                with sp.Fori(0, FT) as i:
                    for s, w in enumerate((w_gate, w_up)):
                        sp.wait_ge(unit_lo.sem, unit_lo.at(l, i * 2 + (u0 + s - 1)))
                        sp.dma_start(wraw[:, slot(s, NC_ * P)].rearrange("p (k n) -> p k n", k=NC_), w[l][:, :, i + blk * FT, :]).then_inc(raw_in[s].sem, 16)
                for d in range(NC_):
                    load(u0 + 2 * FT + d, [(0, 0, P, w_down[l][:, blk * FT:(blk + 1) * FT, d * P:(d + 1) * P])])
        sp.wait_ge(h_lo.sem, h_lo.at(DEPTH, 0))
        sp.dma_start(fg[:, :], a["final_gain"]).then_inc(fg_in.sem, 16)
        for t in range(NT):
            sp.wait_ge(y_pool.sem, t + 1)
            sp.wait_ge(y_dve.sem, t + 1)
            dst = a["out_y"][0, tok(t), :] if t < TS else a["out_ys"].rearrange("b s d -> (b s) d")
            sp.dma_start(dst, yout[:, t, :]).then_inc(out_y.sem, 16)
        sp.wait_ge(out_y.sem, 16 * NT)
        sp.wait_ge(out_hm.sem, 80 * DEPTH)
        sp.wait_ge(out_ckv.sem, 16 * DEPTH)
        sp.wait_ge(out_sample.sem, 32 * DEPTH)
        sp.wait_ge(out_copy.sem, 32 * DEPTH)

    @block.tensor
    def _(pe):
        mm, turn = nc.tensor.matmul, nc.tensor.transpose

        def unit_parts(u, n):
            s = unit_slot(u)
            return [w[:, slot(s, unit_width(u))].rearrange("p (k n) -> p k n", n=n) for w in (whi, wlo)]

        def by_weights(outs, w, k, cols, xh, xl, first, last):
            for part, (wt, xs) in enumerate(((w[0], (xh, xl)), (w[1], (xh,)))):
                for x in xs:
                    for j in range(2):
                        ins = mm(outs[j], wt[:, k, cols], x[:, half(j)], start=first and part == 0 and x is xh,
                                 stop=last and part == 1)
            return ins

        def sums(source, bank, col):
            for t in range(NT):
                ins = mm(ps[:, bank, col + t:col + t + 1], source[:, tok(t)], one, start=True, stop=True)
            ins.then_inc(stat_sum.sem, 1)

        def spread(n, bank):
            for t in range(NT):
                ins = mm(ps[:, bank + t // 4, (t % 4) * P:(t % 4 + 1) * P], onesq, diag[:, NT * n + t, :], start=True, stop=True)
            ins.then_inc(bcast.sem, 1)

        pe.sem_inc(unit_used.sem, 2)
        pe.wait_ge(consts_in.sem, 48)
        pe.wait_ge(x_in.sem, 16 * NT)
        for c in range(NC_):
            if c >= 4:
                pe.wait_ge(x_new.sem, c - 3)
            for t in range(NT):
                bank = 2 * (c % 4) + t // 4
                ins = turn(ps[:, bank, (t % 4) * P:(t % 4 + 1) * P], xin[:, t, c * P:(c + 1) * P], ident)
            ins.then_inc(x_turned.sem, 1)
        for l in layers(pe):
            pe.wait_ge(x_new.sem, x_new.at(l, -1))
            for u in range(WIN_U):
                g, kp = divmod(u, 4)
                w = GROUPS[g][1]
                wh, wl = unit_parts(u, 512)
                pe.wait_ge(unit_lo.sem, unit_lo.at(l, u + 1))
                for t in range(NT):
                    i = g * NT + t
                    if kp == 0 and i >= 7:
                        pe.wait_ge(hm_new.sem, hm_new.at(l, i - 6))
                    for k in range(2):
                        c = 2 * kp + k
                        if g == 0 and t == 0:
                            pe.wait_ge(n_lo.sem, n_lo.at(l, c - 6))
                        o = ps[:, i % 7, 0:w]
                        mm(o, nh[:, c, tok(t)], wh[:, k, 0:w], start=c == 0, stop=False)
                        mm(o, nh[:, c, tok(t)], wl[:, k, 0:w], start=False, stop=False)
                        ins = mm(o, nl[:, c, tok(t)], wh[:, k, 0:w], start=False, stop=c == NC_ - 1)
                    if t == TS:
                        ins.then_inc(unit_used.sem, 1)
                    elif kp == 3:
                        ins.then_inc(in_done.sem, 1)
                if u == 3:
                    pe.wait_ge(ssq_new.sem, ssq_new.at(l, 1))
                    sums(ssq, 7, 0)
            def batch(bank, pieces, done):
                for j, src in enumerate(pieces):
                    ins = turn(ps[:, bank, j * P:(j + 1) * P], src, ident)
                ins.then_inc(done.sem, 1)

            pe.wait_ge(k_lo.sem, k_lo.at(l, 1))
            pe.wait_ge(ckv_norm.sem, ckv_norm.at(l, NT))
            pe.wait_ge(cq_norm.sem, cq_norm.at(l, NT))
            def rope_q(t):
                if t >= 2:
                    pe.wait_ge(uqr_new_read.sem, uqr_new_read.at(l, t - 1))
                for k in range(3):
                    o = ps[:, 2 if t % 2 else 5, 0:256]
                    mm(o, cqh[:, k, tok(t)], rope_cols(uq_hi, k), start=k == 0, stop=False)
                    mm(o, cqh[:, k, tok(t)], rope_cols(uq_lo, k), start=False, stop=False)
                    ins = mm(o, cql[:, k, tok(t)], rope_cols(uq_hi, k), start=False, stop=k == 2)
                ins.then_inc(uqr_done.sem, 1)

            def rope_q_turn(t):
                pe.wait_ge(uqr_lo.sem, uqr_lo.at(l, t + 1))
                if t >= 2:
                    pe.wait_ge(uqr_new.sem, uqr_new.at(l, t - 1))
                for h in range(BH):
                    ins = turn(ps[:, 1 if t % 2 else 7, h * P:(h + 1) * P], q2r[:, t % 2, h, :].bitcast(F32), ident)
                ins.then_inc(uqr_turned.sem, 1)

            def queries_turn(t):
                banks = (3, 4) if t % 2 else (6, 0)
                if t == 0:
                    pe.wait_ge(hm_new.sem, hm_new.at(l, 15))
                if t >= 2:
                    pe.wait_ge(q_act.sem, q_act.at(l, t - 1))
                    pe.wait_ge(q_dve.sem, q_dve.at(l, t - 1))
                if t < TS:
                    pe.wait_ge(q_lo.sem, q_lo.at(l, t + 1))
                    heads = [q2[:, t % 2, h, :].bitcast(F32) for h in range(AH)]
                    batch(banks[0], heads[0:4], q_turned)
                    batch(banks[1], heads[4:8], q_turned)
                else:
                    pe.wait_ge(q_hi.sem, q_hi.at(l, NT))
                    batch(banks[0], [q2s[:, g, :, :].rearrange("p e d -> p (e d)") for g in range(4)], q_turned)

            def keys_turn(t):
                banks = (3, 4, 5) if t % 2 else (1, 2, 7)
                if t == 1:
                    pe.wait_ge(hm_new.sem, hm_new.at(l, 13))
                if t >= 2:
                    pe.wait_ge(k_act.sem, k_act.at(l, 3 * (t - 1)))
                    pe.wait_ge(k_dve.sem, k_dve.at(l, 2 * (t - 1)))
                latents = [ckv[:, t, c * P:(c + 1) * P] for c in range(2)]
                if t < TS:
                    pairs = [k2[:, t, 2 * x:2 * x + 2, :].rearrange("p a d -> p (a d)").bitcast(F32) for x in range(6)]
                    batch(banks[0], pairs[0:4], k_turned)
                    batch(banks[1], pairs[4:6] + latents, k_turned)
                else:
                    batch(banks[1], [hm[:, TS, C_K:C_V], krd[:, :, :].rearrange("p a d -> p (a d)")] + latents, k_turned)
                batch(banks[2], [hm[:, t, C_Q + k * P:C_Q + (k + 1) * P] for k in range(3)], k_turned)

            for t in range(TS):
                keys_turn(t)
            queries_turn(0)
            keys_turn(TS)
            pe.wait_ge(k_act.sem, k_act.at(l, 12))
            pe.wait_ge(k_dve.sem, k_dve.at(l, 8))
            queries_turn(1)
            pe.wait_ge(uq_lo_first.sem, uq_lo_first.at(l, 1))
            pe.wait_ge(unit_lo.sem, unit_lo.at(l, U_UQ + 1))
            pe.wait_ge(k_act.sem, k_act.at(l, 13))
            pe.wait_ge(k_dve.sem, k_dve.at(l, 10))
            rope_q(0)
            rope_q(1)
            for t in range(2):
                rope_q_turn(t)
                rope_q(t + 2)
                queries_turn(t + 2)
            rope_q_turn(2)
            rope_q(TS)
            rope_q_turn(3)
            queries_turn(TS)
            rope_q_turn(TS)
            pe.wait_ge(q_dve.sem, q_dve.at(l, TS))
            pe.wait_ge(uqr_new_read.sem, uqr_new_read.at(l, NT))
            pe.wait_ge(raw_in[0].sem, raw_value(0, l, "uk"))
            for cc in range(2):
                for h in range(BH):
                    o = cc * 512 + h * P
                    ins = turn(ps[:, 4 + cc, h * P:(h + 1) * P], wraw[:, o:o + P], ident)
                ins.then_inc(uk_turned.sem, 1)
            pe.wait_ge(q_act.sem, q_act.at(l, NT))
            pe.wait_ge(uqr_new.sem, uqr_new.at(l, TS))
            pe.wait_ge(uqr_new_read.sem, uqr_new_read.at(l, NT))
            pe.wait_ge(v_new.sem, v_new.at(l, 1))

            def w_scores(n):
                i, kv = divmod(n, 2)
                k0 = max(i - 1, 0) * P
                if n >= 2:
                    pe.wait_ge(w_e.sem, w_e.at(l, n - 1))
                for g in range(4):
                    o = ps[:, 2 * (n % 2) + g // 2, (g % 2) * 256:(g % 2 + 1) * 256]
                    for x in range(2):
                        mm(o, qaT[:, kv * 4 + g, tok(i)], kaT[:, kv * 2 + x, k0:k0 + 256], start=x == 0, stop=False)
                    ins = mm(o, ident_r, mask_band if i else mask_first, start=False, stop=True)
                ins.then_inc(w_s.sem, 1)

            def w_turn(n):
                pe.wait_ge(w_p.sem, w_p.at(l, n + 1))
                for kt in range(2 if n >= 2 else 1):
                    if kt == 0 and n >= 1:
                        pe.wait_ge(w_tact.sem, w_tact.at(l, n))
                    if kt == 0 and n == 0:
                        pe.wait_ge(uk_lo.sem, uk_lo.at(l, 2))
                        pe.wait_ge(uqr_new.sem, uqr_new.at(l, NT))
                    if kt == 1 and n >= 3:
                        pe.wait_ge(w_tdve.sem, w_tdve.at(l, n - 2))
                    for g in range(4):
                        ins = turn(ps[:, 4 + kt, g * P:(g + 1) * P], pwb[n % 4][:, g, kt * P:(kt + 1) * P], ident)
                    ins.then_inc(w_t.sem, 1)

            def w_values(n):
                i, kv = divmod(n, 2)
                pe.wait_ge(w_tact.sem, w_tact.at(l, n + 1))
                if n >= 2:
                    pe.wait_ge(w_tdve.sem, w_tdve.at(l, n - 1))
                if kv == 0 and i >= 2:
                    pe.wait_ge(w_o.sem, w_o.at(l, i - 1))
                tiles = [0] if i == 0 else [i - 1, i]
                for kt, key in enumerate(tiles):
                    ins = mm(ps[kv * 64:kv * 64 + 64, 6 + i % 2, :], v[:, key, kv * 64:kv * 64 + 64], ptb[n % 2][:, kt, :],
                             start=kt == 0, stop=kt == len(tiles) - 1)
                ins.then_inc(w_pv.sem, 1)

            def q_nope(h):
                bank = 6 if h == 0 else 4
                for k in range(3):
                    ins = by_weights([ps[:, bank, 0:HALF], ps[:, bank + 1, 0:HALF]], (uq_hi, uq_lo), k,
                                     slice(h * (NOPE + ROPE), h * (NOPE + ROPE) + NOPE), cqh[:, k], cql[:, k], k == 0, k == 2)
                if h < BH - 1:
                    ins.then_inc(qn_done.sem, 1)
                else:
                    ins.then_inc(unit_used.sem, 1)

            w_scores(0)
            w_scores(1)
            pe.wait_ge(q_act.sem, q_act.at(l, NT))
            pe.wait_ge(uqr_new.sem, uqr_new.at(l, NT))
            q_nope(0)
            w_scores(2)
            for n in range(8):
                w_turn(n)
                if n + 3 < 8:
                    w_scores(n + 3)
                if n == 0:
                    pe.wait_ge(qn_lo.sem, qn_lo.at(l, 1))
                w_values(n)
            def q_latent(h):
                pe.wait_ge(qn_lo.sem, qn_lo.at(l, h + 1))
                for c in range(2):
                    bank = 4 + 2 * c
                    if h == 0 and c == 0:
                        pe.wait_ge(w_tact.sem, w_tact.at(l, 8))
                        pe.wait_ge(w_tdve.sem, w_tdve.at(l, 6))
                    if h >= 1 and c == 1:
                        if h == 1:
                            pe.wait_ge(v_o.sem, v_o.at(l, 1))
                        else:
                            pe.wait_ge(p_o.sem, p_o.at(l, h - 1))
                    if h == 0 and c == 1:
                        pe.wait_ge(w_o.sem, w_o.at(l, 4))
                        pe.wait_ge(v_ktact.sem, v_ktact.at(l, 1))
                        pe.wait_ge(v_knew.sem, v_knew.at(l, 1))
                    ins = by_weights([ps[:, bank, 0:HALF], ps[:, bank + 1, 0:HALF]], (ukh, ukl), h,
                                     slice(c * P, (c + 1) * P), qnh, qnl, True, True)
                    ins.then_inc(ql_done.sem, 1)

            def p_scores(h):
                pe.wait_ge(ql_lo.sem, ql_lo.at(l, 2 * h + 2))
                for i in range(TS):
                    w = max(256, (i + 1) * P)
                    o = ps[:, i, 0:w]
                    if h == 0:
                        if i == 0:
                            pe.wait_ge(v_e.sem, v_e.at(l, 1))
                    else:
                        pe.wait_ge(p_e.sem, p_e.at(l, 4 * (h - 1) + i + 1))
                    for c in range(2):
                        qh, ql = qlh[:, h % 2, c, tok(i)], qll[:, h % 2, c, tok(i)]
                        mm(o, qh, ckh[:, c, 0:w], start=c == 0, stop=False)
                        mm(o, qh, ckl[:, c, 0:w], start=False, stop=False)
                        mm(o, ql, ckh[:, c, 0:w], start=False, stop=False)
                    for x in range(2):
                        mm(o, qrT[:, h, tok(i)], krT[:, x, 0:w], start=False, stop=False)
                    ins = mm(ps[:, i, w - 256:w], ident_r, mask_own if i else mask_first, start=False, stop=True)
                    ins.then_inc(p_s.sem, 1)

            pe.wait_ge(win_in.sem, win_in.at(l, 32))
            pe.wait_ge(w_e.sem, w_e.at(l, 8))
            for b in range(DECB):
                ins = turn(ps[:, b // 4, (b % 4) * P:(b % 4 + 1) * P], wk[:, b, :], ident)
                if b % 4 == 3:
                    ins.then_inc(v_kt.sem, 1)
            q_latent(0)
            for b in range(DECB):
                for kv in range(2):
                    r = slice(kv * 64, kv * 64 + 64)
                    o = (b % 2) * 144
                    ins = mm(ps[r, b // 2, o:o + 144], qTs[r, b].rearrange("p g q -> p (g q)"), kTc[r, b, :], start=True, stop=True)
            ins.then_inc(v_s.sem, 1)
            pe.wait_ge(ql_lo.sem, ql_lo.at(l, 1))
            q_nope(1)
            p_scores(0)
            pe.wait_ge(v_zero.sem, v_zero.at(l, 1))
            pe.wait_ge(v_p.sem, v_p.at(l, 1))
            pe.wait_ge(qn_lo.sem, qn_lo.at(l, 2))
            for j in range(4):
                if j == 2:
                    pe.wait_ge(v_tact.sem, v_tact.at(l, 1))
                if j == 3:
                    pe.wait_ge(v_tdve.sem, v_tdve.at(l, 1))
                for m in range(4):
                    b, kt = 2 * j + m // 2, m % 2
                    ins = turn(ps[:, 4 + j % 2, m * P:(m + 1) * P], pws[:, b, kt * P:(kt + 1) * P], ident)
                ins.then_inc(v_t.sem, 1)
            pe.wait_ge(vnew_in.sem, vnew_in.at(l, 16))
            pe.wait_ge(v_tact.sem, v_tact.at(l, 2))
            pe.wait_ge(v_tdve.sem, v_tdve.at(l, 2))
            for b in range(DECB):
                for kv in range(2):
                    r = slice(kv * 64, kv * 64 + 64)
                    o = ps[r, 6, b * 64:(b + 1) * 64]
                    mm(o, wv[:, b, r], ptw[:, b, 0, r], start=True, stop=False)
                    ins = mm(o, vn[:, b, r], ptw[0:DECS, b, 1, r], start=False, stop=True)
            ins.then_inc(v_pv.sem, 1)

            def p_turn(h):
                pe.wait_ge(p_p.sem, p_p.at(l, 4 * h + 4))
                for j in range(TS):
                    if j == 0:
                        if h < BH - 1:
                            pe.wait_ge(ql_hi.sem, ql_hi.at(l, 2 * h + 3))
                            pe.wait_ge(ql_lo.sem, ql_lo.at(l, 2 * h + 3))
                        else:
                            pe.wait_ge(p_tact.sem, p_tact.at(l, 2 * h))
                            pe.wait_ge(p_tdve.sem, p_tdve.at(l, 2 * h))
                    if j == 2:
                        pe.wait_ge(p_tact.sem, p_tact.at(l, 2 * h + 1))
                    if j == 3:
                        pe.wait_ge(p_tdve.sem, p_tdve.at(l, 2 * h + 1))
                    for i in range(j, TS):
                        ins = turn(ps[:, 4 + j % 2, (i - j) * P:(i - j + 1) * P], pm[:, POFF[i] + j * P:POFF[i] + (j + 1) * P], ident)
                    ins.then_inc(p_t.sem, 1)

            def p_values(h):
                pe.wait_ge(p_tact.sem, p_tact.at(l, 2 * h + 2))
                pe.wait_ge(p_tdve.sem, p_tdve.at(l, 2 * h + 2))
                if h == BH - 1:
                    pe.wait_ge(p_o.sem, p_o.at(l, h))
                for c in range(2):
                    for j in range(TS):
                        ins = mm(ps[:, 6 + c, j * P:512], ckv[:, j, c * P:(c + 1) * P], ptm[:, TOFF[j]:TOFF[j] + (4 - j) * P],
                                 start=j == 0, stop=j == TS - 1)
                    ins.then_inc(p_pv.sem, 1)

            def p_out(h):
                if h == 0:
                    pe.wait_ge(uv_in.sem, uv_in.at(l, 16))
                pe.wait_ge(p_lat.sem, p_lat.at(l, h + 1))
                pe.wait_ge(p_latd.sem, p_latd.at(l, h + 1))
                for cc in range(2):
                    ins = mm(ps[:, 6, :], uv[:, cc, h * P:(h + 1) * P], olat[:, cc, :], start=cc == 0, stop=cc == 1)
                ins.then_inc(p_ob.sem, 1)

            def c_turn(b):
                pe.wait_ge(cache_in[b].sem, cache_in[b].at(l, 64))
                if b >= 2:
                    pe.wait_ge(c_act.sem, c_act.at(l, b - 1))
                    pe.wait_ge(c_dve.sem, c_dve.at(l, b - 1))
                for c in range(3):
                    for kt in range(2):
                        o = (c % 2) * 256 + kt * P
                        ins = turn(ps[:, 2 + 2 * (b % 2) + c // 2, o:o + P], cache(b)[:, kt * 384 + c * P:kt * 384 + (c + 1) * P], ident)
                ins.then_inc(c_t.sem, 1)

            def c_score(b):
                pe.wait_ge(c_act.sem, c_act.at(l, b + 1))
                pe.wait_ge(c_dve.sem, c_dve.at(l, b + 1))
                if b % 2 == 0 and b >= 4:
                    pe.wait_ge(c_e.sem, c_e.at(l, b // 2 - 1))
                r = slice((b % 2) * 64, (b % 2) * 64 + 64)
                keys = cTo if b % 2 else cT
                for c in range(3):
                    q = (qlTs[:, c, b] if c < 2 else qrTs[:, b]).rearrange("p h q -> p (h q)")
                    ins = mm(ps[r, (b // 2) % 2, 0:272], q, keys[:, c, :], start=c == 0, stop=c == 2)
                ins.then_inc(c_s.sem, 1)

            def c_probs(p):
                if p == 0:
                    pe.wait_ge(c_zero.sem, c_zero.at(l, 1))
                    pe.wait_ge(p_o.sem, p_o.at(l, 4))
                else:
                    pe.wait_ge(c_ptact.sem, c_ptact.at(l, p))
                pe.wait_ge(c_p.sem, c_p.at(l, p + 1))
                for kt in range(3):
                    ins = turn(ps[:, 6, kt * P:(kt + 1) * P], psm[:, p % 2, kt * P:(kt + 1) * P], ident)
                ins.then_inc(c_pt.sem, 1)

            def c_values(p):
                pe.wait_ge(c_ptact.sem, c_ptact.at(l, p + 1))
                if p >= 1:
                    pe.wait_ge(c_ltact.sem, c_ltact.at(l, p))
                for b in (2 * p, 2 * p + 1):
                    r = slice((b % 2) * 64, (b % 2) * 64 + 64)
                    for kt in range(2):
                        mm(ps[r, 7, 0:KL], pts[:, kt, r], cache(b)[:, kt * 384:kt * 384 + KL], start=kt == 0, stop=False)
                    ins = mm(ps[r, 7, 0:KL], pts[0:DECS, 2, r], cache(b)[0:DECS, 768:1024], start=False, stop=True)
                    ins.then_inc(c_pv.sem, 1)

            def c_lat_turn(p):
                pe.wait_ge(c_lat.sem, c_lat.at(l, p + 1))
                for c in range(2):
                    ins = turn(ps[:, 7, 256 + c * P:256 + (c + 1) * P], olats[:, c * P:(c + 1) * P], ident)
                ins.then_inc(c_lt.sem, 1)

            for h in range(BH):
                if h + 1 < BH:
                    q_latent(h + 1)
                p_turn(h)
                if h + 1 < BH:
                    p_scores(h + 1)
                else:
                    c_turn(0)
                p_values(h)
                if h + 2 < BH:
                    q_nope(h + 2)
                if h == BH - 1:
                    c_turn(1)
                p_out(h)

            def out_part(d, group):
                u = U_OUT + d
                w = unit_parts(u, P)
                pe.wait_ge(unit_lo.sem, unit_lo.at(l, u + 1))
                if d >= 2:
                    pe.wait_ge(x_new.sem, x_new.at(l, d - 1))
                b0 = 4 * group + 2 * (d % 2)
                for c in range(4 * group, 4 * group + 4):
                    if d == 0:
                        pe.wait_ge(m_lo.sem, m_lo.at(l, c + 1))
                    ins = by_weights([ps[:, b0, 0:HALF], ps[:, b0 + 1, 0:HALF]], w, c, slice(0, P), mh[:, c], ml[:, c], c % 4 == 0, c % 4 == 3)
                if group == 1:
                    ins.then_inc(unit_used.sem, 1)

            for b in range(11):
                if 2 <= b + 1 < DECB:
                    c_turn(b + 1)
                if b % 2 and b >= 3:
                    c_probs((b - 3) // 2)
                if b < DECB:
                    c_score(b)
                if b == 9:
                    out_part(1, 0)
                if b % 2 and b >= 3:
                    c_values((b - 3) // 2)
                if b == 10:
                    pe.wait_ge(ssq_new.sem, ssq_new.at(l, 7))
                    sums(ssq, 5, 0)
                if b % 2 == 0 and b >= 4:
                    c_lat_turn((b - 4) // 2)
                if b == 8:
                    pe.wait_ge(c_e.sem, c_e.at(l, 4))
                    pe.wait_ge(c_act.sem, c_act.at(l, 8))
                    pe.wait_ge(c_dve.sem, c_dve.at(l, 8))
                    out_part(0, 0)
            pe.wait_ge(c_ltact.sem, c_ltact.at(l, 4))
            for h in range(BH):
                for cc in range(2):
                    ins = mm(ps[:, 6, h * P:(h + 1) * P], uv[:, cc, h * P:(h + 1) * P], olTs[:, cc, h, :], start=cc == 0, stop=cc == 1)
            ins.then_inc(c_ob.sem, 1)
            pe.wait_ge(c_o.sem, c_o.at(l, 1))
            pe.wait_ge(diag_new.sem, diag_new.at(l, 1))
            spread(0, 6)
            out_part(0, 1)
            pe.wait_ge(ssq_new.sem, ssq_new.at(l, 10))
            pe.wait_ge(r_new.sem, r_new.at(l, 1))
            sums(ssqB, 7, 500)
            pe.wait_ge(diag_new.sem, diag_new.at(l, 2))
            spread(1, 6)
            pe.wait_ge(dve_r.sem, dve_r.at(l, 1))
            out_part(1, 1)
            for d in range(2, NC_):
                out_part(d, 0)
                out_part(d, 1)

            def ffn_tile(unit, odd, first=False):
                for up in range(2):
                    b0 = 4 * odd + 2 * up
                    w = unit_parts(U_FFN + up, P)
                    pe.wait_ge(unit_lo.sem, unit_lo.at(l, unit + (up + 1)))
                    for c in range(NC_):
                        if first and up == 0:
                            pe.wait_ge(n_lo.sem, n_lo.at(l, c + 2))
                        ins = by_weights([ps[:, b0, 0:HALF], ps[:, b0 + 1, 0:HALF]], w, c, slice(0, P), nh[:, c], nl[:, c], c == 0, c == NC_ - 1)
                    ins.then_inc(unit_used.sem, 1)
                    if first and up == 0:
                        pe.wait_ge(ssq_new.sem, ssq_new.at(l, 17))
                        sums(ssq, 7, 500)
                if first:
                    pe.wait_ge(diag_new.sem, diag_new.at(l, 3))
                    spread(0, 4)
                    pe.wait_ge(r_new.sem, r_new.at(l, 2))

            for blk in range(NBLK):
                u0, n0 = U_FFN + blk * BLK_U, blk * FT
                pe.wait_ge(x_new.sem, x_new.at(l, 8 + 8 * blk - 1))
                ffn_tile(u0, 0, first=blk == 0)
                pe.wait_ge(x_new.sem, x_new.at(l, 8 + 8 * blk))
                ffn_tile(u0 + 2, 1)
                pe.wait_ge(u_scaled.sem, u_scaled.at(l, n0 + 1))
                ffn_tile(u0 + 4, 0)
                with pe.Fori(0, (FT - 3) // 2) as pair:
                    for odd in (1, 0):
                        i = 4 - odd
                        pe.wait_ge(u_scaled.sem, u_scaled.at(l, pair * 2 + (n0 + i - 1)))
                        ffn_tile(pair * 4 + (u0 + 2 * i), odd)
                for d in range(NC_):
                    u = u0 + 2 * FT + d
                    w = unit_parts(u, P)
                    b0 = 2 * DOWN_PAIR[d]
                    pe.wait_ge(unit_lo.sem, unit_lo.at(l, u + 1))
                    if d < 4:
                        pe.wait_ge(u_scaled.sem, u_scaled.at(l, blk * FT + (FT - 1 if d < 2 else FT)))
                    elif d < 6:
                        pe.wait_ge(x_new.sem, x_new.at(l, 8 + 8 * blk + d - 1))
                    for f in range(FT):
                        if d == 0:
                            pe.wait_ge(h_lo.sem, h_lo.at(l, blk * FT + f + 1))
                        ins = by_weights([ps[:, b0, 0:HALF], ps[:, b0 + 1, 0:HALF]], w, f, slice(0, P), hh[:, f], hl[:, f], f == 0, f == FT - 1)
                    ins.then_inc(unit_used.sem, 1)
        def y_turn(t):
            for c in range(NC_):
                ins = turn(ps[:, 2 * (t % 3) + c // 4, (c % 4) * P:(c % 4 + 1) * P], xT[:, c, tok(t)], ident)
            ins.then_inc(y_turned.sem, 1)

        pe.wait_ge(x_new.sem, x_new.at(DEPTH, 0))
        for t in range(3):
            y_turn(t)
        pe.wait_ge(ssq_new.sem, ssq_new.at(DEPTH, 1))
        sums(ssq, 7, 500)
        for t in range(3, NT):
            pe.wait_ge(y_scaled.sem, t - 2)
            pe.wait_ge(y_dve.sem, t - 2)
            y_turn(t)

    def adds_before(c):
        return 0 if c < 2 else max(1, c - 2)

    @block.scalar
    def _(act):
        run = nc.scalar.activation

        def normed(l, c, src, gain, hi, hi_done, sq_done_before):
            run(hi[:, c, :], src[:, c, :], ACT.Copy, scale=gain).then_inc(hi_done.sem, 1)
            act.wait_ge(ssq_new.sem, sq_done_before)
            run(sq[:, c % 2, :], src[:, c, :], ACT.Square).then_inc(sq_new.sem, 1)

        def weight_hi(l, u):
            s = unit_slot(u)
            act.wait_ge(raw_in[s].sem, raw_value(s, l, u))
            act.wait_ge(unit_used.sem, unit_used.at(l, used_before(u)))
            run(whi[:, slot(s, unit_width(u))], wraw[:, slot(s, unit_width(u))], ACT.Copy).then_inc(unit_hi.sem, 1)

        act.wait_ge(consts_in.sem, 48)
        for c in range(NC_ - 1):
            act.wait_ge(x_turned.sem, c + 1)
            turned = ps[:, 2 * (c % 4):2 * (c % 4) + 2, :].rearrange("p a n -> p (a n)")[:, 0:T]
            run(nh[:, c, :], turned, ACT.Copy, scale=gv[:, G_NEXT + c:G_NEXT + c + 1]).then_inc(n_hi.sem, 1)
        for l in layers(act):
            last = NC_ - 1
            weight_hi(l, 0)
            act.wait_ge(x_new.sem, x_new.at(l, 0))
            run(nh[:, last, :], xT[:, last, :], ACT.Copy, scale=gv[:, G_NEXT + last:G_NEXT + last + 1]).then_inc(n_hi.sem, 1)
            weight_hi(l, 1)
            act.wait_ge(ssq_new.sem, ssq_new.at(l, adds_before(last) - 6))
            run(sq[:, last % 2, :], xT[:, last, :], ACT.Square).then_inc(sq_new.sem, 1)
            for u in range(WIN_U):
                g, kp = divmod(u, 4)
                if u + 2 < WIN_U:
                    weight_hi(l, u + 2)
                if u == WIN_U - 1:
                    act.wait_ge(raw_in[0].sem, raw_value(0, l, U_UQ))
                    act.wait_ge(unit_used.sem, unit_used.at(l, WIN_U - 1))
                    run(whi[:, slot(0)], wraw[:, slot(0)], ACT.Copy).then_inc(uq_hi_first.sem, 1)
                if kp == 3:
                    if g == 0:
                        act.wait_ge(stat_sum.sem, stat_sum.at(l, 1))
                        run(sd[:, 0:NT], ps[:, 7, 0:NT], ACT.Sqrt, bias=eps, scale=1.0 / D).then_inc(stat_sd.sem, 1)
                        act.wait_ge(stat_r.sem, stat_r.at(l, 1))
                    c0, w = GROUPS[g]
                    for t in range(NT):
                        if t < TS:
                            act.wait_ge(in_done.sem, in_done.at(l, 4 * g + t + 1))
                        else:
                            act.wait_ge(unit_used.sem, unit_used.at(l, u + 1))
                        run(hm[:, t, c0:c0 + w], ps[:, (g * NT + t) % 7, 0:w], ACT.Copy, scale=rs[:, t:t + 1]).then_inc(hm_new.sem, 1)
                    if g == 1:
                        act.wait_ge(hm_new.sem, hm_new.at(l, 10))
                        for t in range(NT):
                            run(junk[:, t, 0:QL], hm[:, t, C_Q:C_KV], ACT.Square, scale=QL ** -0.5, accum_out=ms[:, t:t + 1]).then_inc(lat_ms.sem, 1)
                            run(junk[:, t, QL:], hm[:, t, C_KV:C_KR], ACT.Square, scale=KL ** -0.5, accum_out=ms[:, NT + t:NT + t + 1]).then_inc(lat_ms.sem, 1)
                        act.wait_ge(lat_ms.sem, lat_ms.at(l, 10))
                        run(sd[:, 0:10], ms[:, 0:10], ACT.Sqrt, bias=eps).then_inc(stat_sd.sem, 1)
                        run(v[:, :, :], hm[:, :, C_V:C_Q], ACT.Copy).then_inc(v_new.sem, 1)
                if u == 8:
                    act.wait_ge(k_roped.sem, k_roped.at(l, 1))
                    k = hm[:, 0:TS, C_K:C_V].rearrange("p t (h d) -> p t h d", d=64)
                    for x in range(2):
                        run(k2[:, :, x:8:4, :], k, ACT.Copy)
                    for x in range(2):
                        run(k2[:, :, 8 + x, :], hm[:, 0:TS, C_KR:IN_W], ACT.Copy)
                    for x in range(2):
                        ins = run(krd[:, x, :], hm[:, TS, C_KR:IN_W], ACT.Copy)
                    ins.then_inc(k_hi.sem, 1)

            def keys_out_act(t):
                banks = (3, 4, 5) if t % 2 else (1, 2, 7)
                if t < TS:
                    act.wait_ge(k_turned.sem, k_turned.at(l, 3 * t + 1))
                    run(kaT[:, :, tok(t)], ps[:, banks[0], :].rearrange("p (h n) -> p h n", h=4), ACT.Copy).then_inc(k_act.sem, 1)
                    act.wait_ge(k_turned.sem, k_turned.at(l, 3 * t + 2))
                    run(ckh[:, :, tok(t)], ps[:, banks[1], 256:512].rearrange("p (h n) -> p h n", h=2), ACT.Copy).then_inc(k_act.sem, 1)
                act.wait_ge(k_turned.sem, k_turned.at(l, min(3 * t + 3, 14)))
                run(cqh[:, :, tok(t)], ps[:, banks[2], 0:QL].rearrange("p (k n) -> p k n", k=3), ACT.Copy).then_inc(k_act.sem, 1)

            def queries_hi(t):
                act.wait_ge(q_roped.sem, q_roped.at(l, t + 1))
                if t < 2:
                    act.wait_ge(k_turned.sem, k_turned.at(l, 3 * t + 5))
                else:
                    act.wait_ge(q_turned.sem, q_turned.at(l, 2 * (t - 1)))
                q = hm[:, t, 0:C_K]
                if t < TS:
                    run(q2[:, t % 2, :, 0:64], q.rearrange("p (h d) -> p h d", d=64), ACT.Copy).then_inc(q_hi.sem, 1)
                else:
                    run(q2s[:, :, :, :], q.rearrange("p (e g d) -> p g e d", e=2, g=4), ACT.Copy).then_inc(q_hi.sem, 1)

            def queries_out_act(t):
                bank = 3 if t % 2 else 6
                act.wait_ge(q_turned.sem, q_turned.at(l, 2 * t + 1))
                if t < TS:
                    run(qaT[:, 0:4, tok(t)], ps[:, bank, :].rearrange("p (h n) -> p h n", h=4), ACT.Copy).then_inc(q_act.sem, 1)
                else:
                    run(qTs[:, :, :, :], ps[:, bank, :].rearrange("p (g b q) -> p b g q", g=4, b=DECB), ACT.Copy).then_inc(q_act.sem, 1)

            def rope_q_hi(t):
                act.wait_ge(uqr_rope.sem, uqr_rope.at(l, t + 1))
                if t >= 2:
                    act.wait_ge(uqr_turned.sem, uqr_turned.at(l, t - 1))
                run(q2r[:, t % 2, :, 0:64], qra[:, t % 2, :].rearrange("p (h d) -> p h d", d=64), ACT.Copy).then_inc(uqr_hi.sem, 1)

            def rope_q_out(t):
                act.wait_ge(uqr_turned.sem, uqr_turned.at(l, t + 1))
                src = ps[:, 1 if t % 2 else 7, :]
                if t < TS:
                    dst, src = qrT[:, :, tok(t)], src.rearrange("p (h n) -> p h n", h=BH)
                else:
                    dst, src = qrTs[:, :, :, :], src.rearrange("p (h b q) -> p b h q", h=BH, b=DECB)
                run(dst, src, ACT.Copy).then_inc(uqr_new.sem, 1)

            rest = slice(SLOT, unit_width(U_UQ))
            keys_out_act(0)
            keys_out_act(1)
            queries_hi(0)
            act.wait_ge(unit_used.sem, unit_used.at(l, WIN_U))
            run(whi[:, rest], wraw[:, rest], ACT.Copy).then_inc(unit_hi.sem, 1)
            keys_out_act(2)
            queries_hi(1)
            keys_out_act(3)
            queries_out_act(0)
            keys_out_act(4)
            queries_hi(2)
            queries_out_act(1)
            rope_q_hi(0)
            rope_q_hi(1)
            queries_hi(3)
            rope_q_out(0)
            queries_out_act(2)
            rope_q_hi(2)
            rope_q_out(1)
            queries_out_act(3)
            rope_q_hi(3)
            rope_q_out(2)
            queries_hi(4)
            rope_q_hi(4)
            rope_q_out(3)
            queries_out_act(4)
            rope_q_out(4)
            for cc in range(2):
                act.wait_ge(uk_turned.sem, uk_turned.at(l, cc + 1))
                run(ukh[:, :, cc * P:(cc + 1) * P], ps[:, 4 + cc, :].rearrange("p (h n) -> p h n", h=BH), ACT.Copy).then_inc(uk_hi.sem, 1)

            def w_exps(n):
                act.wait_ge(w_nm.sem, w_nm.at(l, n + 1))
                if n >= 4:
                    act.wait_ge(w_t.sem, w_t.at(l, turned_by(n - 4)))
                for g in range(4):
                    run(pwb[n % 4][:, g, :], ps[:, 2 * (n % 2) + g // 2, (g % 2) * 256:(g % 2 + 1) * 256], ACT.Exp,
                        bias=four_of(nm, n)[:, g:g + 1], scale=A_SCALE, accum_out=four_of(rsum, n)[:, g:g + 1])
                run(four_of(es, n), four_of(ed, n), ACT.Exp).then_inc(w_e.sem, 1)

            def w_out_act(i):
                act.wait_ge(w_pv.sem, w_pv.at(l, 2 * i + 2))
                run(oT[:, 0:4, tok(i)], ps[:, 6 + i % 2, :].rearrange("p (g n) -> p g n", g=4), ACT.Copy).then_inc(w_o.sem, 1)

            def q_nope_hi(h):
                if h < BH - 1:
                    act.wait_ge(qn_done.sem, qn_done.at(l, h + 1))
                else:
                    act.wait_ge(unit_used.sem, unit_used.at(l, U_UQ + 1))
                bank = 6 if h == 0 else 4
                run(halves(qnh[:, :]), ps[:, bank:bank + 2, 0:HALF], ACT.Copy).then_inc(qn_hi.sem, 1)

            w_exps(0)
            w_exps(1)
            q_nope_hi(0)
            act.wait_ge(out_hm.sem, out_hm.at(l, 80))
            for n in range(8):
                act.wait_ge(w_t.sem, w_t.at(l, turned_by(n) - (n >= 2)))
                if n >= 2:
                    act.wait_ge(w_pv.sem, w_pv.at(l, n - 1))
                run(ptb[n % 2][:, 0, :], ps[:, 4, :], ACT.Copy).then_inc(w_tact.sem, 1)
                if n + 2 < 8:
                    w_exps(n + 2)
                if n >= 2 and n % 2 == 0:
                    w_out_act(n // 2 - 1)
            w_out_act(3)
            def q_latent_hi(h):
                rest = PROMPT - HALF
                for c in range(2):
                    act.wait_ge(ql_done.sem, ql_done.at(l, 2 * h + c + 1))
                    bank = 4 + 2 * c
                    run(qlh[:, h % 2, c, 0:HALF], ps[:, bank, 0:HALF], ACT.Copy)
                    run(qlh[:, h % 2, c, HALF:PROMPT], ps[:, bank + 1, 0:rest], ACT.Copy)
                    run(qlTs[:, c, :, h, :], ps[:, bank + 1, rest:HALF].rearrange("p (b q) -> p b q", b=DECB), ACT.Copy).then_inc(ql_hi.sem, 1)

            def p_exps(h):
                for i in range(TS):
                    w = (i + 1) * P
                    act.wait_ge(p_nm.sem, p_nm.at(l, 4 * h + i + 1))
                    if h >= 1 and i == 0:
                        act.wait_ge(p_t.sem, p_t.at(l, 4 * h))
                    run(pm[:, POFF[i]:POFF[i] + w], ps[:, i, 0:w], ACT.Exp, bias=nm[0][:, i:i + 1], scale=B_SCALE,
                        accum_out=rsum[0][:, i:i + 1]).then_inc(p_e.sem, 1)

            act.wait_ge(v_kt.sem, v_kt.at(l, 1))
            run(kTc[:, 0:4, 0:P], ps[:, 0, :].rearrange("p (b n) -> p b n", b=4), ACT.Copy).then_inc(v_ktact.sem, 1)
            q_latent_hi(0)
            act.wait_ge(v_nm.sem, v_nm.at(l, 1))
            for b in range(DECB):
                run(pws[:, b, 0:144], ps[:, b // 2, (b % 2) * 144:(b % 2 + 1) * 144], ACT.Exp, bias=nm[0][:, b:b + 1],
                    scale=A_SCALE, accum_out=rsum[0][:, b:b + 1])
            run(es[0][:, 0:8], nm[0][:, 0:8], ACT.Exp, bias=gv[:, G_SINKS:G_SINKS + 1]).then_inc(v_e.sem, 1)
            q_nope_hi(1)
            p_exps(0)
            for j in (0, 2):
                act.wait_ge(v_t.sem, v_t.at(l, j + 1))
                run(ptw[:, 2 * j:2 * j + 2, :, :], ps[:, 4, :].rearrange("p (b k n) -> p b k n", b=2, k=2), ACT.Copy).then_inc(v_tact.sem, 1)
            act.wait_ge(v_pv.sem, v_pv.at(l, 1))
            for g in range(4):
                ins = run(oT[:, g, PROMPT:T].rearrange("p (b q) -> p b q", b=DECB),
                          ps[:, 6, :].rearrange("p (b g q) -> p b g q", b=DECB, g=4)[:, :, g, :], ACT.Copy)
            ins.then_inc(v_o.sem, 1)

            def keys_copy(b):
                act.wait_ge(c_t.sem, c_t.at(l, b + 1))
                if b >= 2:
                    act.wait_ge(c_s.sem, c_s.at(l, b - 1))
                keys, bank = (cTo, 4) if b % 2 else (cT, 2)
                run(keys[:, 0:2, 0:PAST], ps[:, bank, :].rearrange("p (c n) -> p c n", c=2), ACT.Copy).then_inc(c_act.sem, 1)

            for h in range(BH):
                if h + 1 < BH:
                    q_latent_hi(h + 1)
                for j in (0, 2):
                    act.wait_ge(p_t.sem, p_t.at(l, 4 * h + j + 1))
                    run(ptm[:, TOFF[j]:TOFF[j] + (4 - j) * P], ps[:, 4, 0:(4 - j) * P], ACT.Copy).then_inc(p_tact.sem, 1)
                if h + 1 < BH:
                    p_exps(h + 1)
                else:
                    keys_copy(0)
                act.wait_ge(p_pv.sem, p_pv.at(l, 2 * h + 1))
                run(olat[:, 0, :], ps[:, 6, :], ACT.Copy).then_inc(p_lat.sem, 1)
                if h + 2 < BH:
                    q_nope_hi(h + 2)
                if h == BH - 1:
                    keys_copy(1)
                act.wait_ge(p_ob.sem, p_ob.at(l, h + 1))
                run(oT[:, 4 + h, 0:PROMPT], ps[:, 6, :], ACT.Copy).then_inc(p_o.sem, 1)
                act.wait_ge(p_o.sem, p_o.at(l, h + 1))
                act.wait_ge(ssq_new.sem, ssq_new.at(l, 1 + h // 2))
                run(sq[:, h % 2, 0:PROMPT], oT[:, 4 + h, 0:PROMPT], ACT.Square).then_inc(sq_new.sem, 1)

            def mixed(c):
                run(mh[:, c, :], oT[:, c, :], ACT.Copy, scale=gv[:, G_MIX + c:G_MIX + c + 1]).then_inc(m_hi.sem, 1)

            def mixed_square(c):
                act.wait_ge(ssq_new.sem, ssq_new.at(l, min(c + 3, 5)))
                run(sq[:, c % 2, :], oT[:, c, :], ACT.Square).then_inc(sq_new.sem, 1)

            def spread_out(k, read):
                act.wait_ge(bcast.sem, bcast.at(l, k))
                run(rA[:, :], read.rearrange("p a n -> p (a n)")[:, 0:T], ACT.Copy).then_inc(r_new.sem, 1)

            act.wait_ge(out_ckv.sem, out_ckv.at(l, 16))
            for b in range(11):
                if 2 <= b + 1 < DECB:
                    keys_copy(b + 1)
                if b % 2 and b >= 3:
                    p = (b - 3) // 2
                    act.wait_ge(c_pt.sem, c_pt.at(l, p + 1))
                    run(pts[:, :, :], ps[:, 6, 0:384].rearrange("p (k n) -> p k n", k=3), ACT.Copy).then_inc(c_ptact.sem, 1)
                if b % 2 and b < DECB:
                    p = b // 2
                    act.wait_ge(c_nm.sem, c_nm.at(l, p + 1))
                    if p >= 2:
                        act.wait_ge(c_pt.sem, c_pt.at(l, p - 1))
                    run(psm[:, p % 2, 0:272], ps[:, p % 2, 0:272], ACT.Exp, bias=nm[1][:, p:p + 1], scale=B_SCALE,
                        accum_out=rsum[1][:, p:p + 1]).then_inc(c_e.sem, 1)
                    mixed(p)
                if b in (2, 4, 6, 8):
                    mixed_square(b // 2 - 1)
                if b == 10:
                    act.wait_ge(stat_sum.sem, stat_sum.at(l, 2))
                    run(sd[:, 0:NT], ps[:, 5, 0:NT], ACT.Sqrt, bias=eps, scale=2.0 / D).then_inc(stat_sd.sem, 1)
                if b % 2 == 0 and b >= 4:
                    p = (b - 4) // 2
                    act.wait_ge(c_lt.sem, c_lt.at(l, p + 1))
                    for c in range(2):
                        dst = olTs[:, c, :, 32 * p:32 * (p + 1)].rearrange("p h (b q) -> p h b q", b=2)
                        src = ps[:, 7, 256 + c * P:256 + (c + 1) * P].rearrange("p (b h q) -> p h b q", b=2, h=BH)
                        ins = run(dst, src, ACT.Copy)
                    ins.then_inc(c_ltact.sem, 1)
                if b in (4, 6):
                    weight_hi(l, U_OUT + b // 2 - 2)
            act.wait_ge(c_ob.sem, c_ob.at(l, 1))
            run(oT[:, 4:8, PROMPT:T], ps[:, 6, :].rearrange("p (h n) -> p h n", h=BH), ACT.Copy).then_inc(c_o.sem, 1)
            act.wait_ge(c_o.sem, c_o.at(l, 1))
            mixed(4)
            act.wait_ge(ssq_new.sem, ssq_new.at(l, 6))
            run(sq[:, 0, 0:PROMPT].rearrange("p (h n) -> p h n", h=BH), oT[:, 4:8, PROMPT:T], ACT.Square).then_inc(sq_new.sem, 1)
            mixed(5)
            spread_out(1, ps[:, 6:8, :])
            mixed(6)
            mixed(7)
            act.wait_ge(stat_sum.sem, stat_sum.at(l, 3))
            run(sd[:, NT:10], ps[:, 7, 500:505], ACT.Sqrt, bias=eps, scale=2.0 / D).then_inc(stat_sd.sem, 1)
            for d in range(NC_):
                weight_hi(l, U_OUT + d + 2)
                act.wait_ge(x_new.sem, x_new.at(l, d + 1))
                normed(l, d, xT, gv[:, G_FFN + d:G_FFN + d + 1], nh, n_hi, ssq_new.at(l, 10 + adds_before(d)))
            for blk in range(NBLK):
                u0 = U_FFN + blk * BLK_U
                n0 = blk * FT

                def ffn_hi(s, i):
                    act.wait_ge(raw_in[s].sem, raw_ffn(s, l, blk, i))
                    act.wait_ge(unit_used.sem, unit_used.at(l, i * 2 + (u0 + s - 1)))
                    w = slot(s, NC_ * P)
                    run(whi[:, w], wraw[:, w], ACT.Copy).then_inc(unit_hi.sem, 1)

                def ffn_tile(i, odd):
                    if isinstance(i, int) and i == FT - 1:
                        weight_hi(l, u0 + 2 * FT)
                    else:
                        ffn_hi(0, i + 1)
                    if isinstance(i, int) and n0 + i == 0:
                        act.wait_ge(stat_sum.sem, stat_sum.at(l, 4))
                        run(sd[:, 0:NT], ps[:, 7, 500:505], ACT.Sqrt, bias=eps, scale=1.0 / D).then_inc(stat_sd.sem, 1)
                        spread_out(3, ps[:, 4:6, :])
                    act.wait_ge(g_scaled.sem, g_scaled.at(l, i + (n0 + 1)))
                    run(tg[:, odd, :], tg[:, odd, :], ACT.Silu).then_inc(silu_new.sem, 1)
                    act.wait_ge(h_new.sem, h_new.at(l, i + (n0 + 1)))
                    if isinstance(i, int) and i == FT - 1:
                        weight_hi(l, u0 + 2 * FT + 1)
                    else:
                        ffn_hi(1, i + 1)
                    run(hh[:, i, :], tu[:, odd, :], ACT.Copy).then_inc(h_hi.sem, 1)

                ffn_tile(0, 0)
                with act.Fori(0, (FT - 3) // 2) as pair:
                    ffn_tile(pair * 2 + 1, 1)
                    ffn_tile(pair * 2 + 2, 0)
                ffn_tile(FT - 2, 1)
                ffn_tile(FT - 1, 0)
                for d in range(NC_):
                    u = u0 + 2 * FT + d
                    if u + 2 < UNITS:
                        weight_hi(l, u + 2)
                    if blk == NBLK - 1 and d < NC_ - 1:
                        act.wait_ge(x_new.sem, x_new.at(l, 8 + 8 * blk + d + 1))
                        normed(l, d, xT, gv[:, G_NEXT + d:G_NEXT + d + 1], nh, n_hi, ssq_new.at(l, 17 + adds_before(d)))
        act.wait_ge(x_new.sem, x_new.at(DEPTH, 0))
        act.wait_ge(ssq_new.sem, ssq_new.at(DEPTH, adds_before(NC_ - 1) - 6))
        run(sq[:, (NC_ - 1) % 2, :], xT[:, NC_ - 1, :], ACT.Square).then_inc(sq_new.sem, 1)
        act.wait_ge(stat_sum.sem, stat_sum.at(DEPTH, 1))
        run(sd[:, 0:NT], ps[:, 7, 500:505], ACT.Sqrt, bias=eps, scale=1.0 / D).then_inc(stat_sd.sem, 1)
        act.wait_ge(stat_r.sem, stat_r.at(DEPTH, 1))
        for t in range(NT):
            act.wait_ge(y_turned.sem, t + 1)
            run(yout[:, t, 0:512], ps[:, 2 * (t % 3), :], ACT.Copy, scale=rs[:, t:t + 1]).then_inc(y_scaled.sem, 1)

    @block.vector
    def _(dve):
        vec = nc.vector
        steps = [0]

        def weight_lo(l, u):
            s = unit_slot(u)
            dve.wait_ge(unit_hi.sem, unit_hi.at(l, u + 1))
            w = slot(s, unit_width(u))
            vec.tensor_tensor(wlo[:, w], wraw[:, w], whi[:, w], ALU.subtract).then_inc(unit_lo.sem, 1)

        def low(out, src, gain, high):
            return vec.scalar_tensor_tensor(out=out, in0=src, scalar=gain, in1=high, op0=ALU.mult, op1=ALU.subtract)

        dve.sem_inc(unit_lo.sem, 2)
        dve.wait_ge(consts_in.sem, 48)
        vec.tensor_copy(kmask[:, :], mask_in[:, :])
        for c in range(NC_):
            if c < NC_ - 1:
                dve.wait_ge(n_hi.sem, c + 1)
            else:
                dve.wait_ge(x_turned.sem, NC_)
            turned = ps[:, 2 * (c % 4):2 * (c % 4) + 2, :].rearrange("p a n -> p (a n)")[:, 0:T]
            vec.tensor_copy(xT[:, c, :], turned).then_inc(x_new.sem, 1)
            if c < NC_ - 1:
                dve.wait_ge(x_new.sem, c + 1)
                low(nl[:, c, :], xT[:, c, :], gv[:, G_NEXT + c:G_NEXT + c + 1], nh[:, c, :]).then_inc(n_lo.sem, 1)
        for l in layers(dve):
            steps[0] = 0

            def link(ins):
                steps[0] += 1
                ins.then_inc(dve_step.sem, 1)
                dve.wait_ge(dve_step.sem, dve_step.at(l, steps[0]))

            def rotate_keys():
                tables = kc[:, K_ROPE:K_ROPE + NT * 128].rearrange("p (t n) -> p t n", t=NT)
                for c0, heads in ((C_K, 2), (C_KR, 1)):
                    for h in range(heads):
                        col = c0 + 64 * h
                        src, o = hm[:, :, col:col + 64], slice(64 * h, 64 * h + 64)
                        vec.tensor_tensor(kcos[:, :, o], src, tables[:, :, 0:64], ALU.mult)
                        vec.tensor_tensor(ksin[:, :, 64 * h:64 * h + 32], src[:, :, 32:64], tables[:, :, 64:96], ALU.mult)
                        ins = vec.tensor_tensor(ksin[:, :, 64 * h + 32:64 * h + 64], src[:, :, 0:32], tables[:, :, 96:128], ALU.mult)
                    link(ins)
                    w = 64 * heads
                    ins = vec.tensor_tensor(hm[:, :, c0:c0 + w], kcos[:, :, 0:w], ksin[:, :, 0:w], ALU.add)
                    if heads == 2:
                        link(ins)
                ins.then_inc(k_roped.sem, 1)

            def rotate_queries(t):
                dve.wait_ge(hm_new.sem, hm_new.at(l, 10 + t + 1))
                q = hm[:, t, 0:C_K].rearrange("p (h d) -> p h d", d=64)
                a3, b3 = (x[:, t % 2, :].rearrange("p (h d) -> p h d", d=64) for x in (qcos, qsin))
                s3 = sin[t].unsqueeze(1)
                vec.tensor_tensor(b3[:, :, 0:32], q[:, :, 32:64], s3[:, :, 0:32].broadcast_to([P, AH, 32]), ALU.mult)
                link(vec.tensor_tensor(b3[:, :, 32:64], q[:, :, 0:32], s3[:, :, 32:64].broadcast_to([P, AH, 32]), ALU.mult))
                dve.wait_ge(q_cos.sem, q_cos.at(l, t + 1))
                vec.tensor_tensor(q, a3, b3, ALU.add).then_inc(q_roped.sem, 1)

            def latents_norm():
                dve.wait_ge(stat_sd.sem, stat_sd.at(l, 2))
                link(vec.reciprocal(rl[:, 0:10], sd[:, 0:10]))
                dve.wait_ge(vectors_in.sem, vectors_in.at(l, 48))
                for t in range(NT):
                    vec.scalar_tensor_tensor(out=ckv[:, t, :], in0=hm[:, t, C_KV:C_KR], scalar=rl[:, NT + t:NT + t + 1], in1=kvg[:, :],
                                             op0=ALU.mult, op1=ALU.mult).then_inc(ckv_norm.sem, 1)
                    q = hm[:, t, C_Q:C_KV]
                    vec.scalar_tensor_tensor(out=q, in0=q, scalar=rl[:, t:t + 1], in1=qg[:, :], op0=ALU.mult, op1=ALU.mult).then_inc(cq_norm.sem, 1)

            last = NC_ - 1
            weight_lo(l, 0)
            dve.wait_ge(n_hi.sem, n_hi.at(l, 1))
            low(nl[:, last, :], xT[:, last, :], gv[:, G_NEXT + last:G_NEXT + last + 1], nh[:, last, :]).then_inc(n_lo.sem, 1)
            weight_lo(l, 1)
            for u in range(WIN_U):
                if u + 2 < WIN_U:
                    weight_lo(l, u + 2)
                if u == 3:
                    dve.wait_ge(stat_sd.sem, stat_sd.at(l, 1))
                    vec.reciprocal(rs[:, 0:NT], sd[:, 0:NT]).then_inc(stat_r.sem, 1)
                if u == WIN_U - 1:
                    dve.wait_ge(uq_hi_first.sem, uq_hi_first.at(l, 1))
                    vec.tensor_tensor(wlo[:, slot(0)], wraw[:, slot(0)], whi[:, slot(0)], ALU.subtract).then_inc(uq_lo_first.sem, 1)
                if u == 7:
                    dve.wait_ge(hm_new.sem, hm_new.at(l, 10))
                    rotate_keys()
                if u == 8:
                    latents_norm()

            def keys_out_dve(t):
                banks = (3, 4, 5) if t % 2 else (1, 2, 7)
                four = ps[:, banks[1], :].rearrange("p (h n) -> p h n", h=4)
                if t < TS:
                    dve.wait_ge(k_turned.sem, k_turned.at(l, 3 * t + 2))
                    dve.wait_ge(k_act.sem, k_act.at(l, 3 * t + 2))
                    vec.tensor_copy(krT[:, :, tok(t)], four[:, 0:2, :])
                    vec.tensor_tensor(ckl[:, :, tok(t)], four[:, 2:4, :], ckh[:, :, tok(t)], ALU.subtract).then_inc(k_dve.sem, 1)
                else:
                    dve.wait_ge(k_turned.sem, k_turned.at(l, 13))
                    vec.tensor_copy(kTs[:, :], four[:, 0, :])
                    vec.tensor_copy(krTs[:, :], four[:, 1, :])
                    vec.tensor_copy(ckTs[:, :, :], four[:, 2:4, :]).then_inc(k_dve.sem, 1)
                dve.wait_ge(k_act.sem, k_act.at(l, min(3 * t + 3, 13)))
                vec.tensor_tensor(cql[:, :, tok(t)], ps[:, banks[2], 0:QL].rearrange("p (k n) -> p k n", k=3), cqh[:, :, tok(t)],
                                  ALU.subtract).then_inc(k_dve.sem, 1)

            def queries_out_dve(t):
                dve.wait_ge(q_turned.sem, q_turned.at(l, 2 * t + 2))
                vec.tensor_copy(qaT[:, 4:8, tok(t)], ps[:, 4 if t % 2 else 0, :].rearrange("p (h n) -> p h n", h=4)).then_inc(q_dve.sem, 1)

            def rotate_rope_queries(t):
                dve.wait_ge(uqr_done.sem, uqr_done.at(l, t + 1))
                src = ps[:, 2 if t % 2 else 5, 0:256].rearrange("p (h d) -> p h d", d=64)
                dst = qra[:, t % 2, :].rearrange("p (h d) -> p h d", d=64)
                c3 = cos[t].unsqueeze(1).broadcast_to([P, BH, 64])
                s3 = sin[t].unsqueeze(1)
                b3 = qrb[:, :].rearrange("p (h d) -> p h d", d=64)
                if t >= 1:
                    dve.wait_ge(uqr_rope.sem, uqr_rope.at(l, t))
                if t >= 2:
                    dve.wait_ge(uqr_lo.sem, uqr_lo.at(l, t - 1))
                vec.tensor_tensor(dst, src, c3, ALU.mult)
                vec.tensor_tensor(b3[:, :, 0:32], src[:, :, 32:64], s3[:, :, 0:32].broadcast_to([P, BH, 32]), ALU.mult)
                vec.tensor_tensor(b3[:, :, 32:64], src[:, :, 0:32], s3[:, :, 32:64].broadcast_to([P, BH, 32]), ALU.mult).then_inc(uqr_new_read.sem, 1)
                dve.wait_ge(uqr_new_read.sem, uqr_new_read.at(l, t + 1))
                vec.tensor_tensor(dst, dst, b3, ALU.add).then_inc(uqr_rope.sem, 1)

            rest = slice(SLOT, unit_width(U_UQ))
            rotate_queries(0)
            keys_out_dve(0)
            rotate_queries(1)
            keys_out_dve(1)
            dve.wait_ge(unit_hi.sem, unit_hi.at(l, U_UQ + 1))
            vec.tensor_tensor(wlo[:, rest], wraw[:, rest], whi[:, rest], ALU.subtract).then_inc(unit_lo.sem, 1)
            keys_out_dve(2)
            keys_out_dve(3)
            queries_out_dve(0)
            keys_out_dve(4)
            rotate_queries(2)
            queries_out_dve(1)
            rotate_rope_queries(0)
            rotate_rope_queries(1)
            rotate_queries(3)
            rotate_rope_queries(2)
            queries_out_dve(2)
            rotate_queries(4)
            rotate_rope_queries(3)
            queries_out_dve(3)
            rotate_rope_queries(4)
            for cc in range(2):
                dve.wait_ge(uk_hi.sem, uk_hi.at(l, cc + 1))
                vec.tensor_tensor(ukl[:, :, cc * P:(cc + 1) * P], ps[:, 4 + cc, :].rearrange("p (h n) -> p h n", h=BH),
                                  ukh[:, :, cc * P:(cc + 1) * P], ALU.subtract).then_inc(uk_lo.sem, 1)

            link(vec.tensor_scalar(nsink[:, 0:9], gv[:, G_SINK:G_SINK + 9], -1.0, None, ALU.mult))

            def w_max(n):
                kv = n % 2
                dve.wait_ge(w_s.sem, w_s.at(l, n + 1))
                s3 = ps[:, 2 * (n % 2):2 * (n % 2) + 2, :].rearrange("p a (g n) -> p a g n", g=2)
                link(vec.tensor_reduce(mx[:, 0:4].rearrange("p (a g) -> p a g", a=2), s3, AX.X, ALU.max))
                link(vec.scalar_tensor_tensor(out=four_of(nm, n), in0=mx[:, 0:4], scalar=-A_SCALE, in1=nsink[:, 4 * kv:4 * kv + 4],
                                              op0=ALU.mult, op1=ALU.min))
                vec.tensor_tensor(four_of(ed, n), four_of(nm, n), nsink[:, 4 * kv:4 * kv + 4], ALU.subtract).then_inc(w_nm.sem, 1)

            def w_norm(n):
                dve.wait_ge(w_e.sem, w_e.at(l, n + 1))
                link(vec.tensor_tensor(four_of(rsum, n), four_of(rsum, n), four_of(es, n), ALU.add))
                vec.reciprocal(four_of(rinv, n), four_of(rsum, n)).then_inc(w_rinv.sem, 1)

            def q_nope_lo(h):
                dve.wait_ge(qn_hi.sem, qn_hi.at(l, h + 1))
                bank = 6 if h == 0 else 4
                vec.tensor_tensor(halves(qnl[:, :]), ps[:, bank:bank + 2, 0:HALF], halves(qnh[:, :]), ALU.subtract).then_inc(qn_lo.sem, 1)

            w_max(0)
            w_max(1)
            w_norm(0)
            q_nope_lo(0)
            w_max(2)
            for n in range(8):
                if n + 1 < 8:
                    w_norm(n + 1)
                if n >= 2:
                    dve.wait_ge(w_t.sem, w_t.at(l, turned_by(n)))
                    dve.wait_ge(w_pv.sem, w_pv.at(l, n - 1))
                    vec.tensor_copy(ptb[n % 2][:, 1, :], ps[:, 5, :]).then_inc(w_tdve.sem, 1)
                if n + 3 < 8:
                    w_max(n + 3)
            vec.memset(pws[:, :, 144:256], 0.0).then_inc(v_zero.sem, 1)
            dve.wait_ge(v_kt.sem, v_kt.at(l, 2))
            vec.tensor_copy(kTc[:, 4:8, 0:P], ps[:, 1, :].rearrange("p (b n) -> p b n", b=4))
            vec.tensor_copy(kTc[:, :, P:144], kTs[:, :].rearrange("p (b n) -> p b n", b=DECB)).then_inc(v_knew.sem, 1)

            def q_latent_lo(h):
                rest = PROMPT - HALF
                for c in range(2):
                    dve.wait_ge(ql_hi.sem, ql_hi.at(l, 2 * h + c + 1))
                    bank = 4 + 2 * c
                    vec.tensor_tensor(qll[:, h % 2, c, 0:HALF], ps[:, bank, 0:HALF], qlh[:, h % 2, c, 0:HALF], ALU.subtract)
                    vec.tensor_tensor(qll[:, h % 2, c, HALF:PROMPT], ps[:, bank + 1, 0:rest], qlh[:, h % 2, c, HALF:PROMPT], ALU.subtract)\
                       .then_inc(ql_lo.sem, 1)

            def p_max(h):
                for i in range(TS):
                    dve.wait_ge(p_s.sem, p_s.at(l, 4 * h + i + 1))
                    link(vec.tensor_reduce(mx[:, i:i + 1], ps[:, i, 0:(i + 1) * P], AX.X, ALU.max))
                    vec.tensor_scalar(nm[0][:, i:i + 1], mx[:, i:i + 1], -B_SCALE, None, ALU.mult).then_inc(p_nm.sem, 1)

            def p_norm(h):
                for i in range(TS):
                    dve.wait_ge(p_e.sem, p_e.at(l, 4 * h + i + 1))
                    link(vec.reciprocal(rinv[0][:, i:i + 1], rsum[0][:, i:i + 1]))
                    q = pm[:, POFF[i]:POFF[i] + (i + 1) * P]
                    vec.tensor_scalar(q, q, rinv[0][:, i:i + 1], None, ALU.mult).then_inc(p_p.sem, 1)

            q_latent_lo(0)
            dve.wait_ge(v_s.sem, v_s.at(l, 1))
            link(vec.tensor_reduce(mx[:, 0:8].rearrange("p (a b) -> p a b", a=4), ps[:, 0:4, 0:288].rearrange("p a (b n) -> p a b n", b=2), AX.X, ALU.max))
            vec.tensor_scalar(nm[0][:, 0:8], mx[:, 0:8], -A_SCALE, nsink[:, 8:9], ALU.mult, ALU.min).then_inc(v_nm.sem, 1)
            dve.wait_ge(v_e.sem, v_e.at(l, 1))
            link(vec.tensor_tensor(rsum[0][:, 0:8], rsum[0][:, 0:8], es[0][:, 0:8], ALU.add))
            link(vec.reciprocal(rinv[0][:, 0:8], rsum[0][:, 0:8]))
            vec.tensor_tensor(pws[:, :, 0:144], pws[:, :, 0:144], rinv[0][:, 0:8].unsqueeze(2).broadcast_to([P, DECB, 144]), ALU.mult).then_inc(v_p.sem, 1)
            q_nope_lo(1)
            p_max(0)
            for j in (1, 3):
                dve.wait_ge(v_t.sem, v_t.at(l, j + 1))
                vec.tensor_copy(ptw[:, 2 * j:2 * j + 2, :, :], ps[:, 5, :].rearrange("p (b k n) -> p b k n", b=2, k=2)).then_inc(v_tdve.sem, 1)
            p_norm(0)

            def keys_copy(b):
                mine = slice(b * DECS, (b + 1) * DECS)
                keys, bank = (cTo, 5) if b % 2 else (cT, 3)
                if b >= 2:
                    dve.wait_ge(c_s.sem, c_s.at(l, b - 1))
                vec.tensor_copy(keys[:, 0:2, PAST:272], ckTs[:, :, mine])
                vec.tensor_copy(keys[:, 2, PAST:272], krTs[:, mine])
                dve.wait_ge(c_t.sem, c_t.at(l, b + 1))
                vec.tensor_copy(keys[:, 2, 0:PAST], ps[:, bank, 0:PAST]).then_inc(c_dve.sem, 1)

            for h in range(BH):
                if h + 1 < BH:
                    q_latent_lo(h + 1)
                for j in (1, 3):
                    dve.wait_ge(p_t.sem, p_t.at(l, 4 * h + j + 1))
                    vec.tensor_copy(ptm[:, TOFF[j]:TOFF[j] + (4 - j) * P], ps[:, 5, 0:(4 - j) * P]).then_inc(p_tdve.sem, 1)
                if h + 1 < BH:
                    p_max(h + 1)
                else:
                    keys_copy(0)
                dve.wait_ge(p_pv.sem, p_pv.at(l, 2 * h + 2))
                vec.tensor_copy(olat[:, 1, :], ps[:, 7, :]).then_inc(p_latd.sem, 1)
                if h + 2 < BH:
                    q_nope_lo(h + 2)
                if h + 1 < BH:
                    p_norm(h + 1)
                else:
                    keys_copy(1)
            vec.memset(psm[:, :, 272:384], 0.0).then_inc(c_zero.sem, 1)

            def mixed_lo(c):
                dve.wait_ge(m_hi.sem, m_hi.at(l, c + 1))
                low(ml[:, c, :], oT[:, c, :], gv[:, G_MIX + c:G_MIX + c + 1], mh[:, c, :]).then_inc(m_lo.sem, 1)

            for b in range(10):
                if 2 <= b + 1 < DECB:
                    keys_copy(b + 1)
                if b % 2 and b < DECB:
                    p = b // 2
                    dve.wait_ge(c_s.sem, c_s.at(l, b + 1))
                    link(vec.tensor_reduce(mx[:, 0:1], ps[:, p % 2, 0:272], AX.X, ALU.max))
                    vec.tensor_scalar(nm[1][:, p:p + 1], mx[:, 0:1], -B_SCALE, None, ALU.mult).then_inc(c_nm.sem, 1)
                    dve.wait_ge(c_e.sem, c_e.at(l, p + 1))
                    link(vec.reciprocal(rinv[1][:, p:p + 1], rsum[1][:, p:p + 1]))
                    vec.tensor_scalar(psm[:, p % 2, 0:272], psm[:, p % 2, 0:272], rinv[1][:, p:p + 1], None, ALU.mult).then_inc(c_p.sem, 1)
                if b % 2 and b >= 3:
                    dve.wait_ge(c_pv.sem, c_pv.at(l, b - 1))
                    vec.tensor_copy(olats[:, :], ps[:, 7, 0:KL]).then_inc(c_lat.sem, 1)
                if b % 2 and b < DECB:
                    mixed_lo(b // 2)
                if b in (4, 6):
                    weight_lo(l, U_OUT + b // 2 - 2)

            def diagonal(k, n):
                dve.wait_ge(stat_sd.sem, stat_sd.at(l, k))
                g = slice(NT * n, NT * n + NT)
                link(vec.reciprocal(rs[:, g], sd[:, g]))
                vec.tensor_tensor(diag[:, g, :], ident.unsqueeze(1).broadcast_to([P, NT, P]), rs[:, g].unsqueeze(2).broadcast_to([P, NT, P]),
                                  ALU.mult).then_inc(diag_new.sem, 1)

            diagonal(3, 0)
            for c in range(4, NC_):
                mixed_lo(c)
            diagonal(4, 1)
            dve.wait_ge(bcast.sem, bcast.at(l, 2))
            vec.tensor_copy(rB[:, :], ps[:, 6:8, :].rearrange("p a n -> p (a n)")[:, 0:T]).then_inc(dve_r.sem, 1)
            dve.wait_ge(r_new.sem, r_new.at(l, 1))
            dve.wait_ge(dve_r.sem, dve_r.at(l, 1))
            for d in range(NC_):
                b0 = 2 * (d % 2)
                dve.wait_ge(unit_used.sem, unit_used.at(l, U_OUT + d + 1))
                vec.tensor_tensor(halves(xt[:, 0, :]), ps[:, b0:b0 + 2, 0:HALF], halves(rA[:, :]), ALU.mult)
                link(vec.tensor_tensor(halves(xt[:, 1, :]), ps[:, b0 + 4:b0 + 6, 0:HALF], halves(rB[:, :]), ALU.mult))
                link(vec.tensor_tensor(xt[:, 0, :], xt[:, 0, :], xt[:, 1, :], ALU.add))
                vec.tensor_tensor(xT[:, d, :], xT[:, d, :], xt[:, 0, :], ALU.add).then_inc(x_new.sem, 1)
                weight_lo(l, U_OUT + d + 2)
                dve.wait_ge(n_hi.sem, n_hi.at(l, d + 2))
                low(nl[:, d, :], xT[:, d, :], gv[:, G_FFN + d:G_FFN + d + 1], nh[:, d, :]).then_inc(n_lo.sem, 1)
            for blk in range(NBLK):
                u0 = U_FFN + blk * BLK_U
                n0 = blk * FT

                def ffn_lo(s, i):
                    dve.wait_ge(unit_hi.sem, unit_hi.at(l, i * 2 + (u0 + s + 1)))
                    w = slot(s, NC_ * P)
                    vec.tensor_tensor(wlo[:, w], wraw[:, w], whi[:, w], ALU.subtract).then_inc(unit_lo.sem, 1)

                def hidden_lo(i, odd):
                    vec.tensor_tensor(hl[:, i, :], tu[:, odd, :], hh[:, i, :], ALU.subtract).then_inc(h_lo.sem, 1)

                def ffn_tile(i, odd):
                    first, final = (isinstance(i, int) and i == k for k in (0, FT - 1))
                    if not first:
                        dve.wait_ge(h_hi.sem, h_hi.at(l, i + n0))
                    if final:
                        weight_lo(l, u0 + 2 * FT)
                    else:
                        ffn_lo(0, i + 1)
                    if not first:
                        hidden_lo(i - 1, 1 - odd)
                    if first and blk == 0:
                        diagonal(5, 0)
                        dve.wait_ge(r_new.sem, r_new.at(l, 2))
                    base = 4 * odd
                    dve.wait_ge(unit_used.sem, unit_used.at(l, i * 2 + (u0 + 1)))
                    vec.tensor_tensor(halves(tg[:, odd, :]), ps[:, base:base + 2, 0:HALF], halves(rA[:, :]), ALU.mult).then_inc(g_scaled.sem, 1)
                    dve.wait_ge(unit_used.sem, unit_used.at(l, i * 2 + (u0 + 2)))
                    vec.tensor_tensor(halves(tu[:, odd, :]), ps[:, base + 2:base + 4, 0:HALF], halves(rA[:, :]), ALU.mult).then_inc(u_scaled.sem, 1)
                    dve.wait_ge(u_scaled.sem, u_scaled.at(l, i + (n0 + 1)))
                    dve.wait_ge(silu_new.sem, silu_new.at(l, i + (n0 + 1)))
                    vec.tensor_tensor(tu[:, odd, :], tu[:, odd, :], tg[:, odd, :], ALU.mult).then_inc(h_new.sem, 1)
                    if final:
                        weight_lo(l, u0 + 2 * FT + 1)
                        dve.wait_ge(h_hi.sem, h_hi.at(l, n0 + FT))
                        hidden_lo(i, odd)
                    else:
                        ffn_lo(1, i + 1)

                ffn_tile(0, 0)
                with dve.Fori(0, (FT - 3) // 2) as pair:
                    ffn_tile(pair * 2 + 1, 1)
                    ffn_tile(pair * 2 + 2, 0)
                ffn_tile(FT - 2, 1)
                ffn_tile(FT - 1, 0)
                for d in range(NC_):
                    u = u0 + 2 * FT + d
                    if u + 2 < UNITS:
                        weight_lo(l, u + 2)
                    b0 = 2 * DOWN_PAIR[d]
                    dve.wait_ge(unit_used.sem, unit_used.at(l, u + 1))
                    vec.tensor_tensor(halves(xT[:, d, :]), ps[:, b0:b0 + 2, 0:HALF], halves(xT[:, d, :]), ALU.add).then_inc(x_new.sem, 1)
                    if blk == NBLK - 1 and d < NC_ - 1:
                        dve.wait_ge(n_hi.sem, n_hi.at(l, 9 + d + 1))
                        low(nl[:, d, :], xT[:, d, :], gv[:, G_NEXT + d:G_NEXT + d + 1], nh[:, d, :]).then_inc(n_lo.sem, 1)
            assert steps[0] == dve_step.per, steps[0]
        dve.wait_ge(stat_sd.sem, stat_sd.at(DEPTH, 1))
        vec.reciprocal(rs[:, 0:NT], sd[:, 0:NT]).then_inc(stat_r.sem, 1)
        dve.wait_ge(stat_r.sem, stat_r.at(DEPTH, 1))
        for t in range(NT):
            dve.wait_ge(y_turned.sem, t + 1)
            if t == 0:
                dve.wait_ge(fg_in.sem, 16)
            vec.scalar_tensor_tensor(out=yout[:, t, 512:D], in0=ps[:, 2 * (t % 3) + 1, :], scalar=rs[:, t:t + 1], in1=fg[:, 512:D],
                                     op0=ALU.mult, op1=ALU.mult).then_inc(y_dve.sem, 1)

    @block.gpsimd
    def _(pool):
        add = nc.gpsimd.tensor_tensor

        def sum_squares(l, into, squares_before, adds_before_, chunks):
            for c in range(1, chunks):
                pool.wait_ge(sq_new.sem, sq_new.at(l, squares_before + c + 1))
                if c >= 2:
                    pool.wait_ge(ssq_new.sem, ssq_new.at(l, adds_before_ + c - 1))
                first = sq[:, 0, :] if c == 1 else into[:, :]
                add(into[:, :], first, sq[:, c % 2, :], ALU.add).then_inc(ssq_new.sem, 1)

        for c in range(NC_ - 1):
            pool.wait_ge(x_new.sem, c + 1)
            add(sq[:, c % 2, :] if c else ssq[:, :], xT[:, c, :], xT[:, c, :], ALU.mult).then_inc(x_squared.sem, 1)
            pool.wait_ge(x_squared.sem, c + 1)
            if c >= 1:
                if c >= 2:
                    pool.wait_ge(ssq_new.sem, c - 1)
                add(ssq[:, :], ssq[:, :], sq[:, c % 2, :], ALU.add).then_inc(ssq_new.sem, 1)
        for l in layers(pool):
            pool.wait_ge(sq_new.sem, sq_new.at(l, 1))
            pool.wait_ge(ssq_new.sem, ssq_new.at(l, 0))
            add(ssq[:, :], ssq[:, :], sq[:, 1, :], ALU.add).then_inc(ssq_new.sem, 1)
            pool.wait_ge(k_hi.sem, k_hi.at(l, 1))
            k = hm[:, 0:TS, C_K:C_V].rearrange("p t (h d) -> p t h d", d=64)
            for x in range(2):
                add(k2[:, :, 2 + x:8:4, :], k, k2[:, :, x:8:4, :], ALU.subtract)
            for x in range(2):
                ins = add(k2[:, :, 10 + x, :], hm[:, 0:TS, C_KR:IN_W], k2[:, :, 8 + x, :], ALU.subtract)
            ins.then_inc(k_lo.sem, 1)

            def cos_queries(t):
                pool.wait_ge(hm_new.sem, hm_new.at(l, 10 + t + 1))
                if t >= 2:
                    pool.wait_ge(q_roped.sem, q_roped.at(l, t - 1))
                c3 = cos[t].unsqueeze(1).broadcast_to([P, AH, 64])
                q, a3 = (x.rearrange("p (h d) -> p h d", d=64) for x in (hm[:, t, 0:C_K], qcos[:, t % 2, :]))
                add(a3, q, c3, ALU.mult).then_inc(q_cos.sem, 1)

            def queries_lo(t):
                pool.wait_ge(q_hi.sem, q_hi.at(l, t + 1))
                q = hm[:, t, 0:C_K].rearrange("p (h d) -> p h d", d=64)
                add(q2[:, t % 2, :, 64:128], q, q2[:, t % 2, :, 0:64], ALU.subtract).then_inc(q_lo.sem, 1)

            def rope_q_lo(t):
                pool.wait_ge(uqr_hi.sem, uqr_hi.at(l, t + 1))
                q = qra[:, t % 2, :].rearrange("p (h d) -> p h d", d=64)
                add(q2r[:, t % 2, :, 64:128], q, q2r[:, t % 2, :, 0:64], ALU.subtract).then_inc(uqr_lo.sem, 1)

            cos_queries(0)
            cos_queries(1)
            queries_lo(0)
            queries_lo(1)
            cos_queries(2)
            cos_queries(3)
            queries_lo(2)
            rope_q_lo(0)
            rope_q_lo(1)
            queries_lo(3)
            rope_q_lo(2)
            cos_queries(4)
            rope_q_lo(3)
            rope_q_lo(4)
            for n in range(8):
                pool.wait_ge(w_rinv.sem, w_rinv.at(l, n + 1))
                r = four_of(rinv, n).unsqueeze(2).broadcast_to([P, 4, 256])
                add(pwb[n % 4], pwb[n % 4], r, ALU.mult).then_inc(w_p.sem, 1)
            for h in range(1, BH):
                pool.wait_ge(sq_new.sem, sq_new.at(l, h + 2))
                if h >= 2:
                    pool.wait_ge(ssq_new.sem, ssq_new.at(l, h))
                first = sq[:, 0, 0:PROMPT] if h == 1 else ssqB[:, 0:PROMPT]
                add(ssqB[:, 0:PROMPT], first, sq[:, h % 2, 0:PROMPT], ALU.add).then_inc(ssq_new.sem, 1)
            sum_squares(l, ssq, 5, 4, 4)
            pool.wait_ge(sq_new.sem, sq_new.at(l, 10))
            for h in range(1, BH):
                if h >= 2:
                    pool.wait_ge(ssq_new.sem, ssq_new.at(l, 6 + h))
                first = sq[:, 0, 0:P] if h == 1 else ssqB[:, PROMPT:T]
                add(ssqB[:, PROMPT:T], first, sq[:, 0, h * P:(h + 1) * P], ALU.add).then_inc(ssq_new.sem, 1)
            sum_squares(l, ssq, 10, 10, NC_)
            sum_squares(l, ssq, 18, 17, NC_ - 1)
        pool.wait_ge(sq_new.sem, sq_new.at(DEPTH, 1))
        pool.wait_ge(ssq_new.sem, ssq_new.at(DEPTH, 0))
        add(ssq[:, :], ssq[:, :], sq[:, 1, :], ALU.add).then_inc(ssq_new.sem, 1)
        pool.wait_ge(fg_in.sem, 16)
        for t in range(NT):
            pool.wait_ge(y_scaled.sem, t + 1)
            add(yout[:, t, 0:512], yout[:, t, 0:512], fg[:, 0:512], ALU.mult).then_inc(y_pool.sem, 1)


def constants():
    import numpy as np

    k = np.zeros((P, K_W + M_W), np.float32)
    k[:, K_ID:K_ID + P] = np.eye(P, dtype=np.float32)
    row, key = np.arange(P)[:, None], np.arange(256)[None, :]
    masks = k[:, K_W:]
    masks[:, M_OWN + P:M_OWN + P + 256] = np.where(key // 64 <= row // 64, 0, HIDDEN)
    masks[:, M_BAND:M_BAND + 256] = np.where((key // 64 >= row // 64) & (key // 64 <= row // 64 + 2), 0, HIDDEN)
    masks[:, M_ID:M_ID + P] = np.eye(P, dtype=np.float32)
    half = ROPE // 2
    inv = np.power(np.float32(10000.0), -np.arange(half, dtype=np.float32) / np.float32(half)).astype(np.float32)
    pos = np.concatenate([np.arange(PROMPT), np.tile(PAST + np.arange(DECS), DECB)]).astype(np.float32)
    ang = pos[:, None] * inv[None, :]
    c, s = np.cos(ang).astype(np.float32), np.sin(ang).astype(np.float32)
    table = np.concatenate([c, c, -s, s], axis=1).reshape(NT, P, 128)
    k[:, K_ROPE:K_ROPE + NT * 128] = table.transpose(1, 0, 2).reshape(P, NT * 128)
    k[:, K_ONE] = 1.0
    k[:, K_EPS] = EPS
    k[:, K_ONES:K_ONES + P] = 1.0
    return k


_INS = ["x_prompt", "x_sample", "cache_win_k", "cache_win_v", "cache_mla_ckv", "cache_mla_krope", "w_in", "w_uq", "w_uk",
        "w_uv", "w_out", "w_gate", "w_up", "w_down"]
_OUTS = {"out_y": (1, PROMPT, D), "out_ys": (DECB, DECS, D),
         "out_wk": (DEPTH, 1, WIN, 2, HD), "out_wv": (DEPTH, 1, WIN, 2, HD), "out_ckv": (DEPTH, 1, PROMPT, KL), "out_kr": (DEPTH, 1, PROMPT, ROPE),
         "out_wks": (DEPTH, DECB, WIN, 2, HD), "out_wvs": (DEPTH, DECB, WIN, 2, HD), "out_ckvs": (DEPTH, DECB, DECS, KL), "out_krs": (DEPTH, DECB, DECS, ROPE)}


def kernel(**inputs):
    import numpy as np
    from concourse import bacc
    from concourse.bass_utils import run_bass_kernel_spmd

    arrays = {n: np.ascontiguousarray(inputs[n]) for n in _INS}
    g = {n: np.asarray(inputs[n]) for n in ("attn_norm", "ffn_norm", "gn_a", "gn_b", "q_norm", "kv_norm", "sinks", "final_norm")}
    packed = np.empty((DEPTH, P, G_W), np.float32)
    for l in range(DEPTH):
        following = g["attn_norm"][l + 1] if l + 1 < DEPTH else g["final_norm"]
        packed[l, :, G_NEXT:G_NEXT + 8] = following.reshape(8, P).T
        packed[l, :, G_FFN:G_FFN + 8] = g["ffn_norm"][l].reshape(8, P).T
        packed[l, :, G_MIX:G_MIX + 4] = g["gn_a"][l].reshape(2, 4, 64).transpose(0, 2, 1).reshape(P, 4)
        packed[l, :, G_MIX + 4:G_MIX + 8] = g["gn_b"][l].reshape(4, P).T
        packed[l, :, G_Q:G_W] = g["q_norm"][l][None, :]
        packed[l, :, G_SINK:G_SINK + 8] = g["sinks"][l][None, :]
        packed[l, :, G_SINKS] = np.repeat(g["sinks"][l], DECS)
        packed[l, :, G_KV:G_Q] = g["kv_norm"][l][None, :]
    arrays["vectors"] = packed
    arrays["final_gain"] = np.ascontiguousarray(np.broadcast_to(g["final_norm"], (P, D)))
    arrays["consts"] = constants()
    arrays["consts"][:, K_GAIN:K_GAIN + 8] = g["attn_norm"][0].reshape(8, P).T
    nc = bacc.Bacc("TRN2", target_bir_lowering=False, num_devices=1)
    a = {n: nc.dram_tensor(n, v.shape, F32, kind="ExternalInput").ap() for n, v in arrays.items()}
    a.update({n: nc.dram_tensor(n, s, F32, kind="ExternalOutput").ap() for n, s in _OUTS.items()})
    hybrid_encoder_step(nc, a)
    r = run_bass_kernel_spmd(nc, [arrays], core_ids=[0]).results[0]
    return tuple(r[n] for n in _OUTS)
```
